# Optimizing a Trainium2 kernel written in Bass

```python
import functools
import jax, jax.numpy as jnp
from jax import lax
import numpy as np

D_MODEL = 1024
BATCH = 1
SEQ = 2048
DEPTH = 1
DEC_BATCH = 8
DEC_SEQ = 4
PAST_LEN = 16384
PAGE_SIZE = 128

HEAD_DIM = 64
ATTN_HEADS = D_MODEL // 2 // HEAD_DIM
KV_HEADS = 2
GROUP = ATTN_HEADS // KV_HEADS
IDX_HEADS = 8
IDX_DIM = 64
TOPK_MAX = 256
Q_BLOCK = 128
RET_DK = 128
RET_DV = 128
RET_HEADS = D_MODEL // 2 // RET_DV
RET_CHUNK = 128
D_FF = -(-8 * D_MODEL // (3 * 256)) * 256
PLE_DIM = 256
ROPE_THETA = 10000.0
EPS = 1e-6
GN_EPS = 1e-5
IN_SIZES = (ATTN_HEADS * HEAD_DIM, KV_HEADS * HEAD_DIM, KV_HEADS * HEAD_DIM, IDX_HEADS * IDX_DIM, IDX_DIM, IDX_HEADS,
            RET_HEADS * RET_DK, RET_HEADS * RET_DK, RET_HEADS * RET_DV, RET_HEADS * RET_DV)
IN_TOTAL = sum(IN_SIZES)

kernel_name = 'hymba_dsa_retnet_step'

def rms_norm(x, g):
    xf = x.astype(jnp.float32)
    y = xf * lax.rsqrt(jnp.mean(xf * xf, axis=-1, keepdims=True) + EPS)
    return (y * g.astype(jnp.float32)).astype(x.dtype)

def rope(x, pos):
    half = x.shape[-1] // 2
    inv = ROPE_THETA ** (-jnp.arange(half, dtype=jnp.float32) / half)
    ang = pos.astype(jnp.float32)[:, None] * inv[None, :]
    cos = jnp.cos(ang)[:, None, :]
    sin = jnp.sin(ang)[:, None, :]
    xf = x.astype(jnp.float32)
    x1, x2 = xf[..., :half], xf[..., half:]
    return jnp.concatenate([x1 * cos - x2 * sin, x1 * sin + x2 * cos], axis=-1).astype(x.dtype)

def gather_rows(rows, idx):
    return jax.vmap(lambda r, i: r[i])(rows, idx)

def project_mixers(a, w_in, pos):
    b, t, _ = a.shape
    offsets = [int(o) for o in np.cumsum(IN_SIZES)[:-1]]
    q, k, v, qi, ki, wi, rq, rk, rv, rg = jnp.split(a @ w_in, offsets, axis=-1)
    q = rope(q.reshape(b, t, ATTN_HEADS, HEAD_DIM), pos)
    k = rope(k.reshape(b, t, KV_HEADS, HEAD_DIM), pos)
    v = v.reshape(b, t, KV_HEADS, HEAD_DIM)
    qi = rope(qi.reshape(b, t, IDX_HEADS, IDX_DIM), pos)
    ki = rope(ki.reshape(b, t, 1, IDX_DIM), pos)[:, :, 0]
    wi = wi * (IDX_HEADS ** -0.5)
    rq = rope(rq.reshape(b, t, RET_HEADS, RET_DK), pos)
    rk = rope(rk.reshape(b, t, RET_HEADS, RET_DK), pos) * (RET_DK ** -0.5)
    rv = rv.reshape(b, t, RET_HEADS, RET_DV)
    return q, k, v, qi, wi, ki, rq, rk, rv, rg

def indexer_scores(qi, wi, ki, qpos, kpos):
    s = jnp.einsum('bqhd,bkd->bqhk', qi.astype(jnp.float32), ki.astype(jnp.float32)) * (IDX_DIM ** -0.5)
    s = jnp.einsum('bqhk,bqh->bqk', jax.nn.relu(s), wi.astype(jnp.float32))
    return jnp.where(kpos[None, None, :] <= qpos[None, :, None], s, -jnp.inf)

def sparse_attend(q, k_sel, v_sel, valid):
    b, nq = q.shape[:2]
    qg = q.reshape(b, nq, KV_HEADS, GROUP, HEAD_DIM).astype(jnp.float32)
    logits = jnp.einsum('bqngd,bqknd->bqngk', qg, k_sel.astype(jnp.float32)) * (HEAD_DIM ** -0.5)
    logits = jnp.where(valid[:, :, None, None, :], logits, -jnp.inf)
    probs = jax.nn.softmax(logits, axis=-1)
    o = jnp.einsum('bqngk,bqknd->bqngd', probs, v_sel.astype(jnp.float32))
    return o.reshape(b, nq, ATTN_HEADS * HEAD_DIM).astype(q.dtype)

def dsa_prompt(q, k, v, qi, wi, ki, topk):
    b, s = q.shape[:2]
    kpos = jnp.arange(s)

    def block(bi):
        start = bi * Q_BLOCK
        qb = lax.dynamic_slice_in_dim(q, start, Q_BLOCK, axis=1)
        qib = lax.dynamic_slice_in_dim(qi, start, Q_BLOCK, axis=1)
        wib = lax.dynamic_slice_in_dim(wi, start, Q_BLOCK, axis=1)
        qpos = start + jnp.arange(Q_BLOCK)
        _, idx = lax.top_k(indexer_scores(qib, wib, ki, qpos, kpos), topk)
        valid = idx <= qpos[None, :, None]
        return sparse_attend(qb, gather_rows(k, idx), gather_rows(v, idx), valid)

    out = lax.map(block, jnp.arange(s // Q_BLOCK))
    return out.transpose(1, 0, 2, 3).reshape(b, s, -1)

def dsa_sample(q, k, v, qi, wi, ki, pool_k, pool_v, pool_ik, page_table, topk):
    db, t = q.shape[:2]
    past = page_table.shape[1] * PAGE_SIZE
    ik_past = pool_ik[page_table].reshape(db, past, IDX_DIM).astype(ki.dtype)
    ik_all = jnp.concatenate([ik_past, ki], axis=1)
    qpos = past + jnp.arange(t)
    kpos = jnp.arange(past + t)
    _, idx = lax.top_k(indexer_scores(qi, wi, ik_all, qpos, kpos), topk)
    valid = idx <= qpos[None, :, None]
    is_new = idx >= past
    idx_past = jnp.minimum(idx, past - 1)
    phys = jnp.take_along_axis(page_table, (idx_past // PAGE_SIZE).reshape(db, -1), axis=1).reshape(idx.shape)
    off = idx_past % PAGE_SIZE
    idx_new = jnp.clip(idx - past, 0, t - 1)

    def pick(pool, new):
        return jnp.where(is_new[..., None, None], gather_rows(new, idx_new), pool[phys, off].astype(new.dtype))

    return sparse_attend(q, pick(pool_k, k), pick(pool_v, v), valid)

def retention_chunk(state, q, k, v, log_g):
    c = q.shape[1]
    i = jnp.arange(c, dtype=jnp.float32)
    diff = i[:, None] - i[None, :]
    decay = jnp.where(diff >= 0, jnp.exp(log_g[:, None, None] * jnp.maximum(diff, 0.0)), 0.0)
    inner = jnp.einsum('bihd,bjhd->bhij', q, k) * decay[None]
    o = jnp.einsum('bhij,bjhe->bihe', inner, v)
    q_dec = jnp.exp(log_g[None, :] * (i[:, None] + 1.0))
    o = o + jnp.einsum('bihd,bhde->bihe', q, state) * q_dec[None, :, :, None]
    k_dec = jnp.exp(log_g[None, :] * (c - 1.0 - i)[:, None])
    new_state = jnp.exp(log_g * c)[None, :, None, None] * state + jnp.einsum('bjhd,bjhe->bhde', k * k_dec[None, :, :, None], v)
    return new_state, o

def retention(rq, rk, rv, s0, chunk):
    b, t = rq.shape[:2]
    nc = t // chunk
    log_g = jnp.log1p(-jnp.exp2(-5.0 - jnp.arange(RET_HEADS, dtype=jnp.float32)))

    def to_chunks(x):
        return x.astype(jnp.float32).reshape(b, nc, chunk, *x.shape[2:]).swapaxes(0, 1)

    s_fin, o = lax.scan(lambda st, xs: retention_chunk(st, xs[0], xs[1], xs[2], log_g),
                        s0.astype(jnp.float32), (to_chunks(rq), to_chunks(rk), to_chunks(rv)))
    return o.swapaxes(0, 1).reshape(b, t, RET_HEADS, RET_DV), s_fin

def retention_out(o, rg, gain, dtype):
    mu = jnp.mean(o, axis=-1, keepdims=True)
    var = jnp.mean(jnp.square(o - mu), axis=-1, keepdims=True)
    on = ((o - mu) * lax.rsqrt(var + GN_EPS)).reshape(o.shape[0], o.shape[1], -1) * gain.astype(jnp.float32)
    return (jax.nn.silu(rg.astype(jnp.float32)) * on).astype(dtype)

def trunk_layer(h, p, pos, s0, chunk, attend, g_mix, w_in, g_retn, w_out, g_ffn, w_ffn_in, w_ffn_out,
                g_ple, w_ple_gate, w_ple_proj):
    a = rms_norm(h, g_mix)
    q, k, v, qi, wi, ki, rq, rk, rv, rg = project_mixers(a, w_in, pos)
    attn = attend(q, k, v, qi, wi, ki)
    ro, s_fin = retention(rq, rk, rv, s0, chunk)
    ret = retention_out(ro, rg, g_retn, h.dtype)
    h = h + jnp.concatenate([attn, ret], axis=-1) @ w_out
    f = rms_norm(h, g_ffn)
    gt, up = jnp.split(f @ w_ffn_in, 2, axis=-1)
    h = h + (jax.nn.silu(gt) * up) @ w_ffn_out
    gate = jax.nn.sigmoid(rms_norm(h, g_ple) @ w_ple_gate)
    h = h + gate * (p.astype(h.dtype) @ w_ple_proj)
    return h, (k, v, ki, s_fin.astype(h.dtype))

def setup_inputs(seed: int = 0) -> dict:
    key = jax.random.key(seed)
    ks = jax.random.split(key, 20)
    f32 = jnp.float32
    n_pages = PAST_LEN // PAGE_SIZE
    n_used = DEC_BATCH * n_pages
    n_phys = n_used + (n_used + 3) // 4

    def normal(k, shape, scale=1.0):
        return scale * jax.random.normal(k, shape, f32)

    def gain(k, shape):
        return 1.0 + 0.02 * jax.random.normal(k, shape, f32)

    page_table = jax.random.permutation(ks[0], n_phys)[:n_used].reshape(DEC_BATCH, n_pages).astype(jnp.int32)
    return {
        'x_prompt': normal(ks[1], (BATCH, SEQ, D_MODEL)),
        'x_sample': normal(ks[2], (DEC_BATCH, DEC_SEQ, D_MODEL)),
        'cache_k': normal(ks[3], (DEPTH, n_phys, PAGE_SIZE, KV_HEADS, HEAD_DIM)),
        'cache_v': normal(ks[4], (DEPTH, n_phys, PAGE_SIZE, KV_HEADS, HEAD_DIM)),
        'cache_idx_k': normal(ks[5], (DEPTH, n_phys, PAGE_SIZE, IDX_DIM)),
        'state_retn': normal(ks[6], (DEPTH, DEC_BATCH, RET_HEADS, RET_DK, RET_DV), 0.5),
        'page_table': page_table,
        'p_prompt': normal(ks[7], (DEPTH, BATCH, SEQ, PLE_DIM)),
        'p_sample': normal(ks[8], (DEPTH, DEC_BATCH, DEC_SEQ, PLE_DIM)),
        'g_mix': gain(ks[9], (DEPTH, D_MODEL)),
        'w_in': normal(ks[10], (DEPTH, D_MODEL, IN_TOTAL), D_MODEL ** -0.5),
        'g_retn': gain(ks[11], (DEPTH, RET_HEADS * RET_DV)),
        'w_out': normal(ks[12], (DEPTH, D_MODEL, D_MODEL), D_MODEL ** -0.5),
        'g_ffn': gain(ks[13], (DEPTH, D_MODEL)),
        'w_ffn_in': normal(ks[14], (DEPTH, D_MODEL, 2 * D_FF), D_MODEL ** -0.5),
        'w_ffn_out': normal(ks[15], (DEPTH, D_FF, D_MODEL), D_FF ** -0.5),
        'g_ple': gain(ks[16], (DEPTH, D_MODEL)),
        'w_ple_gate': normal(ks[17], (DEPTH, D_MODEL, D_MODEL), D_MODEL ** -0.5),
        'w_ple_proj': normal(ks[18], (DEPTH, PLE_DIM, D_MODEL), PLE_DIM ** -0.5),
        'g_final': gain(ks[19], (D_MODEL,)),
    }

def reference(x_prompt, x_sample, cache_k, cache_v, cache_idx_k, state_retn, page_table, p_prompt, p_sample,
              g_mix, w_in, g_retn, w_out, g_ffn, w_ffn_in, w_ffn_out, g_ple, w_ple_gate, w_ple_proj, g_final):
    seq = x_prompt.shape[1]
    dec_seq = x_sample.shape[1]
    past = page_table.shape[1] * PAGE_SIZE
    topk_prompt = min(TOPK_MAX, seq // 4)
    topk_sample = min(TOPK_MAX, (past + dec_seq) // 4)
    pos_prompt = jnp.arange(seq)
    pos_sample = past + jnp.arange(dec_seq)
    h_p, h_s = x_prompt, x_sample
    new_p, new_s = [], []
    for i in range(DEPTH):
        weights = (g_mix[i], w_in[i], g_retn[i], w_out[i], g_ffn[i], w_ffn_in[i], w_ffn_out[i],
                   g_ple[i], w_ple_gate[i], w_ple_proj[i])
        s0 = jnp.zeros((x_prompt.shape[0], RET_HEADS, RET_DK, RET_DV), jnp.float32)
        attend_p = functools.partial(dsa_prompt, topk=topk_prompt)
        h_p, st_p = trunk_layer(h_p, p_prompt[i], pos_prompt, s0, RET_CHUNK, attend_p, *weights)
        attend_s = functools.partial(dsa_sample, pool_k=cache_k[i], pool_v=cache_v[i], pool_ik=cache_idx_k[i],
                                     page_table=page_table, topk=topk_sample)
        h_s, st_s = trunk_layer(h_s, p_sample[i], pos_sample, state_retn[i], dec_seq, attend_s, *weights)
        new_p.append(st_p)
        new_s.append(st_s)
    y_prompt = rms_norm(h_p, g_final)
    y_sample = rms_norm(h_s, g_final)
    k_prompt = jnp.stack([st[0] for st in new_p])
    v_prompt = jnp.stack([st[1] for st in new_p])
    idx_k_prompt = jnp.stack([st[2] for st in new_p])
    retn_prompt = jnp.stack([st[3] for st in new_p])
    k_sample = jnp.stack([st[0] for st in new_s])
    v_sample = jnp.stack([st[1] for st in new_s])
    idx_k_sample = jnp.stack([st[2] for st in new_s])
    retn_sample = jnp.stack([st[3] for st in new_s])
    return (y_prompt, y_sample, k_prompt, v_prompt, idx_k_prompt, retn_prompt, k_sample, v_sample, idx_k_sample, retn_sample)


_drawn_inputs = setup_inputs


def setup_inputs(seed=0):
    import zlib

    import numpy as np

    out = dict(_drawn_inputs(seed))
    spreads = {}
    factors = {'g_retn': 6.607, 'g_ffn': 4.216, 'g_ple': 8.0, 'g_final': 2.832}
    for name, (base, spread) in spreads.items():
        noise = np.random.default_rng([zlib.crc32(name.encode()), seed]).standard_normal(out[name].shape)
        drawn = base * np.exp(spread * noise) if base else spread * noise
        out[name] = __import__('jax').numpy.asarray(drawn.astype(out[name].dtype))
    for name, factor in factors.items():
        out[name] = (out[name] * factor).astype(out[name].dtype)
    return out
```

```python
from contextlib import ExitStack

import numpy as np

import concourse.bass as bass
from concourse import mybir

F32 = mybir.dt.float32
I32 = mybir.dt.int32
U32 = mybir.dt.uint32
ALU = mybir.AluOpType
ACT = mybir.ActivationFunctionType
AX = mybir.AxisListType

P = 128
D = 1024
KD = D // P
SEQ = 2048
NB, TS = 8, 4
NS = NB * TS
PAST = 16384
PAGE = 128
NPAGES = PAST // PAGE
HD = 64
AH, KVH, GRP = 8, 2, 4
IH = 8
TOPK = 256
RH, RD = 4, 128
DFF = 2816
PLE = 256
NT = SEQ // P
ROWS = (NT + 1) * P
EPS, GN_EPS = 1e-6, 1e-5
BIG = 1.0e30

GROUPS = {
    "rq": [(1352, 512)], "rk": [(1864, 512)], "rv": [(2376, 512)], "rg": [(2888, 512)],
    "q": [(0, 512)], "qi": [(768, 512)], "kiv": [(512, 128), (1280, 64), (640, 128), (1344, 8)],
}
ORDER = ["rq", "rk", "rv", "rg", "q", "qi", "kiv"]
WIDTH = {g: sum(w for _, w in GROUPS[g]) for g in ORDER}
START = {g: sum(WIDTH[x] for x in ORDER[:n]) for n, g in enumerate(ORDER)}
WIN = sum(WIDTH.values())
KIV = WIDTH["kiv"]
TRW = 10 * P


def log_gamma():
    return np.log1p(-np.exp2(-5.0 - np.arange(RH, dtype=np.float64)))


def rope_table():
    pos = np.concatenate([np.arange(SEQ), np.tile(PAST + np.arange(TS), NB), np.zeros(ROWS - SEQ - NS, int)])
    cols = []
    for half in (32, 64):
        inv = 10000.0 ** (-np.arange(half, dtype=np.float64) / half)
        ang = pos.astype(np.float32)[:, None] * inv[None, :].astype(np.float32)
        cols += [np.cos(ang), np.sin(ang)]
    return np.concatenate(cols, 1).astype(np.float32)


C_ID, C_DEC, C_DECS, C_QD, C_KD, C_QDS, C_KDS, C_BLK = 0, 128, 640, 768, 772, 776, 780, 784
C_BLKR = C_BLK + NB * NS
C_W = C_BLKR + NB


def constant_table():
    c = np.zeros((P, C_W), np.float64)
    c[:, C_ID:C_ID + P] = np.eye(P)
    i = np.arange(P)
    s = RD ** -0.5
    for h, lg in enumerate(log_gamma()):
        c[:, C_DEC + h * P:C_DEC + (h + 1) * P] = np.where(i[None, :] >= i[:, None], s * np.exp(-lg * (i[:, None] + 1.0)), 0)
        r = np.arange(NS)
        same = (r[:, None] // TS == r[None, :] // TS) & (r[None, :] >= r[:, None])
        c[:NS, C_DECS + h * NS:C_DECS + (h + 1) * NS] = np.where(same, s * np.exp(-lg * (r[:, None] % TS + 1.0)), 0)
        c[:, C_QD + h] = np.exp(lg * (i + 1.0))
        c[:, C_KD + h] = s * np.exp(lg * (P - 1.0 - i))
        c[:NS, C_QDS + h] = np.exp(lg * (r % TS + 1.0))
        c[:NS, C_KDS + h] = s * np.exp(lg * (TS - 1.0 - r % TS))
    for b in range(NB):
        c[:, C_BLK + b * NS + b * TS:C_BLK + b * NS + (b + 1) * TS] = 1
        c[b * TS:(b + 1) * TS, C_BLKR + b] = 1
    return c.astype(np.float32)


class Signal:

    def __init__(self, sem, per, tiles=2):
        self.sem, self.per, self.tiles = sem, per, tiles

    def seed(self, eng):
        eng.sem_inc(self.sem, 2 * self.per)

    def at(self, n, k=None):
        i, u = n
        return i * (self.tiles * self.per) + (u + 2) * self.per + (self.per if k is None else k)


def bc(ap, axis, n):
    v = ap.unsqueeze(axis)
    shape = list(v.shape)
    shape[axis] = n
    return v.broadcast_to(shape)


def project_phase(nc, t):
    with ExitStack() as ctx:
        sb = lambda name, shape, dt=F32: ctx.enter_context(nc.sbuf_tensor("a_" + name, shape, dt))
        sem = lambda name: ctx.enter_context(nc.semaphore("a_" + name))
        signal = lambda name, per: Signal(sem(name), per)

        w = sb("w", [P, KD, WIN])
        c = sb("c", [P, C_W])
        ident = c[:, C_ID:C_ID + P]
        gmix = sb("gmix", [P, D])
        gretn = sb("gretn", [P, RH * RD])
        x = sb("x", [P, 2, D])
        rope = sb("rope", [P, 2, 192])
        ssq = sb("ssq", [P, 2])
        rstd = sb("rstd", [P, 2])
        mhalf = sb("mhalf", [P, RH])
        xn = sb("xn", [P, D])
        xT = sb("xT", [P, 2, KD, P])
        ta = sb("ta", [P, 512])
        tb = sb("tb", [P, 512])
        rq = sb("rq", [P, 512])
        rk = sb("rk", [P, 512])
        rkd = sb("rkd", [P, 512])
        rv = sb("rv", [P, 512])
        rg = sb("rg", [P, 512])
        erg = sb("erg", [P, 512])
        gate = sb("gate", [P, 512])
        q = sb("q", [P, 4, KVH, HD])
        qi = sb("qi", [P, 4, KVH, HD])
        kiv = sb("kiv", [P, 2, KIV])
        kid = sb("kid", [P, 2, HD])
        rqT = sb("rqT", [P, 512])
        rkT = sb("rkT", [P, 512])
        innT = sb("innT", [P, 512])
        o = sb("o", [P, 512])
        stats = sb("stats", [P, RH, 6])
        mv = sb("mv", [P, RH, 2])
        orstd = sb("orstd", [P, RH])
        ret = sb("ret", [P, 2, 512])
        state = sb("state", [P, RH * RD])
        trs = sb("trs", [P, 2, TRW])

        pxT = ctx.enter_context(nc.psum_tensor("a_pxT", [P, 2, 512], F32))
        pproj = ctx.enter_context(nc.psum_tensor("a_pproj", [P, 4, 512], F32))
        pr = ctx.enter_context(nc.psum_tensor("a_pr", [P, 2, 512], F32))

        consts = sem("consts")
        w_landed = [sem(f"w_{g}") for g in ORDER]
        x_landed = [sem(f"x_landed{u}") for u in range(2)]
        stored = [sem(f"stored{u}") for u in range(2)]
        state_out = sem("state_out")
        sstate_in = sem("sstate_in")
        ssq_done = signal("ssq_done", 1)
        xn_done = signal("xn_done", 1)
        xT_done = signal("xT_done", 2)
        xT_copied = signal("xT_copied", 2)
        proj = signal("proj", 7)
        roped = signal("roped", 5)
        taken = signal("taken", 2)
        mixed = signal("mixed", 8)
        moved = signal("moved", 5)
        folded = signal("folded", 3)
        rkd_done = signal("rkd_done", 1)
        gate_done = signal("gate_done", 1)
        var_done = signal("var_done", 1)
        orstd_done = signal("orstd_done", 1)
        ret_done = signal("ret_done", 1)
        blk_done = sem("blk_done")
        snew_done = sem("snew_done")
        snew_taken = sem("snew_taken")

        zeroed = sem("zeroed")

        wflat = w[:].rearrange("p k n -> p (k n)")
        sst = wflat[:, 0:4096].rearrange("p (h b e) -> p h b e", h=RH, b=NB)
        rqb = wflat[:, 4096:5120].rearrange("p (h b r) -> p h b r", h=RH, b=NB)
        rvb = wflat[0:NS, 5120:9216].rearrange("p (h b e) -> p h b e", h=RH, b=NB)

        block = ctx.enter_context(nc.Block())
        last = (NT // 2, 0)
        PAIRS = NT // 2

        def heads(ap, n=RH):
            return ap.rearrange("p (h e) -> p h e", h=n)

        @block.sync
        def _(sp):
            sp.sem_inc(stored[0], 48)
            sp.sem_inc(stored[1], 48)

            def load(row, i, u):
                sp.dma_start(x[:, u, :], t.x[bass.ds(row, P), :]).then_inc(x_landed[u], 16)
                sp.dma_start(rope[:, u, :], t.rope[bass.ds(row, P), :]).then_inc(x_landed[u], 16)

            def store(row, n):
                i, u = n
                sp.wait_ge(moved.sem, moved.at(n))
                sp.dma_start(t.tr[bass.ds(row, P), :], trs[:, u, :]).then_inc(stored[u], 16)
                sp.dma_start(t.kiv[bass.ds(row, P), :], kiv[:, u, :]).then_inc(stored[u], 16)
                sp.wait_ge(ret_done.sem, ret_done.at(n))
                sp.dma_start(t.cat[bass.ds(row, P), 512:D], ret[:, u, :]).then_inc(stored[u], 16)

            load(0, 0, 0)
            sp.dma_start(c[:], t.c).then_inc(consts, 16)
            sp.dma_start(gmix[:], t.g_mix.partition_broadcast(P)).then_inc(consts, 16)
            sp.dma_start(gretn[:], t.g_retn.partition_broadcast(P)).then_inc(consts, 16)
            for g, landed in zip(ORDER, w_landed):
                at = START[g]
                for src, width in GROUPS[g]:
                    sp.dma_start(w[:, :, at:at + width],
                                 t.w_in[:, src:src + width].rearrange("(k p) n -> p k n", p=P)).then_inc(landed, 16)
                    at += width
            with sp.Fori(0, PAIRS) as i:
                rows = [sp.snap((i * 2 + v) * P) for v in range(3)]
                for u in range(2):
                    sp.wait_ge(xn_done.sem, xn_done.at((i, u - 1)))
                    sp.wait_ge(roped.sem, roped.at((i, u - 1)))
                    load(rows[u + 1], i, (u + 1) % 2)
                    store(rows[u], (i, u))
            for h in range(RH):
                if h == 0:
                    sp.wait_ge(proj.sem, proj.at(last))
                sp.dma_start(sst[:, h], t.state_retn[:, h].rearrange("b d e -> d b e")).then_inc(sstate_in, 16)
            store(NT * P, last)
            sp.wait_ge(folded.sem, folded.at((PAIRS - 1, 1)))
            sp.dma_start(t.retn_prompt.rearrange("h d e -> d h e"), heads(state[:])).then_inc(state_out, 16)
            for h in range(RH):
                sp.wait_ge(snew_taken, 2 * h + 2)
                sp.dma_start(t.retn_sample[:, h].rearrange("b d e -> d b e"), sst[:, h]).then_inc(state_out, 16)
            sp.wait_ge(state_out, 16 * (1 + RH))
            for u, tiles in ((0, PAIRS + 1), (1, PAIRS)):
                sp.wait_ge(stored[u], 48 * (tiles + 1))

        @block.tensor
        def _(pe):
            for s in (xT_done, proj, mixed):
                s.seed(pe)
            pe.wait_ge(consts, 48)

            def transpose_x(n):
                i, u = n
                pe.wait_ge(xn_done.sem, xn_done.at(n))
                pe.wait_ge(xT_copied.sem, xT_copied.at((i, u - 1)))
                for half in range(2):
                    for k in range(4):
                        at = (half * 4 + k) * P
                        m = pe.transpose(pxT[:, half, k * P:(k + 1) * P], xn[:, at:at + P], ident)
                    m.then_inc(xT_done.sem, 1)

            def project(n, g):
                i, u = n
                s = ORDER.index(g)
                pe.wait_ge(w_landed[s], 16 * len(GROUPS[g]))
                if g == "rq":
                    pe.wait_ge(xT_copied.sem, xT_copied.at(n))
                before = {"rq": (roped, (i, u - 1), 3), "rk": (roped, (i, u - 1), 4), "rv": (roped, (i, u - 1), 5),
                          "rg": (taken, (i, u - 1), 2), "q": (roped, n, 1), "qi": (roped, n, 2), "kiv": (taken, n, 1)}[g]
                pe.wait_ge(before[0].sem, before[0].at(before[1], before[2]))
                for k in range(KD):
                    m = pe.matmul(pproj[:, s % 4, 0:WIDTH[g]], xT[:, u % 2, k, :], w[:, k, START[g]:START[g] + WIDTH[g]],
                                  start=(k == 0), stop=(k == KD - 1))
                m.then_inc(proj.sem, 1)

            def body(n, m_rows, sample=False):
                i, u = n
                R = m_rows
                for g in ("rq", "rk", "rv", "rg", "q"):
                    project(n, g)
                for j, (src, before) in enumerate(((rq, 4), (rk, 5))):
                    pe.wait_ge(roped.sem, roped.at(n, j + 1))
                    pe.wait_ge(moved.sem, moved.at((i, u - 1), before))
                    for h in range(RH):
                        m = pe.transpose(pr[:, j, h * P:h * P + R], src[0:R, h * P:(h + 1) * P], ident[0:R, 0:R])
                    m.then_inc(mixed.sem, 1)
                project(n, "qi")
                pe.wait_ge(moved.sem, moved.at(n, 2))
                for h in range(RH):
                    m = pe.matmul(pr[0:R, 0, h * R:(h + 1) * R], rkT[:, h * P:h * P + R], rqT[:, h * P:h * P + R],
                                  start=True, stop=True)
                m.then_inc(mixed.sem, 1)
                project(n, "kiv")
                if not sample:
                    transpose_x((i, u + 1))
                pe.wait_ge(folded.sem, folded.at(n, 1))
                pe.wait_ge(taken.sem, taken.at(n, 1))
                pe.wait_ge(folded.sem, folded.at((i, u - 1), 3))
                if sample:
                    pe.wait_ge(blk_done, 2)
                    pe.wait_ge(sstate_in, 16 * RH)
                for h in range(RH):
                    out = pr[0:R, 1, h * P:(h + 1) * P]
                    pe.matmul(out, innT[0:R, h * R:(h + 1) * R], rv[0:R, h * P:(h + 1) * P], start=True, stop=False)
                    if sample:
                        for b in range(NB):
                            m = pe.matmul(out, rqb[:, h, b, :], sst[:, h, b, :], start=False, stop=(b == NB - 1))
                    else:
                        m = pe.matmul(out, rqT[:, h * P:(h + 1) * P], state[:, h * P:(h + 1) * P], start=False, stop=True)
                m.then_inc(mixed.sem, 1)
                pe.wait_ge(rkd_done.sem, rkd_done.at(n))
                if sample:
                    m = None
                    for h in range(RH):
                        for half in range(2):
                            pos = h * 2 + half
                            pe.wait_ge(snew_taken, pos - 1) if pos > 1 else None
                            m = pe.matmul(pxT[:, half, :], rkd[0:NS, h * P:(h + 1) * P],
                                          rvb[:, h, half * 4:half * 4 + 4, :].rearrange("p b e -> p (b e)"),
                                          start=True, stop=True)
                            if pos < 2 * RH - 1:
                                m.then_inc(snew_done, 1)
                    m.then_inc(snew_done, 1)
                    pe.transpose(pr[0:1, 0, 0:1], ident[0:1, 0:1], ident[0:1, 0:1]).then_inc(mixed.sem, 1)
                else:
                    for h in range(RH):
                        m = pe.matmul(pr[:, 0, h * P:(h + 1) * P], rkd[:, h * P:(h + 1) * P], rv[:, h * P:(h + 1) * P],
                                      start=True, stop=True)
                    m.then_inc(mixed.sem, 1)
                pe.wait_ge(roped.sem, roped.at(n, 3))
                pe.wait_ge(folded.sem, folded.at(n, 2))
                for j in range(4):
                    m = pe.transpose(pr[:, 1, j * P:j * P + R], q[0:R, j].rearrange("p a d -> p (a d)"), ident[0:R, 0:R])
                m.then_inc(mixed.sem, 1)
                pe.wait_ge(roped.sem, roped.at(n, 4))
                pe.wait_ge(folded.sem, folded.at(n, 3))
                for j in range(4):
                    m = pe.transpose(pr[:, 0, j * P:j * P + R], qi[0:R, j].rearrange("p a d -> p (a d)"), ident[0:R, 0:R])
                m.then_inc(mixed.sem, 1)
                pe.wait_ge(roped.sem, roped.at(n, 5))
                pe.wait_ge(moved.sem, moved.at(n, 3))
                pe.transpose(pr[:, 1, 0:R], kiv[0:R, u % 2, 0:P], ident[0:R, 0:R])
                pe.transpose(pr[:, 1, P:P + R], kid[0:R].rearrange("p a d -> p (a d)"), ident[0:R, 0:R]).then_inc(mixed.sem, 1)

            transpose_x((0, 0))
            with pe.Fori(0, PAIRS) as i:
                body((i, 0), P)
                body((i, 1), P)
            body(last, NS, sample=True)

        @block.scalar
        def _(act):
            for s in (ssq_done, xT_copied, taken, moved):
                s.seed(act)

            def square(n):
                i, u = n
                act.wait_ge(x_landed[u % 2], i * 32 + 32 * (u // 2 + 1))
                act.wait_ge(xn_done.sem, xn_done.at((i, u - 1)))
                act.activation(xn[:], x[:, u % 2, :], ACT.Square, accum_out=ssq[:, u % 2:u % 2 + 1])
                act.drain()
                act.activation(ssq[:, u % 2:u % 2 + 1], ssq[:, u % 2:u % 2 + 1], ACT.Copy, scale=1.0 / D, bias=EPS).then_inc(ssq_done.sem, 1)

            def copy_xT(n):
                i, u = n
                act.wait_ge(proj.sem, proj.at((i, u - 2)))
                for half in range(2):
                    act.wait_ge(xT_done.sem, xT_done.at(n, half + 1))
                    act.activation(xT[:, u % 2, half * 4:half * 4 + 4, :].rearrange("p k c -> p (k c)"), pxT[:, half, :],
                                   ACT.Copy).then_inc(xT_copied.sem, 1)

            def body(n, R, sample=False):
                i, u = n
                s = u % 2
                act.wait_ge(proj.sem, proj.at(n, 3))
                act.wait_ge(mixed.sem, mixed.at((i, u - 1), 5))
                act.activation(rv[:], pproj[:, 2, :], ACT.Copy).then_inc(taken.sem, 1)
                act.wait_ge(proj.sem, proj.at(n, 4))
                act.wait_ge(gate_done.sem, gate_done.at((i, u - 1)))
                act.activation(erg[:], pproj[:, 3, :], ACT.Sigmoid)
                act.activation(rg[:], pproj[:, 3, :], ACT.Copy)
                act.drain().then_inc(taken.sem, 1)
                for j, dst in enumerate((rqT, rkT)):
                    act.wait_ge(mixed.sem, mixed.at(n, j + 1))
                    act.activation(heads(dst[:])[:, :, 0:R], heads(pr[:, j, :])[:, :, 0:R], ACT.Copy).then_inc(moved.sem, 1)
                if not sample:
                    act.wait_ge(xT_done.sem, xT_done.at(n))
                    square((i, u + 1))
                    copy_xT((i, u + 1))
                act.wait_ge(stored[s], (u // 2 + 1) * 48 + i * 48)
                for j, (bank, width, at) in enumerate(((1, 4, 0), (0, 4, 4), (1, 2, 8))):
                    act.wait_ge(mixed.sem, mixed.at(n, 6 + j))
                    act.activation(heads(trs[:, s, at * P:(at + width) * P], width)[:, :, 0:R],
                                   heads(pr[:, bank, 0:width * P], width)[:, :, 0:R], ACT.Copy).then_inc(moved.sem, 1)

            act.wait_ge(zeroed, 2)
            square((0, 0))
            copy_xT((0, 0))
            with act.Fori(0, PAIRS) as i:
                body((i, 0), P)
                body((i, 1), P)
            body(last, NS, sample=True)

        @block.vector
        def _(dve):
            for s in (roped, folded, var_done, ret_done):
                s.seed(dve)
            dve.memset(state[:], 0.0).then_inc(zeroed, 1)
            dve.memset(trs[:].rearrange("p s n -> p (s n)"), 0.0).then_inc(zeroed, 1)
            dve.wait_ge(zeroed, 2)
            dve.wait_ge(consts, 48)

            def rotate(src, s, half, n, outs):
                base = 0 if half == 32 else 64
                width = 2 * n * half
                view = lambda a: a.rearrange("p (m d) -> p m d", d=half)
                cos = bc(rope[:, s, base:base + half], 1, 2 * n)
                sin = bc(rope[:, s, base + half:base + 2 * half], 1, 2 * n)
                dve.tensor_tensor(view(ta[:, 0:width]), view(src), cos, ALU.mult)
                m = dve.tensor_tensor(view(tb[:, 0:width]), view(src), sin, ALU.mult)
                dve.drain()
                a = ta[:, 0:width].rearrange("p (n s d) -> p n s d", s=2, d=half)
                b = tb[:, 0:width].rearrange("p (n s d) -> p n s d", s=2, d=half)
                return a, b

            def rotate_heads(src, s, dst, order):
                a, b = rotate(src, s, 32, 8, None)
                re = lambda v, s_: v[:, :, s_, :].rearrange("p (v j) d -> p v j d", v=KVH)
                out = lambda s_: dst[:, :, :, s_ * 32:s_ * 32 + 32].rearrange("p j v d -> p v j d")
                dve.tensor_tensor(out(0), re(a, 0), re(b, 1), ALU.subtract)
                return dve.tensor_tensor(out(1), re(a, 1), re(b, 0), ALU.add)

            def rotate_plain(src, s, half, n, dst):
                a, b = rotate(src, s, half, n, None)
                o_ = dst.rearrange("p (n s d) -> p n s d", s=2, d=half)
                dve.tensor_tensor(o_[:, :, 0, :], a[:, :, 0, :], b[:, :, 1, :], ALU.subtract)
                return dve.tensor_tensor(o_[:, :, 1, :], a[:, :, 1, :], b[:, :, 0, :], ALU.add)

            def body(n, R, sample=False):
                i, u = n
                s = u % 2
                before = (i, u - 1)
                decay = c[0:R, C_DECS:C_DECS + RH * NS] if sample else c[:, C_DEC:C_DEC + RH * P]
                qdec = c[:, C_QDS:C_QDS + RH] if sample else c[:, C_QD:C_QD + RH]
                for j, (g, dst) in enumerate((("rq", rq), ("rk", rk))):
                    dve.wait_ge(proj.sem, proj.at(n, ORDER.index(g) + 1))
                    dve.wait_ge(mixed.sem, mixed.at(before, j + 1))
                    if g == "rk":
                        dve.wait_ge(rkd_done.sem, rkd_done.at(before))
                    if g == "rq":
                        dve.wait_ge(x_landed[s], i * 32 + 32 * (u // 2 + 1))
                    rotate_plain(pproj[:, j, :], s, 64, RH, dst[:]).then_inc(roped.sem, 1)
                    dve.drain()
                for j, (g, dst) in enumerate((("q", q), ("qi", qi))):
                    dve.wait_ge(proj.sem, proj.at(n, ORDER.index(g) + 1))
                    dve.wait_ge(mixed.sem, mixed.at(before, 6 + j))
                    rotate_heads(pproj[:, j, :], s, dst[:], None).then_inc(roped.sem, 1)
                    dve.drain()
                dve.wait_ge(mixed.sem, mixed.at(n, 3))
                dve.tensor_tensor(innT[0:R, 0:RH * R], pr[0:R, 0, 0:RH * R], decay, ALU.mult).then_inc(folded.sem, 1)
                dve.wait_ge(proj.sem, proj.at(n, 7))
                dve.wait_ge(stored[s], (u // 2 + 1) * 48 + i * 48)
                dve.wait_ge(mixed.sem, mixed.at(before, 8))
                kv = kiv[:, s, :]
                rotate_plain(pproj[:, 2, 0:192], s, 32, 3, kv[:, 0:192])
                dve.tensor_copy(kv[:, 192:KIV], pproj[:, 2, 192:KIV])
                dve.drain()
                dve.tensor_copy(kid[:], bc(kv[:, P:P + HD], 1, 2)).then_inc(roped.sem, 1)
                if sample:
                    r4 = heads(rqT[:])[:, :, 0:NS].unsqueeze(2).broadcast_to([P, RH, NB, NS])
                    blk = c[:, C_BLK:C_BLK + NB * NS].rearrange("p (b r) -> p b r", b=NB)
                    dve.wait_ge(moved.sem, moved.at(n, 2))
                    dve.wait_ge(proj.sem, proj.at(n))
                    dve.tensor_tensor(rqb, r4, blk.unsqueeze(1).broadcast_to([P, RH, NB, NS]), ALU.mult).then_inc(blk_done, 1)
                    dve.wait_ge(taken.sem, taken.at(n, 1))
                    for b in range(NB):
                        m = dve.tensor_scalar(rvb[:, :, b, :], heads(rv[0:NS, :]), c[0:NS, C_BLKR + b:C_BLKR + b + 1], None, ALU.mult)
                    m.then_inc(blk_done, 1)
                dve.wait_ge(mixed.sem, mixed.at(n, 4))
                dve.tensor_tensor(heads(o[0:R, :]), heads(pr[0:R, 1, :]), bc(qdec[0:R], 2, RD), ALU.mult).then_inc(folded.sem, 1)
                if sample:
                    for h in range(RH):
                        for half in range(2):
                            dve.wait_ge(snew_done, 2 * h + half + 1)
                            st = sst[:, h, half * 4:half * 4 + 4, :].rearrange("p b e -> p (b e)")
                            dve.scalar_tensor_tensor(st, st, float(np.exp(log_gamma()[h] * TS)), pxT[:, half, :],
                                                     ALU.mult, ALU.add).then_inc(snew_taken, 1)
                    dve.wait_ge(mixed.sem, mixed.at(n, 5))
                    dve.memset(stats[0:1, 0, 0:1], 0.0).then_inc(folded.sem, 1)
                    dve.drain()
                else:
                    dve.wait_ge(mixed.sem, mixed.at(n, 5))
                    for h in range(RH):
                        st = state[:, h * P:(h + 1) * P]
                        m = dve.scalar_tensor_tensor(st, st, float(np.exp(log_gamma()[h] * P)), pr[:, 0, h * P:(h + 1) * P],
                                                     ALU.mult, ALU.add)
                    m.then_inc(folded.sem, 1)
                    dve.drain()
                for h in range(RH):
                    dve.bn_stats(stats[0:R, h, :], o[0:R, h * P:(h + 1) * P])
                dve.drain()
                for h in range(RH):
                    dve.bn_aggr(mv[0:R, h, :], stats[0:R, h, :])
                dve.drain()
                dve.tensor_scalar(mv[0:R, :, 1], mv[0:R, :, 1], GN_EPS, None, ALU.add).then_inc(var_done.sem, 1)
                dve.wait_ge(orstd_done.sem, orstd_done.at(n))
                dve.wait_ge(var_done.sem, var_done.at(n))
                dve.wait_ge(gate_done.sem, gate_done.at(n))
                for h in range(RH):
                    oh = o[0:R, h * P:(h + 1) * P]
                    dve.tensor_scalar(oh, oh, mv[0:R, h, 0:1], orstd[0:R, h:h + 1], ALU.subtract, ALU.mult)
                dve.drain()
                dve.tensor_tensor(ret[0:R, s, :], o[0:R, :], gate[0:R, :], ALU.mult).then_inc(ret_done.sem, 1)

            dve.memset(ret[:].rearrange("p s n -> p (s n)"), 0.0)
            dve.drain()
            with dve.Fori(0, PAIRS) as i:
                body((i, 0), P)
                body((i, 1), P)
            body(last, NS, sample=True)

        @block.gpsimd
        def _(pool):
            for s in (xn_done, rkd_done, gate_done, orstd_done):
                s.seed(pool)
            pool.memset(mhalf[:], -0.5)
            pool.wait_ge(consts, 48)
            pool.drain()

            def normalise(n):
                i, u = n
                s = u % 2
                pool.wait_ge(ssq_done.sem, ssq_done.at(n))
                pool.tensor_tensor(rstd[:, s:s + 1], ssq[:, s:s + 1], mhalf[:, 0:1], ALU.pow)
                pool.drain()
                pool.tensor_scalar(xn[:], x[:, s, :], rstd[:, s:s + 1], None, ALU.mult)
                pool.drain()
                pool.tensor_tensor(xn[:], xn[:], gmix[:], ALU.mult).then_inc(xn_done.sem, 1)

            def body(n, R, sample=False):
                i, u = n
                before = (i, u - 1)
                kdec = c[:, C_KDS:C_KDS + RH] if sample else c[:, C_KD:C_KD + RH]
                pool.wait_ge(roped.sem, roped.at(n, 2))
                pool.wait_ge(mixed.sem, mixed.at(before, 5))
                pool.tensor_tensor(heads(rkd[0:R, :]), heads(rk[0:R, :]), bc(kdec[0:R], 2, RD), ALU.mult).then_inc(rkd_done.sem, 1)
                if not sample:
                    normalise((i, u + 1))
                pool.wait_ge(taken.sem, taken.at(n, 2))
                pool.wait_ge(ret_done.sem, ret_done.at(before))
                pool.tensor_tensor(gate[:], rg[:], erg[:], ALU.mult)
                pool.drain()
                pool.tensor_tensor(gate[:], gate[:], gretn[:], ALU.mult).then_inc(gate_done.sem, 1)
                pool.wait_ge(var_done.sem, var_done.at(n))
                pool.wait_ge(ret_done.sem, ret_done.at(before))
                pool.tensor_tensor(orstd[0:R], mv[0:R, :, 1], mhalf[0:R], ALU.pow).then_inc(orstd_done.sem, 1)

            normalise((0, 0))
            with pool.Fori(0, PAIRS) as i:
                body((i, 0), P)
                body((i, 1), P)
            body(last, NS, sample=True)


NSTEP = 24
B_ID, B_CAUSAL, B_HALF, B_W = 0, 128, 256, 256 + NSTEP


def attention_table():
    c = np.zeros((P, B_W), np.float32)
    i = np.arange(P)
    c[:, B_ID:B_ID + P] = np.eye(P)
    c[:, B_CAUSAL:B_CAUSAL + P] = np.where(i[None, :] > i[:, None], -BIG, 0)
    c[:, B_HALF:B_HALF + NSTEP] = 2.0 ** -(np.arange(NSTEP) + 1.0)
    return c


def prompt_phase(nc, t):
    with ExitStack() as ctx:
        sb = lambda name, shape, dt=F32: ctx.enter_context(nc.sbuf_tensor("b_" + name, shape, dt))
        sem = lambda name: ctx.enter_context(nc.semaphore("b_" + name))

        c = sb("consts", [P, B_W])
        ident = c[:, B_ID:B_ID + P]
        kT = sb("kT", [P, NT * P])
        kiT = sb("kiT", [P, NT * P])
        v = sb("v", [P, NT, P])
        wi = sb("wi", [P, NT, IH])
        qT = sb("qT", [P, 2, 4 * P])
        qiT = sb("qiT", [P, 2, 4 * P])
        relu = sb("relu", [P, 3, 512])
        score = sb("score", [P, 2, SEQ])
        mask = sb("mask", [P, 2, SEQ])
        above = sb("above", [P, SEQ])
        band = sb("band", [P, SEQ])
        rank = sb("rank", [P, SEQ])
        lim = sb("lim", [P, 8])
        step = sb("step", [P, NSTEP])
        mid = sb("mid", [P, NSTEP])
        cnt = sb("cnt", [P, NSTEP])
        logit = sb("logit", [P, 2, SEQ])
        mx = sb("mx", [P, 2, 4])
        nb = sb("nb", [P, 4])
        rs = sb("rs", [P, 2, AH])
        rrs = sb("rrs", [P, AH])
        pT = sb("pT", [P, 2, SEQ])
        att = sb("att", [P, 2, AH, HD])
        pi = ctx.enter_context(nc.psum_tensor("b_pi", [P, 2, 512], F32))
        pl = ctx.enter_context(nc.psum_tensor("b_pl", [P, 3, 512], F32))
        pt = ctx.enter_context(nc.psum_tensor("b_pt", [P, 2, 512], F32))
        po = ctx.enter_context(nc.psum_tensor("b_po", [P, 512], F32))

        loaded = sem("loaded")
        q_in = [sem(f"q_in{s}") for s in range(2)]
        qi_in = [sem(f"qi_in{s}") for s in range(2)]
        att_out = [sem(f"att_out{s}") for s in range(2)]
        scored = sem("scored")
        relued = sem("relued")
        weighed = sem("weighed")
        logits = sem("logits")
        masked = sem("masked")
        max_done = sem("max_done")
        exp_done = sem("exp_done")
        turned = sem("turned")
        pT_done = sem("pT_done")
        pv = sem("pv")
        att_done = sem("att_done")
        zeroed = sem("zeroed")

        def chunks(T):
            return [(a, min(512, (T + 1) * P - a)) for a in range(0, (T + 1) * P, 512)]

        FIRST = TOPK // P
        ibase = {T: IH * sum(len(chunks(x)) for x in range(FIRST, T)) for T in range(FIRST, NT + 1)}
        lbase = {T: AH * sum(len(chunks(x)) for x in range(T)) for T in range(NT + 1)}

        def icount(T, hh, k):
            return ibase[T] + hh * len(chunks(T)) + k + 1

        def lcount(T, hh, k):
            return lbase[T] + hh * len(chunks(T)) + k + 1

        def head(hh):
            return hh // 2, hh % 2, hh // 2 + 4 * (hh % 2)

        steps = [(T, hh) for T in range(FIRST - 2, NT) for hh in range(AH)]
        block = ctx.enter_context(nc.Block())

        @block.sync
        def _(sp):
            tr = t.tr[0:SEQ, :].rearrange("(n p) c -> p n c", p=P)
            kv = t.kiv[0:SEQ, :].rearrange("(n p) c -> p n c", p=P)

            def load_q(T):
                if T >= 2:
                    sp.wait_ge(logits, lcount(T - 2, AH - 1, len(chunks(T - 2)) - 1))
                sp.dma_start(qT[:, T % 2, :], tr[:, T, 0:4 * P]).then_inc(q_in[T % 2], 16)

            def load_qi(T):
                if T >= FIRST + 2:
                    sp.wait_ge(scored, icount(T - 2, IH - 1, len(chunks(T - 2)) - 1))
                sp.dma_start(qiT[:, T % 2, :], tr[:, T, 4 * P:8 * P]).then_inc(qi_in[T % 2], 16)

            load_qi(FIRST)
            sp.dma_start(kiT[:].rearrange("p (n c) -> p n c", n=NT), tr[:, :, 9 * P:10 * P]).then_inc(loaded, 16)
            sp.dma_start(wi[:], kv[:, :, 320:328]).then_inc(loaded, 16)
            load_q(0)
            sp.dma_start(kT[:].rearrange("p (n c) -> p n c", n=NT), tr[:, :, 8 * P:9 * P]).then_inc(loaded, 16)
            sp.dma_start(c[:], t.b_c).then_inc(loaded, 16)
            sp.dma_start(v[:], kv[:, :, 192:320]).then_inc(loaded, 16)
            load_q(1)
            load_qi(FIRST + 1)
            for T in range(NT):
                if T + 4 < NT:
                    load_qi(T + 4)
                if T + 2 < NT:
                    load_q(T + 2)
                sp.wait_ge(att_done, T + 1)
                sp.dma_start(t.cat[T * P:(T + 1) * P, 0:512], att[:, T % 2].rearrange("p h d -> p (h d)")).then_inc(att_out[T % 2], 16)
            for s in range(2):
                sp.wait_ge(att_out[s], 16 * (NT // 2))

        @block.tensor
        def _(pe):
            pe.wait_ge(loaded, 80)

            def index(T, hh):
                jj, half, _ = head(hh)
                rows = slice(half * HD, half * HD + HD)
                pe.wait_ge(qi_in[T % 2], 16 * ((T - FIRST) // 2 + 1))
                for k, (a, w_) in enumerate(chunks(T)):
                    n = icount(T, hh, k)
                    if n > 2:
                        pe.wait_ge(relued, n - 2)
                    pe.matmul(pi[:, n % 2, 0:w_], qiT[rows, T % 2, jj * P:(jj + 1) * P], kiT[rows, a:a + w_],
                              start=True, stop=True).then_inc(scored, 1)

            def logit_products(T, hh):
                jj, half, _ = head(hh)
                rows = slice(half * HD, half * HD + HD)
                pe.wait_ge(q_in[T % 2], 16 * (T // 2 + 1))
                for k, (a, w_) in enumerate(chunks(T)):
                    n = lcount(T, hh, k)
                    if n > 3:
                        pe.wait_ge(masked, n - 3)
                    pe.matmul(pl[:, n % 3, 0:w_], qT[rows, T % 2, jj * P:(jj + 1) * P], kT[rows, a:a + w_],
                              start=True, stop=True).then_inc(logits, 1)

            def values(T, hh):
                jj, half, hd = head(hh)
                g = T * AH + hh
                pe.wait_ge(exp_done, g + 1)
                for k, (a, w_) in enumerate(chunks(T)):
                    n = lcount(T, hh, k)
                    if n > 2:
                        pe.wait_ge(pT_done, n - 2)
                    for b in range(0, w_, P):
                        m = pe.transpose(pt[:, n % 2, b:b + P], logit[:, g % 2, a + b:a + b + P], ident)
                    m.then_inc(turned, 1)
                if hh == 0 and T >= 1:
                    pe.wait_ge(att_done, T)
                pe.wait_ge(pT_done, lcount(T, hh, len(chunks(T)) - 1))
                for b in range(T + 1):
                    m = pe.matmul(po[:, hd * HD:(hd + 1) * HD], pT[:, g % 2, b * P:(b + 1) * P],
                                  v[:, b, half * HD:half * HD + HD], start=(b == 0), stop=(b == T))
                m.then_inc(pv, 1)

            for T, hh in steps:
                if T + 2 < NT:
                    index(T + 2, hh)
                if T >= 0:
                    logit_products(T, hh)
                if T * AH + hh >= 1:
                    values((T * AH + hh - 1) // AH, (hh - 1) % AH)
            values(NT - 1, AH - 1)

        @block.scalar
        def _(act):
            def relu_chunks(T, hh):
                for k, (a, w_) in enumerate(chunks(T)):
                    n = icount(T, hh, k)
                    act.wait_ge(scored, n)
                    if n > 3:
                        act.wait_ge(weighed, n - 3)
                    act.activation(relu[:, n % 3, 0:w_], pi[:, n % 2, 0:w_], ACT.Relu).then_inc(relued, 1)

            def copy_probs(T, hh):
                g = T * AH + hh
                if g >= 2:
                    act.wait_ge(pv, g - 1)
                for k, (a, w_) in enumerate(chunks(T)):
                    n = lcount(T, hh, k)
                    act.wait_ge(turned, n)
                    act.activation(pT[:, g % 2, a:a + w_], pt[:, n % 2, 0:w_], ACT.Copy).then_inc(pT_done, 1)

            def exponential(T, hh):
                g = T * AH + hh
                hd = head(hh)[2]
                act.wait_ge(max_done, g + 1)
                lg = logit[:, g % 2, 0:(T + 1) * P]
                act.activation(lg, lg, ACT.Exp, bias=nb[:, g % 4:g % 4 + 1], scale=HD ** -0.5,
                               accum_out=rs[:, T % 2, hd:hd + 1]).then_inc(exp_done, 1)

            for T, hh in steps:
                if T + 2 < NT:
                    relu_chunks(T + 2, hh)
                if T * AH + hh >= 1:
                    copy_probs((T * AH + hh - 1) // AH, (hh - 1) % AH)
                if T >= 0:
                    exponential(T, hh)
            copy_probs(NT - 1, AH - 1)

        @block.vector
        def _(dve):
            dve.memset(mask[:].rearrange("p s n -> p (s n)"), 0.0).then_inc(zeroed, 1)
            dve.wait_ge(zeroed, 1)
            dve.wait_ge(loaded, 80)

            def weigh(T, hh):
                hd = head(hh)[2]
                for k, (a, w_) in enumerate(chunks(T)):
                    n = icount(T, hh, k)
                    dve.wait_ge(relued, n)
                    out, r, w1 = score[:, T % 2, a:a + w_], relu[:, n % 3, 0:w_], wi[:, T, hd:hd + 1]
                    if hh == 0:
                        dve.tensor_scalar(out, r, w1, None, ALU.mult).then_inc(weighed, 1)
                    else:
                        dve.scalar_tensor_tensor(out, r, w1, out, ALU.mult, ALU.add).then_inc(weighed, 1)

            lo, hi, need, took = (lim[:, j:j + 1] for j in range(4))

            def open_range(T):
                s = score[:, T % 2, 0:(T + 1) * P]
                diag = score[:, T % 2, T * P:(T + 1) * P]
                dve.tensor_reduce(lo, s, AX.X, ALU.min)
                dve.drain()
                dve.tensor_tensor(diag, diag, c[:, B_CAUSAL:B_CAUSAL + P], ALU.add)
                dve.drain()
                dve.tensor_reduce(hi, s, AX.X, ALU.max)
                dve.drain()
                dve.tensor_tensor(took, hi, lo, ALU.subtract)
                dve.drain()
                dve.tensor_scalar(step[:], c[:, B_HALF:B_HALF + NSTEP], took, None, ALU.mult)
                dve.drain()
                dve.tensor_tensor(mid[:, 0:1], lo, step[:, 0:1], ALU.add)
                dve.drain()

            def halve(T, k):
                s = score[:, T % 2, 0:(T + 1) * P]
                dve.tensor_scalar(above[:, 0:(T + 1) * P], s, mid[:, k:k + 1], None, ALU.is_ge, ALU.add,
                                  accum_out=cnt[:, k:k + 1])
                dve.drain()
                dve.tensor_scalar(took, cnt[:, k:k + 1], TOPK - 0.5, step[:, k:k + 1], ALU.is_ge, ALU.mult)
                dve.drain()
                if k + 1 < NSTEP:
                    dve.scalar_tensor_tensor(mid[:, k + 1:k + 2], lo, took, step[:, k + 1:k + 2], ALU.add, ALU.add)
                dve.tensor_tensor(lo, lo, took, ALU.add)
                dve.drain()

            def close_range(T):
                n = (T + 1) * P
                s = score[:, T % 2, 0:n]
                dve.tensor_scalar(cnt[:], cnt[:], TOPK - 0.5, BIG, ALU.is_ge, ALU.mult)
                dve.drain()
                dve.tensor_tensor(mid[:], mid[:], cnt[:], ALU.add)
                dve.drain()
                dve.tensor_reduce(took, mid[:], AX.X, ALU.min)
                dve.drain()
                dve.tensor_tensor(hi, hi, took, ALU.min)
                dve.drain()
                dve.tensor_scalar(above[:, 0:n], s, hi, None, ALU.is_gt, ALU.add, accum_out=need)
                dve.drain()
                dve.tensor_scalar(need, need, -1.0, float(TOPK), ALU.mult, ALU.add)
                dve.scalar_tensor_tensor(band[:, 0:n], s, lo, above[:, 0:n], ALU.is_ge, ALU.subtract)
                dve.drain()
                dve.tensor_tensor_scan(rank[:, 0:n], band[:, 0:n], band[:, 0:n], 0.0, ALU.add, ALU.max)
                dve.drain()
                dve.scalar_tensor_tensor(band[:, 0:n], rank[:, 0:n], need, band[:, 0:n], ALU.is_le, ALU.mult)
                dve.drain()
                dve.tensor_tensor(band[:, 0:n], band[:, 0:n], above[:, 0:n], ALU.add)
                dve.drain()
                dve.tensor_scalar(mask[:, T % 2, 0:n], band[:, 0:n], -1.0, BIG, ALU.add, ALU.mult)
                dve.drain()

            def mask_logits(T, hh):
                g = T * AH + hh
                if g >= 2:
                    dve.wait_ge(turned, lcount((g - 2) // AH, (g - 2) % AH, len(chunks((g - 2) // AH)) - 1))
                for k, (a, w_) in enumerate(chunks(T)):
                    n = lcount(T, hh, k)
                    dve.wait_ge(logits, n)
                    dve.tensor_tensor_reduce(logit[:, g % 2, a:a + w_], pl[:, n % 3, 0:w_], mask[:, T % 2, a:a + w_],
                                             1.0, -3.0e38, ALU.add, ALU.max, accum_out=mx[:, g % 2, k:k + 1]).then_inc(masked, 1)
                dve.drain()
                m = mx[:, g % 2, 0:1]
                if len(chunks(T)) > 1:
                    dve.tensor_reduce(m, mx[:, g % 2, 0:len(chunks(T))], AX.X, ALU.max)
                    dve.drain()
                if g >= 4:
                    dve.wait_ge(exp_done, g - 3)
                dve.tensor_scalar(nb[:, g % 4:g % 4 + 1], m, -(HD ** -0.5), None, ALU.mult).then_inc(max_done, 1)

            def normalise(T):
                dve.wait_ge(pv, AH * (T + 1))
                dve.wait_ge(exp_done, AH * (T + 1))
                if T >= 2:
                    dve.wait_ge(att_out[T % 2], 16 * (T // 2))
                dve.reciprocal(rrs[:], rs[:, T % 2, :])
                dve.drain()
                dve.tensor_tensor(att[:, T % 2], po[:].rearrange("p (h d) -> p h d", h=AH), bc(rrs[:], 2, HD), ALU.mult).then_inc(att_done, 1)

            for T in range(FIRST):
                dve.tensor_copy(mask[:, T % 2, T * P:(T + 1) * P], c[:, B_CAUSAL:B_CAUSAL + P])
            dve.drain()
            for T, hh in steps:
                if T + 2 < NT:
                    weigh(T + 2, hh)
                if FIRST <= T + 1 < NT:
                    if hh == 0:
                        open_range(T + 1)
                    for k in range(3 * hh, 3 * hh + 3):
                        halve(T + 1, k)
                    if hh == AH - 1:
                        close_range(T + 1)
                if T >= 0:
                    mask_logits(T, hh)
                if T >= 1 and hh == 1:
                    normalise(T - 1)
                if hh == AH - 1:
                    dve.drain()
            normalise(NT - 1)


S_ID, S_PAIR, S_SAME, S_LOWER, S_NEW, S_SLOT, S_ROWBASE, S_IOTA = 0, 128, 144, 272, 400, 404, 406, 470
S_HALF = S_IOTA + TOPK
S_W = S_HALF + 24
CH = 4
CKEYS = PAST // CH
CPAGES = NPAGES // CH


def sample_table():
    c = np.zeros((P, S_W), np.float32)
    p = np.arange(P)
    c[:, S_ID:S_ID + P] = np.eye(P)
    b2, par, tok = p // 64, p // 32 % 2, p % TS
    c[p, S_PAIR + b2 * 8 + par * 4 + tok] = 1
    part, row = p // NS, p % NS
    c[:, S_SAME:S_SAME + P] = row[:, None] == row[None, :]
    c[:, S_LOWER:S_LOWER + P] = (row[:, None] == row[None, :]) & (part[:, None] < part[None, :])
    new = np.arange(TS)
    c[:, S_NEW:S_NEW + TS] = np.where((part[:, None] == CH - 1) & (new[None, :] <= row[:, None] % TS), 0, -BIG)
    for half in range(2):
        c[:, S_SLOT + half] = p + 1 + P * half
        c[:, S_ROWBASE + half:S_ROWBASE + 2 * NS:2] = np.arange(NS) * NPAGES
    c[:, S_IOTA:S_IOTA + TOPK] = np.arange(TOPK) + 1
    c[:, S_HALF:S_W] = 2.0 ** -(np.arange(NSTEP) + 1.0)
    return c


def sample_index_phase(nc, t):
    with ExitStack() as ctx:
        sb = lambda name, shape, dt=F32: ctx.enter_context(nc.sbuf_tensor("s_" + name, shape, dt))
        sem = lambda name: ctx.enter_context(nc.semaphore("s_" + name))
        Q = 4
        GROUPS_Q = 4
        G = Q * GROUPS_Q
        signal = lambda name, per: Signal(sem(name), per, tiles=1)
        PAIRS = NB // 2
        QW = PAGE // Q * HD

        c = sb("consts", [P, S_W])
        ident = c[:, S_ID:S_ID + P]
        pti = sb("pti", [P, NB], I32)
        ptf = sb("ptf", [P, NB])
        rowf = sb("rowf", [P, NB, Q])
        row = sb("row", [P, PAIRS, 2 * Q], U32)
        rown = sb("rown", [P, 2 * Q], U32)
        keys = sb("keys", [P, 2, 2, QW])
        kT = sb("kT", [P, 2, 2, 512])
        qd = sb("qd", [P, IH, NS])
        qb = sb("qb", [P, PAIRS, 2 * 64])
        qn = sb("qn", [P, 2 * 64])
        wv = sb("wv", [P, PAIRS])
        wb = sb("wb", [P, PAIRS, 16])
        wn = sb("wn", [P, 16])
        kin = sb("kin", [P, NS])
        relu = sb("relu", [P, 2, 512])
        out = sb("out", [16, NPAGES, PAGE // 2])
        rnew = sb("rnew", [P, PAIRS * TS])
        onew = sb("onew", [16, PAIRS * TS])
        pk = ctx.enter_context(nc.psum_tensor("s_pk", [P, 2, 2, 512], F32))
        p1 = ctx.enter_context(nc.psum_tensor("s_p1", [P, 2, 512], F32))
        p2 = ctx.enter_context(nc.psum_tensor("s_p2", [P, 2, 512], F32))

        loaded = sem("loaded")
        weights = sem("weights")
        pages = sem("pages")
        ready = sem("ready")
        rows_done = sem("rows_done")
        rown_done = signal("rown_done", 1)
        may_gather = sem("may_gather")
        landed = [sem(f"landed{s}") for s in range(2)]
        new1, new2, new3, new4 = sem("new1"), sem("new2"), sem("new3"), sem("new4")
        pair_ready = signal("pair_ready", 1)
        turned = signal("turned", G)
        kT0 = signal("kT0", G)
        kT1 = signal("kT1", G)
        prod = signal("prod", G)
        relued = signal("relued", G)
        summed = signal("summed", G)
        kept = signal("kept", G)
        stored = sem("stored")
        new_stored = sem("new_stored")

        block = ctx.enter_context(nc.Block())

        @block.sync
        def _(sp):
            sp.sem_inc(stored, 64)
            sp.dma_start(pti[:], t.page_table.rearrange("b p -> p b"), allow_slow_non_contiguous=True).then_inc(pages, 16)
            sp.dma_start(c[:], t.s_c).then_inc(loaded, 16)
            tr = t.tr[SEQ:SEQ + P, :]
            for par in range(2):
                for half in range(2):
                    sp.dma_start(qd[par * HD:(par + 1) * HD, half * 4:half * 4 + 4, :],
                                 tr[half * HD:(half + 1) * HD, 4 * P:8 * P].rearrange("p (j c) -> p j c", j=4)[:, :, 0:NS]).then_inc(loaded, 16)
            sp.dma_start(kin[:], tr[:, 9 * P:9 * P + NS]).then_inc(loaded, 16)
            w = t.kiv[SEQ:SEQ + NS, 320:328].rearrange("(a b t) h -> b h t a", b=2, t=TS)
            for b2 in range(2):
                for par in range(2):
                    for h in range(IH):
                        at = b2 * 64 + par * 32 + h * TS
                        sp.dma_start(wv[at:at + TS, :], w[b2, h], allow_slow_non_contiguous=True).then_inc(weights, 16)
            sp.wait_ge(new4, 1)
            sp.dma_start(t.snew.rearrange("(a r) k -> r a k", a=PAIRS),
                         onew[:].rearrange("r (a k) -> r a k", a=PAIRS)).then_inc(new_stored, 16)
            sp.wait_ge(new_stored, 16)
            sp.nop()
            with sp.Fori(0, PAIRS) as i:
                base = sp.snap(i * 2 * TS)
                dst = t.sscore[bass.ds(base, 2 * TS)].rearrange("(b t) g x k -> b x t g k", b=2)
                sp.wait_ge(kept.sem, kept.at((i, 0)))
                for b2 in range(2):
                    for par in range(2):
                        at = b2 * 8 + par * 4
                        sp.dma_start(dst[b2, par], out[at:at + TS]).then_inc(stored, 16)
            sp.wait_ge(stored, 64 * (PAIRS + 1))

        @block.gpsimd
        def _(pool):
            rown_done.seed(pool)
            src = t.cache_idx.rearrange("n (q w) -> (n q) w", q=Q)
            pool.wait_ge(rows_done, 1)
            with pool.Fori(0, PAIRS) as i:
                pool.tensor_copy(rown[:], row[:, bass.ds(i, 1), :].rearrange("p a n -> p (a n)")).then_inc(rown_done.sem, 1)
                pool.wait_ge(rown_done.sem, rown_done.at((i, 0)))
                for q in range(Q):
                    if q >= 2:
                        pool.wait_ge(turned.sem, turned.at((i, 0), GROUPS_Q * (q - 1)))
                    else:
                        pool.wait_ge(turned.sem, turned.at((i, -1), GROUPS_Q * (q + 3)))
                    pool.sem_inc(may_gather, 1)
                    for b2 in range(2):
                        pool.indirect_dma_start(out=keys[:, q % 2, b2, :], out_offset=None, in_=src,
                                                in_offset=bass.IndirectOffsetOnAxis(ap=rown[:, b2 * Q + q:b2 * Q + q + 1], axis=0)
                                                ).then_inc(landed[q % 2], 16)
                for s in range(2):
                    pool.wait_ge(landed[s], i * 64 + 64)

        @block.tensor
        def _(pe):
            for s in (turned, prod, summed):
                s.seed(pe)
            pe.wait_ge(loaded, 16 * 6)
            pe.wait_ge(ready, 1)
            for a in range(PAIRS):
                for b2 in range(2):
                    m = pe.matmul(p1[b2 * 64:b2 * 64 + 64, 0, a * TS:(a + 1) * TS], qb[:, a, b2 * 64:b2 * 64 + 64],
                                  kin[:, (2 * a + b2) * TS:(2 * a + b2 + 1) * TS], start=True, stop=True)
            m.then_inc(new1, 1)
            pe.wait_ge(new2, 1)
            for a in range(PAIRS):
                m = pe.matmul(p2[0:16, 0, a * TS:(a + 1) * TS], wb[:, a, :], rnew[:, a * TS:(a + 1) * TS], start=True, stop=True)
            m.then_inc(new3, 1)

            def turn(i, g):
                q, gq = divmod(g, GROUPS_Q)
                if gq == 0:
                    pe.wait_ge(landed[q % 2], i * 64 + 32 * (q // 2 + 1))
                for k in (kT0, kT1):
                    pe.wait_ge(k.sem, k.at((i, 0), g - 1))
                for b2 in range(2):
                    for j in range(4):
                        at = (gq * 4 + j) * 2 * HD
                        m = pe.transpose(pk[:, g % 2, b2, j * P:(j + 1) * P], keys[:, q % 2, b2, at:at + 2 * HD], ident)
                m.then_inc(turned.sem, 1)

            def products(i, g):
                pe.wait_ge(relued.sem, relued.at((i, 0), g - 1))
                for b2, k in enumerate((kT0, kT1)):
                    pe.wait_ge(k.sem, k.at((i, 0), g + 1))
                    m = pe.matmul(p1[b2 * 64:b2 * 64 + 64, g % 2, :], qn[:, b2 * 64:b2 * 64 + 64], kT[:, g % 2, b2, :],
                                  start=True, stop=True)
                m.then_inc(prod.sem, 1)

            def sums(i, g):
                pe.wait_ge(kept.sem, kept.at((i, 0), g - 1))
                pe.wait_ge(relued.sem, relued.at((i, 0), g + 1))
                pe.matmul(p2[0:16, g % 2, :], wn[:], relu[:, g % 2, :], start=True, stop=True).then_inc(summed.sem, 1)

            pe.wait_ge(new4, 1)
            with pe.Fori(0, PAIRS) as i:
                for g in range(G + 2):
                    if g < G:
                        turn(i, g)
                    if g == 1:
                        pe.wait_ge(pair_ready.sem, pair_ready.at((i, 0)))
                    if 1 <= g <= G:
                        products(i, g - 1)
                    if g >= 2:
                        sums(i, g - 2)

        @block.scalar
        def _(act):
            for s in (kT0, relued):
                s.seed(act)
            act.wait_ge(new1, 1)
            act.activation(rnew[:], p1[:, 0, 0:PAIRS * TS], ACT.Relu).then_inc(new2, 1)

            with act.Fori(0, PAIRS) as i:
                for g in range(G + 1):
                    if g < G:
                        act.wait_ge(turned.sem, turned.at((i, 0), g + 1))
                        act.wait_ge(prod.sem, prod.at((i, 0), g - 1))
                        act.activation(kT[:, g % 2, 0, :], pk[:, g % 2, 0, :], ACT.Copy).then_inc(kT0.sem, 1)
                    if g >= 1:
                        h = g - 1
                        act.wait_ge(prod.sem, prod.at((i, 0), h + 1))
                        act.wait_ge(summed.sem, summed.at((i, 0), h - 1))
                        act.activation(relu[:, h % 2, :], p1[:, h % 2, :], ACT.Relu).then_inc(relued.sem, 1)

        @block.vector
        def _(dve):
            for s in (pair_ready, kT1, kept):
                s.seed(dve)
            dve.memset(qb[:].rearrange("p a n -> p (a n)"), 0.0)
            dve.wait_ge(pages, 16)
            dve.tensor_copy(ptf[:], pti[:])
            dve.drain()
            for q in range(Q):
                dve.tensor_scalar(rowf[:, :, q], ptf[:], float(Q), float(q), ALU.mult, ALU.add)
            dve.drain()
            dve.tensor_copy(row[:].rearrange("p a n -> p (a n)"), rowf[:].rearrange("p b q -> p (b q)")).then_inc(rows_done, 1)
            dve.wait_ge(loaded, 16 * 6)
            dve.wait_ge(weights, 16 * 4 * IH)
            for par in range(2):
                rows = slice(par * HD, (par + 1) * HD)
                dst = qb[rows].rearrange("p a (b x h t) -> p (a b) x h t", b=2, x=2, h=IH)[:, :, par]
                dve.tensor_copy(dst, qd[rows].rearrange("p h (b t) -> p b h t", b=NB))
            for a in range(PAIRS):
                m = dve.tensor_scalar(wb[:, a, :], c[:, S_PAIR:S_PAIR + 16], wv[:, a:a + 1], None, ALU.mult)
            dve.drain().then_inc(ready, 1)
            dve.wait_ge(new3, 1)
            dve.tensor_copy(onew[:], p2[0:16, 0, 0:PAIRS * TS]).then_inc(new4, 1)

            with dve.Fori(0, PAIRS) as i:
                dve.wait_ge(summed.sem, summed.at((i, -1)))
                dve.wait_ge(stored, i * 64 + 64)
                dve.tensor_copy(qn[:], qb[:, bass.ds(i, 1), :].rearrange("p a n -> p (a n)"))
                dve.tensor_copy(wn[:], wb[:, bass.ds(i, 1), :].rearrange("p a n -> p (a n)"))
                dve.drain().then_inc(pair_ready.sem, 1)
                for g in range(G + 2):
                    if g < G:
                        dve.wait_ge(turned.sem, turned.at((i, 0), g + 1))
                        dve.wait_ge(prod.sem, prod.at((i, 0), g - 1))
                        dve.tensor_copy(kT[:, g % 2, 1, :], pk[:, g % 2, 1, :]).then_inc(kT1.sem, 1)
                    if g >= 2:
                        h = g - 2
                        dve.wait_ge(summed.sem, summed.at((i, 0), h + 1))
                        dve.tensor_copy(out[:, :, h * 4:h * 4 + 4].rearrange("r g k -> r k g"),
                                        p2[0:16, h % 2, :].rearrange("r (k g) -> r k g", k=4)).then_inc(kept.sem, 1)


TABW = PAGE + 1


def sample_select_phase(nc, t):
    with ExitStack() as ctx:
        sb = lambda name, shape, dt=F32: ctx.enter_context(nc.sbuf_tensor("k_" + name, shape, dt))
        sem = lambda name: ctx.enter_context(nc.semaphore("k_" + name))
        N = CKEYS + TS
        c = sb("consts", [P, S_W])
        ident = c[:, S_ID:S_ID + P]
        raw = sb("raw", [P, CKEYS])
        score = sb("score", [P, N])
        new = sb("new", [P, TS])
        above = sb("above", [P, N])
        band = sb("band", [P, N])
        rank = sb("rank", [P, N])
        table = sb("table", [P, CPAGES, TABW])
        phi = sb("phi", [P, CPAGES], I32)
        ends = sb("ends", [P, CPAGES])
        newmask = sb("newmask", [P, TS])
        ext = sb("ext", [P, 2])
        extr = sb("extr", [2, CH, NS])
        lim = sb("lim", [P, 8])
        pair = sb("pair", [P, 2])
        step = sb("step", [P, NSTEP])
        mid = sb("mid", [P, NSTEP])
        cnt = sb("cnt", [P, NSTEP])
        tot = sb("tot", [P, NSTEP])
        ps = ctx.enter_context(nc.psum_tensor("k_ps", [P, 2, 512], F32))
        lo, hi, took, need = (lim[:, j:j + 1] for j in range(4))

        loaded, new_in, pages_in = sem("loaded"), sem("new_in"), sem("pages_in")
        new_clear = sem("new_clear")
        asked = sem("asked")
        told = sem("told")
        done, stored = sem("done"), sem("stored")
        block = ctx.enter_context(nc.Block())

        @block.sync
        def _(sp):
            for a in range(CH):
                sp.dma_start(raw[a * NS:(a + 1) * NS, :],
                             t.sscore.rearrange("r (c g) x k -> c r (g x k)", c=CH)[a]).then_inc(loaded, 16)
            sp.dma_start(c[:], t.s_c).then_inc(loaded, 16)
            for a in range(CH):
                for b in range(NB):
                    at = a * NS + b * TS
                    sp.dma_start(phi[at:at + TS, :], t.page_table[b, a * CPAGES:(a + 1) * CPAGES].partition_broadcast(TS)
                                 ).then_inc(pages_in, 16)
            sp.wait_ge(new_clear, 1)
            sp.dma_start(new[(CH - 1) * NS:P, :], t.snew.rearrange("(b x t) k -> x b t k", x=2, t=TS)[0]).then_inc(new_in, 16)
            sp.wait_ge(done, 1)
            for a in range(CH):
                rows = slice(a * NS, (a + 1) * NS)
                sp.dma_start(t.table.rearrange("(r c g) n -> c r (g n)", r=NS, c=CH)[a],
                             table[rows].rearrange("p g n -> p (g n)")).then_inc(stored, 16)
                sp.dma_start(t.pagecum.rearrange("r (c g) -> c r g", c=CH)[a], ends[rows, :]).then_inc(stored, 16)
            sp.dma_start(t.newmask, newmask[(CH - 1) * NS:P, :]).then_inc(stored, 16)
            sp.wait_ge(stored, 16 * (2 * CH + 1))

        asks = ["turn", "back"] + ["same"] * NSTEP + ["same", "lower", "lower"]

        @block.tensor
        def _(pe):
            pe.wait_ge(loaded, 16 * (CH + 1))
            for n, kind in enumerate(asks):
                pe.wait_ge(asked, n + 1)
                out = ps[:, n % 2, :]
                if kind == "turn":
                    m = pe.transpose(out[0:2, 0:P], ext[:], ident)
                elif kind == "back":
                    m = pe.transpose(out[:, 0:2], extr[:].rearrange("x c r -> x (c r)"), ident[0:2, 0:2])
                elif kind == "same":
                    src = cnt[:, n - 2:n - 1] if n < 2 + NSTEP else pair[:, 0:1]
                    m = pe.matmul(out[:, 0:1], c[:, S_SAME:S_SAME + P], src, start=True, stop=True)
                else:
                    m = pe.matmul(out[:, 0:1], c[:, S_LOWER:S_LOWER + P], pair[:, 1:2], start=True, stop=True)
                m.then_inc(told, 1)

        @block.scalar
        def _(act):
            pass

        @block.vector
        def _(dve):
            asked_n = [0]

            def ask(ins):
                ins.then_inc(asked, 1)
                asked_n[0] += 1
                dve.wait_ge(told, asked_n[0])
                return ps[:, (asked_n[0] - 1) % 2, :]

            dve.memset(new[:], 0.0).then_inc(new_clear, 1)
            dve.wait_ge(loaded, 16 * (CH + 1))
            dve.tensor_copy(score[:, 0:CKEYS].rearrange("p (g k x) -> p g x k", g=CPAGES, x=2),
                            raw[:].rearrange("p (g x k) -> p g x k", g=CPAGES, x=2))
            dve.wait_ge(new_in, 16)
            dve.tensor_tensor(score[:, CKEYS:N], new[:], c[:, S_NEW:S_NEW + TS], ALU.add)
            dve.drain()
            dve.tensor_reduce(ext[:, 0:1], score[:], AX.X, ALU.max)
            dve.tensor_reduce(ext[:, 1:2], score[:, 0:CKEYS], AX.X, ALU.min)
            dve.drain()
            out = ask(dve.tensor_scalar(ext[:, 1:2], ext[:, 1:2], -1.0, None, ALU.mult))
            dve.tensor_reduce(extr[:, 0, :], out[0:2, 0:P].rearrange("x (c r) -> x r c", c=CH), AX.X, ALU.max)
            dve.drain()
            out = ask(dve.tensor_copy(extr[:, 1:CH, :], bc(extr[:, 0, :], 1, CH - 1)))
            dve.tensor_copy(hi, out[:, 0:1])
            dve.tensor_scalar(lo, out[:, 1:2], -1.0, None, ALU.mult)
            dve.drain()
            dve.tensor_tensor(took, hi, lo, ALU.subtract)
            dve.drain()
            dve.tensor_scalar(step[:], c[:, S_HALF:S_HALF + NSTEP], took, None, ALU.mult)
            dve.drain()
            dve.tensor_tensor(mid[:, 0:1], lo, step[:, 0:1], ALU.add)
            dve.drain()
            for k in range(NSTEP):
                out = ask(dve.tensor_scalar(above[:], score[:], mid[:, k:k + 1], None, ALU.is_ge, ALU.add,
                                            accum_out=cnt[:, k:k + 1]))
                dve.tensor_copy(tot[:, k:k + 1], out[:, 0:1])
                dve.tensor_scalar(took, out[:, 0:1], TOPK - 0.5, step[:, k:k + 1], ALU.is_ge, ALU.mult)
                dve.drain()
                if k + 1 < NSTEP:
                    dve.scalar_tensor_tensor(mid[:, k + 1:k + 2], lo, took, step[:, k + 1:k + 2], ALU.add, ALU.add)
                dve.tensor_tensor(lo, lo, took, ALU.add)
                dve.drain()
            dve.tensor_scalar(tot[:], tot[:], TOPK - 0.5, BIG, ALU.is_ge, ALU.mult)
            dve.drain()
            dve.tensor_tensor(mid[:], mid[:], tot[:], ALU.add)
            dve.drain()
            dve.tensor_reduce(took, mid[:], AX.X, ALU.min)
            dve.drain()
            dve.tensor_tensor(hi, hi, took, ALU.min)
            dve.drain()
            out = ask(dve.tensor_scalar(above[:], score[:], hi, None, ALU.is_gt, ALU.add, accum_out=pair[:, 0:1]))
            dve.tensor_scalar(need, out[:, 0:1], -1.0, float(TOPK), ALU.mult, ALU.add)
            dve.scalar_tensor_tensor(band[:], score[:], lo, above[:], ALU.is_ge, ALU.subtract)
            dve.drain()
            dve.tensor_tensor_scan(rank[:], band[:], band[:], 0.0, ALU.add, ALU.max)
            dve.drain()
            out = ask(dve.tensor_copy(pair[:, 1:2], rank[:, N - 1:N]))
            dve.tensor_tensor(need, need, out[:, 0:1], ALU.subtract)
            dve.drain()
            dve.scalar_tensor_tensor(band[:], rank[:], need, band[:], ALU.is_le, ALU.mult)
            dve.drain()
            dve.tensor_tensor(band[:], band[:], above[:], ALU.add)
            dve.drain()
            dve.tensor_scalar(newmask[:], band[:, CKEYS:N], -1.0, BIG, ALU.add, ALU.mult)
            dve.tensor_tensor_scan(rank[:, 0:CKEYS], band[:, 0:CKEYS], band[:, 0:CKEYS], 0.0, ALU.add, ALU.max)
            dve.drain()
            out = ask(dve.tensor_copy(pair[:, 1:2], rank[:, CKEYS - 1:CKEYS]))
            dve.tensor_copy(lo, out[:, 0:1])
            dve.drain()
            dve.tensor_scalar(table[:, :, 0:PAGE], rank[:, 0:CKEYS].rearrange("p (g n) -> p g n", g=CPAGES), lo, None, ALU.add)
            dve.wait_ge(pages_in, 16 * CH * NB)
            dve.tensor_copy(table[:, :, PAGE], phi[:])
            dve.drain()
            dve.tensor_copy(ends[:], table[:, :, PAGE - 1])
            dve.drain().then_inc(done, 1)


def sample_attend_phase(nc, t):
    with ExitStack() as ctx:
        sb = lambda name, shape, dt=F32: ctx.enter_context(nc.sbuf_tensor("g_" + name, shape, dt))
        sem = lambda name: ctx.enter_context(nc.semaphore("g_" + name))
        S2 = 2 * NS
        W = TOPK + TS
        HALFR = NS // 2

        c = sb("consts", [P, S_W])
        ident = c[:, S_ID:S_ID + P]
        cum = sb("cum", [P, NS, NPAGES])
        less = sb("less", [P, NS, NPAGES])
        page = sb("page", [P, NS, 2])
        rowt = sb("rowt", [P, S2], U32)
        pages = sb("pages", [P, S2, TABW])
        off = sb("off", [P, NS, 2])
        rowk = sb("rowk", [P, S2], U32)
        kg = sb("kg", [P, S2, P])
        vg = sb("vg", [P, S2, P])
        kT = sb("kT", [P, NS, W])
        kn = sb("kn", [P, NS])
        vn = sb("vn", [TS, NB, P])
        qT = sb("qT", [P, 4, NS])
        qz = sb("qz", [P, NS * P + 256])
        have = sb("have", [P, 2])
        mask = sb("mask", [P, 2, W])
        logit = sb("logit", [P, 2, W])
        mx = sb("mx", [P, 4])
        rs = sb("rs", [P, 2])
        pT = sb("pT", [P, 2, 2, P])
        pTn = sb("pTn", [TS, 2, P])
        at_ = sb("at", [P, 4, NS])
        att = sb("att", [NS, KVH, 4, HD])
        pk = ctx.enter_context(nc.psum_tensor("g_pk", [P, 4, 512], F32))
        pl = ctx.enter_context(nc.psum_tensor("g_pl", [P, 2, 512], F32))
        po = ctx.enter_context(nc.psum_tensor("g_po", [P, 512], F32))
        pf = ctx.enter_context(nc.psum_tensor("g_pf", [P, 512], F32))

        loaded, cum_in, q_in = sem("loaded"), sem("cum_in"), sem("q_in")
        rowt_done, rowk_done = sem("rowt_done"), sem("rowk_done")
        pages_in, k_in, v_in = sem("pages_in"), sem("k_in"), sem("v_in")
        q_ready = sem("q_ready")
        turned, kT_done = sem("turned"), sem("kT_done")
        logits, max_done, exp_done, normed = sem("logits"), sem("max_done"), sem("exp_done"), sem("normed")
        pturned, pT_done = sem("pturned"), sem("pT_done")
        pv, att_done, fturned, out_done, stored = sem("pv"), sem("att_done"), sem("fturned"), sem("out_done"), sem("stored")
        block = ctx.enter_context(nc.Block())

        @block.sync
        def _(sp):
            sp.dma_start(cum[:].rearrange("p r g -> p (r g)"),
                         t.pagecum.rearrange("r g -> (r g)").partition_broadcast(P)).then_inc(cum_in, 16)
            sp.dma_start(c[:], t.s_c).then_inc(loaded, 16)
            tr = t.tr[SEQ:SEQ + P, :]
            sp.dma_start(qT[:], tr[:, 0:4 * P].rearrange("p (j c) -> p j c", j=4)[:, :, 0:NS]).then_inc(q_in, 16)
            sp.dma_start(kn[:], tr[:, 8 * P:8 * P + NS]).then_inc(q_in, 16)
            sp.dma_start(vn[:], t.kiv[SEQ:SEQ + NS, 192:320].rearrange("(b t) d -> t b d", b=NB)).then_inc(q_in, 16)
            for g in range(2):
                for r in range(HALFR):
                    row = g * HALFR + r
                    sp.dma_start(have[r * AH:(r + 1) * AH, g:g + 1],
                                 t.pagecum[row, NPAGES - 1:NPAGES].partition_broadcast(AH)).then_inc(q_in, 16)
                    sp.dma_start(mask[r * AH:(r + 1) * AH, g, TOPK:W],
                                 t.newmask[row, :].partition_broadcast(AH)).then_inc(q_in, 16)
            sp.wait_ge(out_done, 1)
            sp.dma_start(t.cat[SEQ:SEQ + NS, 0:512], att[:].rearrange("p v j d -> p (v j d)")).then_inc(stored, 16)
            sp.wait_ge(stored, 16)

        @block.gpsimd
        def _(pool):
            pool.wait_ge(rowt_done, 1)
            for s in range(S2):
                pool.indirect_dma_start(out=pages[:, s, :], out_offset=None, in_=t.table,
                                        in_offset=bass.IndirectOffsetOnAxis(ap=rowt[:, s:s + 1], axis=0)).then_inc(pages_in, 16)
            pool.wait_ge(rowk_done, 1)
            for s in range(S2):
                pool.indirect_dma_start(out=kg[:, s, :], out_offset=None, in_=t.cache_k,
                                        in_offset=bass.IndirectOffsetOnAxis(ap=rowk[:, s:s + 1], axis=0)).then_inc(k_in, 16)
            for s in range(S2):
                pool.indirect_dma_start(out=vg[:, s, :], out_offset=None, in_=t.cache_v,
                                        in_offset=bass.IndirectOffsetOnAxis(ap=rowk[:, s:s + 1], axis=0)).then_inc(v_in, 16)
            pool.wait_ge(k_in, 16 * S2)
            pool.wait_ge(v_in, 16 * S2)

        KG = S2 // 4

        @block.tensor
        def _(pe):
            pe.wait_ge(loaded, 16)
            pe.wait_ge(k_in, 16 * S2)
            for n in range(KG):
                if n >= 4:
                    pe.wait_ge(kT_done, n - 3)
                for j in range(4):
                    m = pe.transpose(pk[:, n % 4, j * P:(j + 1) * P], kg[:, 4 * n + j, :], ident)
                m.then_inc(turned, 1)
            pe.wait_ge(q_ready, 1)
            pe.wait_ge(kT_done, KG)
            for g in range(2):
                for r in range(HALFR):
                    row = g * HALFR + r
                    m = pe.matmul(pl[:, g, 0:W], qz[:, row * P:(row + 1) * P], kT[:, row, :], start=(r == 0), stop=(r == HALFR - 1))
                m.then_inc(logits, 1)
            for g in range(2):
                pe.wait_ge(normed, g + 1)
                for half in range(2):
                    pe.transpose(pk[:, g, half * P:(half + 1) * P], logit[:, g, half * P:(half + 1) * P], ident)
                pe.transpose(pk[0:TS, g, 2 * P:3 * P], logit[:, g, TOPK:W], ident).then_inc(pturned, 1)
            pe.wait_ge(pT_done, 2)
            pe.wait_ge(v_in, 16 * S2)
            for row in range(NS):
                g, r = divmod(row, HALFR)
                cols = slice(r * AH, (r + 1) * AH)
                out = po[:, row * AH:(row + 1) * AH]
                for half in range(2):
                    pe.matmul(out, vg[:, 2 * row + half, :], pT[:, g, half, cols], start=(half == 0), stop=False)
                m = pe.matmul(out, vn[:, row // TS, :], pTn[:, g, cols], start=False, stop=True)
            m.then_inc(pv, 1)
            pe.wait_ge(att_done, 1)
            for j in range(4):
                m = pe.transpose(pf[0:NS, j * P:(j + 1) * P], at_[:, j, :], ident)
            m.then_inc(fturned, 1)

        @block.scalar
        def _(act):
            for n in range(KG):
                act.wait_ge(turned, n + 1)
                act.activation(kT[:, 2 * n:2 * n + 2, 0:TOPK], pk[:, n % 4, :].rearrange("p (r c) -> p r c", r=2), ACT.Copy).then_inc(kT_done, 1)
            for g in range(2):
                act.wait_ge(max_done, g + 1)
                act.activation(logit[:, g, :], logit[:, g, :], ACT.Exp, bias=mx[:, 2 + g:3 + g], scale=HD ** -0.5,
                               accum_out=rs[:, g:g + 1]).then_inc(exp_done, 1)

        @block.vector
        def _(dve):
            def slots_less(src, out, width):
                for half in range(2):
                    dve.tensor_scalar(less[:], src(half), c[:, S_SLOT + half:S_SLOT + half + 1], None, ALU.is_lt)
                    dve.drain()
                    dve.tensor_reduce(out[:, :, half], less[:], AX.X, ALU.add)
                    dve.drain()

            flat = lambda a: a[:].rearrange("p r h -> p (r h)")
            dve.wait_ge(loaded, 16)
            dve.wait_ge(cum_in, 16)
            slots_less(lambda half: cum[:], page, NPAGES)
            dve.tensor_scalar(flat(page), flat(page), NPAGES - 1.0, None, ALU.min)
            dve.drain()
            dve.tensor_tensor(flat(page), flat(page), c[:, S_ROWBASE:S_ROWBASE + S2], ALU.add)
            dve.drain()
            dve.tensor_copy(rowt[:], flat(page)).then_inc(rowt_done, 1)
            dve.memset(qz[:], 0.0)
            dve.drain()
            dve.wait_ge(q_in, 16 * (3 + 2 * NS))
            for kv in range(KVH):
                rows = slice(kv * HD, (kv + 1) * HD)
                for g in range(2):
                    at = g * HALFR * P + kv * 4
                    dst = qz[rows, at:at + HALFR * (P + AH)].rearrange("p (r x) -> p r x", x=P + AH)[:, :, 0:4]
                    m = dve.tensor_copy(dst, qT[rows, :, g * HALFR:(g + 1) * HALFR].rearrange("p j r -> p r j"))
            for g in range(2):
                dve.tensor_scalar(mask[:, g, 0:TOPK], c[:, S_IOTA:S_IOTA + TOPK], have[:, g:g + 1], -BIG, ALU.is_gt, ALU.mult)
            dve.tensor_copy(kT[:, :, TOPK:W].rearrange("p (b t) k -> p b t k", b=NB),
                            kn[:].rearrange("p (b k) -> p b k", b=NB).unsqueeze(2).broadcast_to([P, NB, TS, TS]))
            dve.drain().then_inc(q_ready, 1)
            dve.wait_ge(pages_in, 16 * S2)
            slots_less(lambda half: pages[:].rearrange("p (r h) n -> p r h n", h=2)[:, :, half, 0:PAGE], off, PAGE)
            dve.tensor_scalar(flat(off), flat(off), PAGE - 1.0, None, ALU.min)
            dve.drain()
            dve.scalar_tensor_tensor(flat(off), pages[:, :, PAGE], float(PAGE), flat(off), ALU.mult, ALU.add)
            dve.drain()
            dve.tensor_copy(rowk[:], flat(off)).then_inc(rowk_done, 1)
            for g in range(2):
                dve.wait_ge(logits, g + 1)
                dve.tensor_tensor_reduce(logit[:, g, :], pl[:, g, 0:W], mask[:, g, :], 1.0, -3.0e38, ALU.add, ALU.max,
                                         accum_out=mx[:, g:g + 1])
                dve.drain()
                dve.tensor_scalar(mx[:, 2 + g:3 + g], mx[:, g:g + 1], -(HD ** -0.5), None, ALU.mult).then_inc(max_done, 1)
            for g in range(2):
                dve.wait_ge(exp_done, g + 1)
                dve.reciprocal(rs[:, g:g + 1], rs[:, g:g + 1])
                dve.drain()
                dve.tensor_scalar(logit[:, g, :], logit[:, g, :], rs[:, g:g + 1], None, ALU.mult).then_inc(normed, 1)
            for g in range(2):
                dve.wait_ge(pturned, g + 1)
                dve.tensor_copy(pT[:, g].rearrange("p h c -> p (h c)"), pk[:, g, 0:2 * P])
                dve.tensor_copy(pTn[:, g, :], pk[0:TS, g, 2 * P:3 * P])
                dve.drain().then_inc(pT_done, 1)
            dve.wait_ge(pv, 1)
            for kv in range(KVH):
                rows = slice(kv * HD, (kv + 1) * HD)
                dve.tensor_copy(at_[rows], po[rows, 0:NS * AH].rearrange("p (r v j) -> p v j r", v=KVH, j=4)[:, kv])
            dve.drain().then_inc(att_done, 1)
            dve.wait_ge(fturned, 1)
            dve.tensor_copy(att[:], pf[0:NS, :].rearrange("p (j v d) -> p v j d", j=4, v=KVH)).then_inc(out_done, 1)


CK = 416
TT = 104
NCHUNK = (SEQ + NS) // CK
FB = DFF // P


def dense_phase(nc, t):
    with ExitStack() as ctx:
        sb = lambda name, shape, dt=F32: ctx.enter_context(nc.sbuf_tensor("d_" + name, shape, dt))
        sem = lambda name: ctx.enter_context(nc.semaphore("d_" + name))
        signal = lambda name, per: Signal(sem(name), per, tiles=1)
        RING = 3
        ident = sb("ident", [P, P])[:]
        ones = sb("ones", [P, P])
        gains = sb("gains", [P, 3, KD])
        wo = sb("wo", [P, KD, D])
        wg = sb("wg", [P, KD, D])
        wp = sb("wp", [P, PLE // P, D])
        ring = sb("ring", [P, RING, FB * P])
        catx = sb("catx", [TT, 2, 2, D])
        ple = sb("ple", [TT, 2, PLE])
        hT = sb("hT", [P, KD, CK])
        nT = sb("nT", [P, KD, CK])
        pT = sb("pT", [P, PLE // P, CK])
        aT = sb("aT", [P, FB, CK])
        sq = sb("sq", [P, 2, CK])
        acc = sb("acc", [P, CK])
        ms = sb("ms", [TT, 4])
        rstd = sb("rstd", [TT, 4])
        mhalf = sb("mhalf", [TT, 4])
        sig = sb("sig", [P, 2, CK])
        y = sb("y", [TT, 2, 512])
        pm = ctx.enter_context(nc.psum_tensor("d_pm", [P, 4, 512], F32))
        pt = ctx.enter_context(nc.psum_tensor("d_pt", [P, 2, 512], F32))
        pn = ctx.enter_context(nc.psum_tensor("d_pn", [P, 512], F32))
        pb = ctx.enter_context(nc.psum_tensor("d_pb", [P, 512], F32))

        ITEMS = FB + KD
        MM = KD + 2 * FB + KD + 2 * KD
        loaded = sem("loaded")
        loaded2 = sem("loaded2")
        in_landed = [sem(f"in_landed{s}") for s in range(2)]
        w_landed = [sem(f"w_landed{s}") for s in range(RING)]
        y_stored = [sem(f"y_stored{s}") for s in range(2)]
        ones_done = sem("ones_done")
        turned = signal("turned", 28)
        cat_moved = signal("cat_moved", 12)
        x_moved = signal("x_moved", 8)
        y_moved = signal("y_moved", 8)
        prod = signal("prod", MM)
        used = signal("used", MM)
        summed = signal("summed", 3 * KD)
        squared = signal("squared", 3 * KD)
        ms_psum = signal("ms_psum", 3)
        ms_done = signal("ms_done", 3)
        rstd_done = signal("rstd_done", 3)
        spread = signal("spread", 3)
        sq_added = signal("sq_added", 3 * KD)
        normed = signal("normed", 3 * KD)
        sig_done = signal("sig_done", FB + KD)
        act_done = signal("act_done", FB)

        OUT0, FFN0, DOWN0, PLE0 = 0, KD, KD + 2 * FB, 2 * KD + 2 * FB
        block = ctx.enter_context(nc.Block())

        @block.sync
        def _(sp):
            sp.dma_start(ident, t.c[:, C_ID:C_ID + P]).then_inc(loaded, 16)
            for j, g in enumerate((t.g_ffn, t.g_ple, t.g_final)):
                sp.dma_start(gains[:, j, :], g.rearrange("(k p) -> p k", p=P), allow_slow_non_contiguous=True).then_inc(loaded, 16)
            sp.dma_start(wo[:], t.w_out.rearrange("(k p) n -> p k n", p=P)).then_inc(loaded, 16)
            with sp.Fori(0, NCHUNK) as i:
                rows = [sp.snap(i * CK + j * TT) for j in range(4)]
                for j in range(4):
                    sp.wait_ge(turned.sem, turned.at((i, 0), 5 * (j - 1)) if j >= 2 else turned.at((i, -1), 5 * (j + 3)))
                    s = j % 2
                    sp.dma_start(catx[:, s, 0, :], t.cat[bass.ds(rows[j], TT), :]).then_inc(in_landed[s], 16)
                    sp.dma_start(catx[:, s, 1, :], t.x[bass.ds(rows[j], TT), :]).then_inc(in_landed[s], 16)
                    sp.dma_start(ple[:, s, :], t.p[bass.ds(rows[j], TT), :]).then_inc(in_landed[s], 16)
                for n in range(ITEMS):
                    s = n % RING
                    before = (n - RING) % ITEMS
                    sp.wait_ge(prod.sem, prod.at((i, (n - RING) // ITEMS), FFN0 + 2 * before + 2 if before < FB else DOWN0 + before - FB + 1))
                    if n < FB:
                        for part in range(2):
                            src = t.w_ffn_in[:, part * DFF + n * P:part * DFF + (n + 1) * P]
                            sp.dma_start(ring[:, s, part * KD * P:(part + 1) * KD * P].rearrange("p (k c) -> p k c", k=KD),
                                         src.rearrange("(k p) c -> p k c", p=P)).then_inc(w_landed[s], 16)
                    else:
                        src = t.w_ffn_out[:, (n - FB) * P:(n - FB + 1) * P].rearrange("(f p) c -> p f c", p=P)
                        for part in range(2):
                            f = slice(part * FB // 2, (part + 1) * FB // 2)
                            sp.dma_start(ring[:, s, :].rearrange("p (f c) -> p f c", f=FB)[:, f], src[:, f]).then_inc(w_landed[s], 16)

        @block.tensor
        def _(pe):
            for s in (turned, prod, ms_psum, spread):
                s.seed(pe)
            pe.wait_ge(loaded, 16 * 5)
            pe.wait_ge(ones_done, 1)

            def turn_inputs(i, j):
                s = j % 2
                pe.wait_ge(in_landed[s], i * 96 + 48 * (j // 2 + 1))
                n = (i, 0)
                for b in range(5):
                    at = 5 * j + b
                    before = at - 2
                    if before < 0:
                        pe.wait_ge(y_moved.sem, y_moved.at(n, before + 1))
                    else:
                        jj, bb = divmod(before, 5)
                        if bb in (1, 3):
                            pe.wait_ge(x_moved.sem, x_moved.at(n, 2 * jj + bb // 2 + 1))
                        else:
                            pe.wait_ge(cat_moved.sem, cat_moved.at(n, 3 * jj + bb // 2 + 1))
                    for k in range(4 if b < 4 else 2):
                        col = (b // 2 * 4 + k) * P
                        src = catx[:, s, b % 2, col:col + P] if b < 4 else ple[:, s, k * P:(k + 1) * P]
                        m = pe.transpose(pt[:, at % 2, k * TT:(k + 1) * TT], src, ident[0:TT, 0:TT])
                    m.then_inc(turned.sem, 1)

            def product(i, at, terms):
                pe.wait_ge(used.sem, used.at((i, 0), at - 3))
                for n, (w_, a) in enumerate(terms):
                    m = pe.matmul(pm[:, at % 4, 0:CK], w_, a, start=(n == 0), stop=(n == len(terms) - 1))
                m.then_inc(prod.sem, 1)
                return m

            def mean_square(i, j):
                pe.wait_ge(sq_added.sem, sq_added.at((i, 0), (j + 1) * KD))
                pe.wait_ge(ms_done.sem, ms_done.at((i, 0), j))
                for b in range(4):
                    m = pe.matmul(pn[0:TT, b:b + 1], acc[:, b * TT:(b + 1) * TT], ones[:, 0:1], start=True, stop=True)
                m.then_inc(ms_psum.sem, 1)
                pe.wait_ge(rstd_done.sem, rstd_done.at((i, 0), j + 1))
                pe.wait_ge(normed.sem, normed.at((i, 0), j * KD))
                for b in range(4):
                    m = pe.matmul(pb[:, b * TT:(b + 1) * TT], rstd[:, b:b + 1].broadcast_to([TT, P]), ident[0:TT, 0:TT],
                                  start=True, stop=True)
                m.then_inc(spread.sem, 1)

            with pe.Fori(0, NCHUNK) as i:
                n = (i, 0)
                for j in range(4):
                    turn_inputs(i, j)
                pe.wait_ge(cat_moved.sem, cat_moved.at(n))
                for d in range(KD):
                    product(i, OUT0 + d, [(wo[:, k, d * P:(d + 1) * P], nT[:, k, :]) for k in range(KD)])
                mean_square(i, 0)
                for f in range(FB):
                    if f == 0:
                        pe.wait_ge(normed.sem, normed.at(n, KD))
                    pe.wait_ge(w_landed[f % RING], i * (32 * ITEMS // RING) + 32 * (f // RING + 1))
                    for part in range(2):
                        at = FFN0 + 2 * f + part
                        pe.wait_ge(used.sem, used.at(n, at - 3))
                        for k in range(KD):
                            col = (part * KD + k) * P
                            m = pe.matmul(pm[:, at % 4, 0:CK], ring[:, f % RING, col:col + P], nT[:, k, :],
                                          start=(k == 0), stop=(k == KD - 1))
                        m.then_inc(prod.sem, 1)
                for d in range(KD):
                    item = FB + d
                    pe.wait_ge(act_done.sem, act_done.at(n))
                    pe.wait_ge(w_landed[item % RING], i * (32 * ITEMS // RING) + 32 * (item // RING + 1))
                    product(i, DOWN0 + d, [(ring[:, item % RING, f * P:(f + 1) * P], aT[:, f, :]) for f in range(FB)])
                mean_square(i, 1)
                pe.wait_ge(loaded2, 32)
                for d in range(KD):
                    product(i, PLE0 + 2 * d, [(wp[:, k, d * P:(d + 1) * P], pT[:, k, :]) for k in range(PLE // P)])
                    if d == 0:
                        pe.wait_ge(normed.sem, normed.at(n, 2 * KD))
                    product(i, PLE0 + 2 * d + 1, [(wg[:, k, d * P:(d + 1) * P], nT[:, k, :]) for k in range(KD)])
                mean_square(i, 2)
                pe.wait_ge(normed.sem, normed.at(n, 3 * KD))
                for b in range(8):
                    at = 20 + b
                    if b < 2:
                        pe.wait_ge(x_moved.sem, x_moved.at(n))
                        pe.wait_ge(cat_moved.sem, cat_moved.at(n))
                    else:
                        pe.wait_ge(y_moved.sem, y_moved.at(n, b - 1))
                    j, half = divmod(b, 2)
                    for k in range(4):
                        m = pe.transpose(pt[0:TT, at % 2, k * P:(k + 1) * P], nT[:, half * 4 + k, j * TT:(j + 1) * TT], ident)
                    m.then_inc(turned.sem, 1)

        @block.scalar
        def _(act):
            for s in (cat_moved, squared, ms_done, sig_done):
                s.seed(act)
            for s in range(2):
                act.sem_inc(y_stored[s], 16)
            act.dma_start(wg[:], t.w_ple_gate.rearrange("(k p) n -> p k n", p=P)).then_inc(loaded2, 16)
            act.dma_start(wp[:], t.w_ple_proj.rearrange("(k p) n -> p k n", p=P)).then_inc(loaded2, 16)

            def squares(i, j, ds):
                n = (i, 0)
                for d in ds:
                    act.wait_ge(summed.sem, summed.at(n, j * KD + d + 1))
                    if d == 0:
                        act.wait_ge(ms_psum.sem, ms_psum.at(n, j))
                        act.activation(acc[:], hT[:, 0, :], ACT.Square).then_inc(squared.sem, 1)
                    else:
                        act.wait_ge(sq_added.sem, sq_added.at(n, j * KD + d - 1))
                        act.activation(sq[:, d % 2, :], hT[:, d, :], ACT.Square).then_inc(squared.sem, 1)

            def mean(i, j):
                n = (i, 0)
                act.wait_ge(ms_psum.sem, ms_psum.at(n, j + 1))
                act.wait_ge(rstd_done.sem, rstd_done.at(n, j))
                act.activation(ms[:], pn[0:TT, 0:4], ACT.Copy, scale=1.0 / D, bias=EPS).then_inc(ms_done.sem, 1)

            with act.Fori(0, NCHUNK) as i:
                n = (i, 0)
                rows = [act.snap(i * CK + j * TT) for j in range(4)]
                act.wait_ge(turned.sem, turned.at(n, 0))
                for j in range(4):
                    cols = slice(j * TT, (j + 1) * TT)
                    for b in (0, 2, 4):
                        at = 5 * j + b
                        act.wait_ge(turned.sem, turned.at(n, at + 1))
                        if b == 4:
                            dst, src = pT[:, :, cols], pt[:, at % 2, 0:2 * TT].rearrange("p (k c) -> p k c", k=2)
                        else:
                            dst, src = nT[:, b // 2 * 4:b // 2 * 4 + 4, cols], pt[:, at % 2, 0:4 * TT].rearrange("p (k c) -> p k c", k=4)
                        act.activation(dst, src, ACT.Copy).then_inc(cat_moved.sem, 1)
                squares(i, 0, range(KD))
                mean(i, 0)
                for f in range(FB):
                    act.wait_ge(prod.sem, prod.at(n, FFN0 + 2 * f + 1))
                    act.wait_ge(used.sem, used.at(n, FFN0 + 2 * f - 2))
                    act.activation(sig[:, f % 2, :], pm[:, (FFN0 + 2 * f) % 4, 0:CK], ACT.Sigmoid).then_inc(sig_done.sem, 1)
                squares(i, 1, range(KD))
                mean(i, 1)
                for d in range(KD):
                    at = PLE0 + 2 * d + 1
                    act.wait_ge(prod.sem, prod.at(n, at + 1))
                    act.wait_ge(used.sem, used.at(n, at - 3))
                    act.activation(sig[:, d % 2, :], pm[:, at % 4, 0:CK], ACT.Sigmoid).then_inc(sig_done.sem, 1)
                    if d:
                        squares(i, 2, [d - 1])
                squares(i, 2, [KD - 1])
                mean(i, 2)
                for b in range(8):
                    j, half = divmod(b, 2)
                    act.wait_ge(y_moved.sem, y_moved.at(n, b + 1))
                    act.dma_start(t.y[bass.ds(rows[j], TT), half * 512:(half + 1) * 512], y[:, b % 2, :]).then_inc(y_stored[b % 2], 16)
            for s in range(2):
                act.wait_ge(y_stored[s], 16 + 64 * NCHUNK)

        @block.vector
        def _(dve):
            for s in (x_moved, y_moved, used, summed, normed, act_done):
                s.seed(dve)
            dve.memset(ones[:], 1.0).then_inc(ones_done, 1)
            dve.wait_ge(loaded, 16 * 5)

            def normalise(i, j):
                dve.wait_ge(spread.sem, spread.at((i, 0), j + 1))
                for d in range(KD):
                    dve.scalar_tensor_tensor(nT[:, d, :], hT[:, d, :], gains[:, j, d:d + 1], pb[:, 0:CK], ALU.mult, ALU.mult
                                             ).then_inc(normed.sem, 1)

            def add_block(i, at, d):
                dve.wait_ge(prod.sem, prod.at((i, 0), at + 1))
                m = dve.tensor_tensor(hT[:, d, :], pm[:, at % 4, 0:CK], hT[:, d, :], ALU.add)
                m.then_inc(used.sem, 1)

            with dve.Fori(0, NCHUNK) as i:
                n = (i, 0)
                for j in range(4):
                    cols = slice(j * TT, (j + 1) * TT)
                    for b in (1, 3):
                        at = 5 * j + b
                        dve.wait_ge(turned.sem, turned.at(n, at + 1))
                        dve.tensor_copy(hT[:, b // 2 * 4:b // 2 * 4 + 4, cols],
                                        pt[:, at % 2, 0:4 * TT].rearrange("p (k c) -> p k c", k=4)).then_inc(x_moved.sem, 1)
                dve.drain()
                for d in range(KD):
                    add_block(i, OUT0 + d, d)
                    dve.drain().then_inc(summed.sem, 1)
                normalise(i, 0)
                for f in range(FB):
                    at = FFN0 + 2 * f
                    dve.wait_ge(sig_done.sem, sig_done.at(n, f + 1))
                    dve.tensor_tensor(sig[:, f % 2, :], pm[:, at % 4, 0:CK], sig[:, f % 2, :], ALU.mult).then_inc(used.sem, 1)
                    dve.drain()
                    dve.wait_ge(prod.sem, prod.at(n, at + 2))
                    dve.tensor_tensor(aT[:, f, :], pm[:, (at + 1) % 4, 0:CK], sig[:, f % 2, :], ALU.mult).then_inc(used.sem, 1)
                    dve.drain().then_inc(act_done.sem, 1)
                for d in range(KD):
                    add_block(i, DOWN0 + d, d)
                    dve.drain().then_inc(summed.sem, 1)
                normalise(i, 1)
                for d in range(KD):
                    at = PLE0 + 2 * d
                    dve.wait_ge(sig_done.sem, sig_done.at(n, FB + d + 1))
                    dve.tensor_tensor(sig[:, d % 2, :], pm[:, at % 4, 0:CK], sig[:, d % 2, :], ALU.mult).then_inc(used.sem, 1)
                    dve.drain()
                    dve.tensor_tensor(hT[:, d, :], hT[:, d, :], sig[:, d % 2, :], ALU.add).then_inc(used.sem, 1)
                    dve.drain().then_inc(summed.sem, 1)
                normalise(i, 2)
                for b in range(8):
                    dve.wait_ge(turned.sem, turned.at(n, 21 + b))
                    dve.wait_ge(y_stored[b % 2], i * 64 + 16 * (b // 2 + 1))
                    dve.tensor_copy(y[:, b % 2, :], pt[0:TT, b % 2, :]).then_inc(y_moved.sem, 1)

        @block.gpsimd
        def _(pool):
            for s in (rstd_done, sq_added):
                s.seed(pool)
            pool.memset(mhalf[:], -0.5)
            pool.drain()
            with pool.Fori(0, NCHUNK) as i:
                n = (i, 0)
                for j in range(3):
                    pool.wait_ge(squared.sem, squared.at(n, j * KD + 1))
                    pool.sem_inc(sq_added.sem, 1)
                    for d in range(1, KD):
                        pool.wait_ge(squared.sem, squared.at(n, j * KD + d + 1))
                        pool.tensor_tensor(acc[:], acc[:], sq[:, d % 2, :], ALU.add).then_inc(sq_added.sem, 1)
                        pool.drain()
                    pool.wait_ge(ms_done.sem, ms_done.at(n, j + 1))
                    pool.wait_ge(spread.sem, spread.at(n, j))
                    pool.tensor_tensor(rstd[:], ms[:], mhalf[:], ALU.pow).then_inc(rstd_done.sem, 1)


def build(nc, t):
    project_phase(nc, t)
    prompt_phase(nc, t)
    sample_index_phase(nc, t)
    sample_select_phase(nc, t)
    sample_attend_phase(nc, t)
    dense_phase(nc, t)


class Tensors:
    pass


SCRATCH = {
    "tr": (ROWS, TRW), "cat": (ROWS, D), "sscore": (NS, NPAGES, 2, PAGE // 2), "snew": (NB // 2 * 16, TS),
    "table": (NS * NPAGES, TABW), "pagecum": (NS, NPAGES), "newmask": (NS, TS),
}
OUTPUTS = {"y": (ROWS, D), "kiv": (ROWS, KIV), "retn_prompt": (RH, RD, RD), "retn_sample": (NB, RH, RD, RD)}


def kernel(x_prompt, x_sample, cache_k, cache_v, cache_idx_k, state_retn, page_table, p_prompt, p_sample,
           g_mix, w_in, g_retn, w_out, g_ffn, w_ffn_in, w_ffn_out, g_ple, w_ple_gate, w_ple_proj, g_final):
    import concourse.bacc as bacc
    from concourse.bass_utils import run_bass_kernel_spmd

    def rows(prompt, sample, width):
        a = np.asarray(prompt).reshape(SEQ, width)
        b = np.asarray(sample).reshape(NS, width)
        return np.concatenate([a, b, np.zeros((ROWS - SEQ - NS, width), a.dtype)])

    arr = np.asarray
    ins = {
        "x": rows(x_prompt, x_sample, D), "p": rows(p_prompt, p_sample, PLE),
        "cache_k": arr(cache_k).reshape(-1, KVH * HD), "cache_v": arr(cache_v).reshape(-1, KVH * HD),
        "cache_idx": arr(cache_idx_k).reshape(-1, PAGE * HD), "state_retn": arr(state_retn).reshape(NB, RH, RD, RD),
        "page_table": arr(page_table), "g_mix": arr(g_mix)[0], "w_in": arr(w_in)[0], "g_retn": arr(g_retn)[0],
        "w_out": arr(w_out)[0], "g_ffn": arr(g_ffn)[0], "w_ffn_in": arr(w_ffn_in)[0], "w_ffn_out": arr(w_ffn_out)[0],
        "g_ple": arr(g_ple)[0], "w_ple_gate": arr(w_ple_gate)[0], "w_ple_proj": arr(w_ple_proj)[0],
        "g_final": arr(g_final), "rope": rope_table(), "c": constant_table(), "b_c": attention_table(), "s_c": sample_table(),
    }
    nc = bacc.Bacc("TRN2", target_bir_lowering=False, num_devices=1)
    t = Tensors()
    for name, a in ins.items():
        t.__dict__[name] = nc.dram_tensor(name, a.shape, mybir.dt.from_np(a.dtype), kind="ExternalInput").ap()
    for name, shape in SCRATCH.items():
        t.__dict__[name] = nc.dram_tensor(name, shape, F32, kind="Internal").ap()
    for name, shape in OUTPUTS.items():
        t.__dict__[name] = nc.dram_tensor(name, shape, F32, kind="ExternalOutput").ap()
    build(nc, t)
    r = run_bass_kernel_spmd(nc, [{n: np.ascontiguousarray(a) for n, a in ins.items()}], core_ids=[0]).results[0]
    y, kiv = r["y"], r["kiv"]
    k, ki, v = kiv[:, 0:128], kiv[:, 128:192], kiv[:, 192:320]
    past, new = slice(0, SEQ), slice(SEQ, SEQ + NS)
    return (y[past].reshape(1, SEQ, D), y[new].reshape(NB, TS, D),
            k[past].reshape(1, 1, SEQ, KVH, HD), v[past].reshape(1, 1, SEQ, KVH, HD), ki[past].reshape(1, 1, SEQ, HD),
            r["retn_prompt"].reshape(1, 1, RH, RD, RD),
            k[new].reshape(1, NB, TS, KVH, HD), v[new].reshape(1, NB, TS, KVH, HD), ki[new].reshape(1, NB, TS, HD),
            r["retn_sample"].reshape(1, NB, RH, RD, RD))
```

```python
from contextlib import ExitStack

import numpy as np

import concourse.bass as bass
from concourse import mybir

F32 = mybir.dt.float32
I32 = mybir.dt.int32
U32 = mybir.dt.uint32
ALU = mybir.AluOpType
ACT = mybir.ActivationFunctionType
AX = mybir.AxisListType

P = 128
D = 1024
KD = D // P
SEQ = 2048
NB, TS = 8, 4
NS = NB * TS
PAST = 16384
PAGE = 128
NPAGES = PAST // PAGE
HD = 64
AH, KVH, GRP = 8, 2, 4
IH = 8
TOPK = 256
RH, RD = 4, 128
DFF = 2816
PLE = 256
NT = SEQ // P
ROWS = (NT + 1) * P
EPS, GN_EPS = 1e-6, 1e-5
BIG = 1.0e30

GROUPS = {
    "rq": [(1352, 512)], "rk": [(1864, 512)], "rv": [(2376, 512)], "rg": [(2888, 512)],
    "q": [(0, 512)], "qi": [(768, 512)], "kiv": [(512, 128), (1280, 64), (640, 128), (1344, 8)],
}
ORDER = ["rq", "rk", "rv", "rg", "q", "qi", "kiv"]
WIDTH = {g: sum(w for _, w in GROUPS[g]) for g in ORDER}
START = {g: sum(WIDTH[x] for x in ORDER[:n]) for n, g in enumerate(ORDER)}
WIN = sum(WIDTH.values())
KIV = WIDTH["kiv"]
TRW = 10 * P


def log_gamma():
    return np.log1p(-np.exp2(-5.0 - np.arange(RH, dtype=np.float64)))


def rope_table():
    pos = np.concatenate([np.arange(SEQ), np.tile(PAST + np.arange(TS), NB), np.zeros(ROWS - SEQ - NS, int)])
    cols = []
    for half in (32, 64):
        inv = 10000.0 ** (-np.arange(half, dtype=np.float64) / half)
        ang = pos.astype(np.float32)[:, None] * inv[None, :].astype(np.float32)
        cols += [np.cos(ang), np.sin(ang)]
    return np.concatenate(cols, 1).astype(np.float32)


C_ID, C_DEC, C_DECS, C_QD, C_KD, C_QDS, C_KDS, C_BLK = 0, 128, 640, 768, 772, 776, 780, 784
C_BLKR = C_BLK + NB * NS
C_W = C_BLKR + NB


def constant_table():
    c = np.zeros((P, C_W), np.float64)
    c[:, C_ID:C_ID + P] = np.eye(P)
    i = np.arange(P)
    s = RD ** -0.5
    for h, lg in enumerate(log_gamma()):
        c[:, C_DEC + h * P:C_DEC + (h + 1) * P] = np.where(i[None, :] >= i[:, None], s * np.exp(-lg * (i[:, None] + 1.0)), 0)
        r = np.arange(NS)
        same = (r[:, None] // TS == r[None, :] // TS) & (r[None, :] >= r[:, None])
        c[:NS, C_DECS + h * NS:C_DECS + (h + 1) * NS] = np.where(same, s * np.exp(-lg * (r[:, None] % TS + 1.0)), 0)
        c[:, C_QD + h] = np.exp(lg * (i + 1.0))
        c[:, C_KD + h] = s * np.exp(lg * (P - 1.0 - i))
        c[:NS, C_QDS + h] = np.exp(lg * (r % TS + 1.0))
        c[:NS, C_KDS + h] = s * np.exp(lg * (TS - 1.0 - r % TS))
    for b in range(NB):
        c[:, C_BLK + b * NS + b * TS:C_BLK + b * NS + (b + 1) * TS] = 1
        c[b * TS:(b + 1) * TS, C_BLKR + b] = 1
    return c.astype(np.float32)


class Signal:

    def __init__(self, sem, per, tiles=2):
        self.sem, self.per, self.tiles = sem, per, tiles

    def seed(self, eng):
        eng.sem_inc(self.sem, 2 * self.per)

    def at(self, n, k=None):
        i, u = n
        return i * (self.tiles * self.per) + (u + 2) * self.per + (self.per if k is None else k)


def bc(ap, axis, n):
    v = ap.unsqueeze(axis)
    shape = list(v.shape)
    shape[axis] = n
    return v.broadcast_to(shape)


def project_phase(nc, t):
    with ExitStack() as ctx:
        sb = lambda name, shape, dt=F32: ctx.enter_context(nc.sbuf_tensor("a_" + name, shape, dt))
        sem = lambda name: ctx.enter_context(nc.semaphore("a_" + name))
        signal = lambda name, per: Signal(sem(name), per)

        w = sb("w", [P, KD, WIN])
        c = sb("c", [P, C_W])
        ident = c[:, C_ID:C_ID + P]
        gmix = sb("gmix", [P, D])
        gretn = sb("gretn", [P, RH * RD])
        x = sb("x", [P, 2, D])
        rope = sb("rope", [P, 2, 192])
        ssq = sb("ssq", [P, 2])
        rstd = sb("rstd", [P, 2])
        mhalf = sb("mhalf", [P, RH])
        xn = sb("xn", [P, D])
        xT = sb("xT", [P, 2, KD, P])
        ta = sb("ta", [P, 512])
        tb = sb("tb", [P, 512])
        rq = sb("rq", [P, 512])
        rk = sb("rk", [P, 512])
        rkd = sb("rkd", [P, 512])
        rv = sb("rv", [P, 512])
        rg = sb("rg", [P, 512])
        erg = sb("erg", [P, 512])
        gate = sb("gate", [P, 512])
        q = sb("q", [P, 4, KVH, HD])
        qi = sb("qi", [P, 4, KVH, HD])
        kiv = sb("kiv", [P, 2, KIV])
        kid = sb("kid", [P, 2, HD])
        rqT = sb("rqT", [P, 512])
        rkT = sb("rkT", [P, 512])
        innT = sb("innT", [P, 512])
        o = sb("o", [P, 512])
        stats = sb("stats", [P, RH, 6])
        mv = sb("mv", [P, RH, 2])
        orstd = sb("orstd", [P, RH])
        ret = sb("ret", [P, 2, 512])
        state = sb("state", [P, RH * RD])
        trs = sb("trs", [P, 2, TRW])

        pxT = ctx.enter_context(nc.psum_tensor("a_pxT", [P, 2, 512], F32))
        pproj = ctx.enter_context(nc.psum_tensor("a_pproj", [P, 4, 512], F32))
        pr = ctx.enter_context(nc.psum_tensor("a_pr", [P, 2, 512], F32))

        consts = sem("consts")
        w_landed = [sem(f"w_{g}") for g in ORDER]
        x_landed = [sem(f"x_landed{u}") for u in range(2)]
        stored = [sem(f"stored{u}") for u in range(2)]
        state_out = sem("state_out")
        sstate_in = sem("sstate_in")
        ssq_done = signal("ssq_done", 1)
        xn_done = signal("xn_done", 1)
        xT_done = signal("xT_done", 2)
        xT_copied = signal("xT_copied", 2)
        proj = signal("proj", 7)
        roped = signal("roped", 5)
        taken = signal("taken", 2)
        mixed = signal("mixed", 8)
        moved = signal("moved", 5)
        folded = signal("folded", 3)
        rkd_done = signal("rkd_done", 1)
        gate_done = signal("gate_done", 1)
        var_done = signal("var_done", 1)
        orstd_done = signal("orstd_done", 1)
        ret_done = signal("ret_done", 1)
        blk_done = sem("blk_done")
        snew_done = sem("snew_done")
        snew_taken = sem("snew_taken")

        zeroed = sem("zeroed")

        wflat = w[:].rearrange("p k n -> p (k n)")
        sst = wflat[:, 0:4096].rearrange("p (h b e) -> p h b e", h=RH, b=NB)
        rqb = wflat[:, 4096:5120].rearrange("p (h b r) -> p h b r", h=RH, b=NB)
        rvb = wflat[0:NS, 5120:9216].rearrange("p (h b e) -> p h b e", h=RH, b=NB)

        block = ctx.enter_context(nc.Block())
        last = (NT // 2, 0)
        PAIRS = NT // 2

        def heads(ap, n=RH):
            return ap.rearrange("p (h e) -> p h e", h=n)

        @block.sync
        def _(sp):
            sp.sem_inc(stored[0], 48)
            sp.sem_inc(stored[1], 48)

            def load(row, i, u):
                sp.dma_start(x[:, u, :], t.x[bass.ds(row, P), :]).then_inc(x_landed[u], 16)
                sp.dma_start(rope[:, u, :], t.rope[bass.ds(row, P), :]).then_inc(x_landed[u], 16)

            def store(row, n):
                i, u = n
                sp.wait_ge(moved.sem, moved.at(n))
                sp.dma_start(t.tr[bass.ds(row, P), :], trs[:, u, :]).then_inc(stored[u], 16)
                sp.dma_start(t.kiv[bass.ds(row, P), :], kiv[:, u, :]).then_inc(stored[u], 16)
                sp.wait_ge(ret_done.sem, ret_done.at(n))
                sp.dma_start(t.cat[bass.ds(row, P), 512:D], ret[:, u, :]).then_inc(stored[u], 16)

            load(0, 0, 0)
            sp.dma_start(c[:], t.c).then_inc(consts, 16)
            sp.dma_start(gmix[:], t.g_mix.partition_broadcast(P)).then_inc(consts, 16)
            sp.dma_start(gretn[:], t.g_retn.partition_broadcast(P)).then_inc(consts, 16)
            for g, landed in zip(ORDER, w_landed):
                at = START[g]
                for src, width in GROUPS[g]:
                    sp.dma_start(w[:, :, at:at + width],
                                 t.w_in[:, src:src + width].rearrange("(k p) n -> p k n", p=P)).then_inc(landed, 16)
                    at += width
            with sp.Fori(0, PAIRS) as i:
                rows = [sp.snap((i * 2 + v) * P) for v in range(3)]
                for u in range(2):
                    sp.wait_ge(xn_done.sem, xn_done.at((i, u - 1)))
                    sp.wait_ge(roped.sem, roped.at((i, u - 1)))
                    load(rows[u + 1], i, (u + 1) % 2)
                    store(rows[u], (i, u))
            for h in range(RH):
                if h == 0:
                    sp.wait_ge(proj.sem, proj.at(last))
                sp.dma_start(sst[:, h], t.state_retn[:, h].rearrange("b d e -> d b e")).then_inc(sstate_in, 16)
            store(NT * P, last)
            sp.wait_ge(folded.sem, folded.at((PAIRS - 1, 1)))
            sp.dma_start(t.retn_prompt.rearrange("h d e -> d h e"), heads(state[:])).then_inc(state_out, 16)
            for h in range(RH):
                sp.wait_ge(snew_taken, 2 * h + 2)
                sp.dma_start(t.retn_sample[:, h].rearrange("b d e -> d b e"), sst[:, h]).then_inc(state_out, 16)
            sp.wait_ge(state_out, 16 * (1 + RH))
            for u, tiles in ((0, PAIRS + 1), (1, PAIRS)):
                sp.wait_ge(stored[u], 48 * (tiles + 1))

        @block.tensor
        def _(pe):
            for s in (xT_done, proj, mixed):
                s.seed(pe)
            pe.wait_ge(consts, 48)

            def transpose_x(n):
                i, u = n
                pe.wait_ge(xn_done.sem, xn_done.at(n))
                pe.wait_ge(xT_copied.sem, xT_copied.at((i, u - 1)))
                for half in range(2):
                    for k in range(4):
                        at = (half * 4 + k) * P
                        m = pe.transpose(pxT[:, half, k * P:(k + 1) * P], xn[:, at:at + P], ident)
                    m.then_inc(xT_done.sem, 1)

            def project(n, g):
                i, u = n
                s = ORDER.index(g)
                pe.wait_ge(w_landed[s], 16 * len(GROUPS[g]))
                if g == "rq":
                    pe.wait_ge(xT_copied.sem, xT_copied.at(n))
                before = {"rq": (roped, (i, u - 1), 3), "rk": (roped, (i, u - 1), 4), "rv": (roped, (i, u - 1), 5),
                          "rg": (taken, (i, u - 1), 2), "q": (roped, n, 1), "qi": (roped, n, 2), "kiv": (taken, n, 1)}[g]
                pe.wait_ge(before[0].sem, before[0].at(before[1], before[2]))
                for k in range(KD):
                    m = pe.matmul(pproj[:, s % 4, 0:WIDTH[g]], xT[:, u % 2, k, :], w[:, k, START[g]:START[g] + WIDTH[g]],
                                  start=(k == 0), stop=(k == KD - 1))
                m.then_inc(proj.sem, 1)

            def body(n, m_rows, sample=False):
                i, u = n
                R = m_rows
                for g in ("rq", "rk", "rv", "rg", "q"):
                    project(n, g)
                for j, (src, before) in enumerate(((rq, 4), (rk, 5))):
                    pe.wait_ge(roped.sem, roped.at(n, j + 1))
                    pe.wait_ge(moved.sem, moved.at((i, u - 1), before))
                    for h in range(RH):
                        m = pe.transpose(pr[:, j, h * P:h * P + R], src[0:R, h * P:(h + 1) * P], ident[0:R, 0:R])
                    m.then_inc(mixed.sem, 1)
                project(n, "qi")
                pe.wait_ge(moved.sem, moved.at(n, 2))
                for h in range(RH):
                    m = pe.matmul(pr[0:R, 0, h * R:(h + 1) * R], rkT[:, h * P:h * P + R], rqT[:, h * P:h * P + R],
                                  start=True, stop=True)
                m.then_inc(mixed.sem, 1)
                project(n, "kiv")
                if not sample:
                    transpose_x((i, u + 1))
                pe.wait_ge(folded.sem, folded.at(n, 1))
                pe.wait_ge(taken.sem, taken.at(n, 1))
                pe.wait_ge(folded.sem, folded.at((i, u - 1), 3))
                if sample:
                    pe.wait_ge(blk_done, 2)
                    pe.wait_ge(sstate_in, 16 * RH)
                for h in range(RH):
                    out = pr[0:R, 1, h * P:(h + 1) * P]
                    pe.matmul(out, innT[0:R, h * R:(h + 1) * R], rv[0:R, h * P:(h + 1) * P], start=True, stop=False)
                    if sample:
                        for b in range(NB):
                            m = pe.matmul(out, rqb[:, h, b, :], sst[:, h, b, :], start=False, stop=(b == NB - 1))
                    else:
                        m = pe.matmul(out, rqT[:, h * P:(h + 1) * P], state[:, h * P:(h + 1) * P], start=False, stop=True)
                m.then_inc(mixed.sem, 1)
                pe.wait_ge(rkd_done.sem, rkd_done.at(n))
                if sample:
                    m = None
                    for h in range(RH):
                        for half in range(2):
                            pos = h * 2 + half
                            pe.wait_ge(snew_taken, pos - 1) if pos > 1 else None
                            m = pe.matmul(pxT[:, half, :], rkd[0:NS, h * P:(h + 1) * P],
                                          rvb[:, h, half * 4:half * 4 + 4, :].rearrange("p b e -> p (b e)"),
                                          start=True, stop=True)
                            if pos < 2 * RH - 1:
                                m.then_inc(snew_done, 1)
                    m.then_inc(snew_done, 1)
                    pe.transpose(pr[0:1, 0, 0:1], ident[0:1, 0:1], ident[0:1, 0:1]).then_inc(mixed.sem, 1)
                else:
                    for h in range(RH):
                        m = pe.matmul(pr[:, 0, h * P:(h + 1) * P], rkd[:, h * P:(h + 1) * P], rv[:, h * P:(h + 1) * P],
                                      start=True, stop=True)
                    m.then_inc(mixed.sem, 1)
                pe.wait_ge(roped.sem, roped.at(n, 3))
                pe.wait_ge(folded.sem, folded.at(n, 2))
                for j in range(4):
                    m = pe.transpose(pr[:, 1, j * P:j * P + R], q[0:R, j].rearrange("p a d -> p (a d)"), ident[0:R, 0:R])
                m.then_inc(mixed.sem, 1)
                pe.wait_ge(roped.sem, roped.at(n, 4))
                pe.wait_ge(folded.sem, folded.at(n, 3))
                for j in range(4):
                    m = pe.transpose(pr[:, 0, j * P:j * P + R], qi[0:R, j].rearrange("p a d -> p (a d)"), ident[0:R, 0:R])
                m.then_inc(mixed.sem, 1)
                pe.wait_ge(roped.sem, roped.at(n, 5))
                pe.wait_ge(moved.sem, moved.at(n, 3))
                pe.transpose(pr[:, 1, 0:R], kiv[0:R, u % 2, 0:P], ident[0:R, 0:R])
                pe.transpose(pr[:, 1, P:P + R], kid[0:R].rearrange("p a d -> p (a d)"), ident[0:R, 0:R]).then_inc(mixed.sem, 1)

            transpose_x((0, 0))
            with pe.Fori(0, PAIRS) as i:
                body((i, 0), P)
                body((i, 1), P)
            body(last, NS, sample=True)

        @block.scalar
        def _(act):
            for s in (ssq_done, xT_copied, taken, moved):
                s.seed(act)

            def square(n):
                i, u = n
                act.wait_ge(x_landed[u % 2], i * 32 + 32 * (u // 2 + 1))
                act.wait_ge(xn_done.sem, xn_done.at((i, u - 1)))
                act.activation(xn[:], x[:, u % 2, :], ACT.Square, accum_out=ssq[:, u % 2:u % 2 + 1])
                act.drain()
                act.activation(ssq[:, u % 2:u % 2 + 1], ssq[:, u % 2:u % 2 + 1], ACT.Copy, scale=1.0 / D, bias=EPS).then_inc(ssq_done.sem, 1)

            def copy_xT(n):
                i, u = n
                act.wait_ge(proj.sem, proj.at((i, u - 2)))
                for half in range(2):
                    act.wait_ge(xT_done.sem, xT_done.at(n, half + 1))
                    act.activation(xT[:, u % 2, half * 4:half * 4 + 4, :].rearrange("p k c -> p (k c)"), pxT[:, half, :],
                                   ACT.Copy).then_inc(xT_copied.sem, 1)

            def body(n, R, sample=False):
                i, u = n
                s = u % 2
                act.wait_ge(proj.sem, proj.at(n, 3))
                act.wait_ge(mixed.sem, mixed.at((i, u - 1), 5))
                act.activation(rv[:], pproj[:, 2, :], ACT.Copy).then_inc(taken.sem, 1)
                act.wait_ge(proj.sem, proj.at(n, 4))
                act.wait_ge(gate_done.sem, gate_done.at((i, u - 1)))
                act.activation(erg[:], pproj[:, 3, :], ACT.Sigmoid)
                act.activation(rg[:], pproj[:, 3, :], ACT.Copy)
                act.drain().then_inc(taken.sem, 1)
                for j, dst in enumerate((rqT, rkT)):
                    act.wait_ge(mixed.sem, mixed.at(n, j + 1))
                    act.activation(heads(dst[:])[:, :, 0:R], heads(pr[:, j, :])[:, :, 0:R], ACT.Copy).then_inc(moved.sem, 1)
                if not sample:
                    act.wait_ge(xT_done.sem, xT_done.at(n))
                    square((i, u + 1))
                    copy_xT((i, u + 1))
                act.wait_ge(stored[s], (u // 2 + 1) * 48 + i * 48)
                for j, (bank, width, at) in enumerate(((1, 4, 0), (0, 4, 4), (1, 2, 8))):
                    act.wait_ge(mixed.sem, mixed.at(n, 6 + j))
                    act.activation(heads(trs[:, s, at * P:(at + width) * P], width)[:, :, 0:R],
                                   heads(pr[:, bank, 0:width * P], width)[:, :, 0:R], ACT.Copy).then_inc(moved.sem, 1)

            act.wait_ge(zeroed, 2)
            square((0, 0))
            copy_xT((0, 0))
            with act.Fori(0, PAIRS) as i:
                body((i, 0), P)
                body((i, 1), P)
            body(last, NS, sample=True)

        @block.vector
        def _(dve):
            for s in (roped, folded, var_done, ret_done):
                s.seed(dve)
            dve.memset(state[:], 0.0).then_inc(zeroed, 1)
            dve.memset(trs[:].rearrange("p s n -> p (s n)"), 0.0).then_inc(zeroed, 1)
            dve.wait_ge(zeroed, 2)
            dve.wait_ge(consts, 48)

            def rotate(src, s, half, n, outs):
                base = 0 if half == 32 else 64
                width = 2 * n * half
                view = lambda a: a.rearrange("p (m d) -> p m d", d=half)
                cos = bc(rope[:, s, base:base + half], 1, 2 * n)
                sin = bc(rope[:, s, base + half:base + 2 * half], 1, 2 * n)
                dve.tensor_tensor(view(ta[:, 0:width]), view(src), cos, ALU.mult)
                m = dve.tensor_tensor(view(tb[:, 0:width]), view(src), sin, ALU.mult)
                dve.drain()
                a = ta[:, 0:width].rearrange("p (n s d) -> p n s d", s=2, d=half)
                b = tb[:, 0:width].rearrange("p (n s d) -> p n s d", s=2, d=half)
                return a, b

            def rotate_heads(src, s, dst, order):
                a, b = rotate(src, s, 32, 8, None)
                re = lambda v, s_: v[:, :, s_, :].rearrange("p (v j) d -> p v j d", v=KVH)
                out = lambda s_: dst[:, :, :, s_ * 32:s_ * 32 + 32].rearrange("p j v d -> p v j d")
                dve.tensor_tensor(out(0), re(a, 0), re(b, 1), ALU.subtract)
                return dve.tensor_tensor(out(1), re(a, 1), re(b, 0), ALU.add)

            def rotate_plain(src, s, half, n, dst):
                a, b = rotate(src, s, half, n, None)
                o_ = dst.rearrange("p (n s d) -> p n s d", s=2, d=half)
                dve.tensor_tensor(o_[:, :, 0, :], a[:, :, 0, :], b[:, :, 1, :], ALU.subtract)
                return dve.tensor_tensor(o_[:, :, 1, :], a[:, :, 1, :], b[:, :, 0, :], ALU.add)

            def body(n, R, sample=False):
                i, u = n
                s = u % 2
                before = (i, u - 1)
                decay = c[0:R, C_DECS:C_DECS + RH * NS] if sample else c[:, C_DEC:C_DEC + RH * P]
                qdec = c[:, C_QDS:C_QDS + RH] if sample else c[:, C_QD:C_QD + RH]
                for j, (g, dst) in enumerate((("rq", rq), ("rk", rk))):
                    dve.wait_ge(proj.sem, proj.at(n, ORDER.index(g) + 1))
                    dve.wait_ge(mixed.sem, mixed.at(before, j + 1))
                    if g == "rk":
                        dve.wait_ge(rkd_done.sem, rkd_done.at(before))
                    if g == "rq":
                        dve.wait_ge(x_landed[s], i * 32 + 32 * (u // 2 + 1))
                    rotate_plain(pproj[:, j, :], s, 64, RH, dst[:]).then_inc(roped.sem, 1)
                    dve.drain()
                for j, (g, dst) in enumerate((("q", q), ("qi", qi))):
                    dve.wait_ge(proj.sem, proj.at(n, ORDER.index(g) + 1))
                    dve.wait_ge(mixed.sem, mixed.at(before, 6 + j))
                    rotate_heads(pproj[:, j, :], s, dst[:], None).then_inc(roped.sem, 1)
                    dve.drain()
                dve.wait_ge(mixed.sem, mixed.at(n, 3))
                dve.tensor_tensor(innT[0:R, 0:RH * R], pr[0:R, 0, 0:RH * R], decay, ALU.mult).then_inc(folded.sem, 1)
                dve.wait_ge(proj.sem, proj.at(n, 7))
                dve.wait_ge(stored[s], (u // 2 + 1) * 48 + i * 48)
                dve.wait_ge(mixed.sem, mixed.at(before, 8))
                kv = kiv[:, s, :]
                rotate_plain(pproj[:, 2, 0:192], s, 32, 3, kv[:, 0:192])
                dve.tensor_copy(kv[:, 192:KIV], pproj[:, 2, 192:KIV])
                dve.drain()
                dve.tensor_copy(kid[:], bc(kv[:, P:P + HD], 1, 2)).then_inc(roped.sem, 1)
                if sample:
                    r4 = heads(rqT[:])[:, :, 0:NS].unsqueeze(2).broadcast_to([P, RH, NB, NS])
                    blk = c[:, C_BLK:C_BLK + NB * NS].rearrange("p (b r) -> p b r", b=NB)
                    dve.wait_ge(moved.sem, moved.at(n, 2))
                    dve.wait_ge(proj.sem, proj.at(n))
                    dve.tensor_tensor(rqb, r4, blk.unsqueeze(1).broadcast_to([P, RH, NB, NS]), ALU.mult).then_inc(blk_done, 1)
                    dve.wait_ge(taken.sem, taken.at(n, 1))
                    for b in range(NB):
                        m = dve.tensor_scalar(rvb[:, :, b, :], heads(rv[0:NS, :]), c[0:NS, C_BLKR + b:C_BLKR + b + 1], None, ALU.mult)
                    m.then_inc(blk_done, 1)
                dve.wait_ge(mixed.sem, mixed.at(n, 4))
                dve.tensor_tensor(heads(o[0:R, :]), heads(pr[0:R, 1, :]), bc(qdec[0:R], 2, RD), ALU.mult).then_inc(folded.sem, 1)
                if sample:
                    for h in range(RH):
                        for half in range(2):
                            dve.wait_ge(snew_done, 2 * h + half + 1)
                            st = sst[:, h, half * 4:half * 4 + 4, :].rearrange("p b e -> p (b e)")
                            dve.scalar_tensor_tensor(st, st, float(np.exp(log_gamma()[h] * TS)), pxT[:, half, :],
                                                     ALU.mult, ALU.add).then_inc(snew_taken, 1)
                    dve.wait_ge(mixed.sem, mixed.at(n, 5))
                    dve.memset(stats[0:1, 0, 0:1], 0.0).then_inc(folded.sem, 1)
                    dve.drain()
                else:
                    dve.wait_ge(mixed.sem, mixed.at(n, 5))
                    for h in range(RH):
                        st = state[:, h * P:(h + 1) * P]
                        m = dve.scalar_tensor_tensor(st, st, float(np.exp(log_gamma()[h] * P)), pr[:, 0, h * P:(h + 1) * P],
                                                     ALU.mult, ALU.add)
                    m.then_inc(folded.sem, 1)
                    dve.drain()
                for h in range(RH):
                    dve.bn_stats(stats[0:R, h, :], o[0:R, h * P:(h + 1) * P])
                dve.drain()
                for h in range(RH):
                    dve.bn_aggr(mv[0:R, h, :], stats[0:R, h, :])
                dve.drain()
                dve.tensor_scalar(mv[0:R, :, 1], mv[0:R, :, 1], GN_EPS, None, ALU.add).then_inc(var_done.sem, 1)
                dve.wait_ge(orstd_done.sem, orstd_done.at(n))
                dve.wait_ge(var_done.sem, var_done.at(n))
                dve.wait_ge(gate_done.sem, gate_done.at(n))
                for h in range(RH):
                    oh = o[0:R, h * P:(h + 1) * P]
                    dve.tensor_scalar(oh, oh, mv[0:R, h, 0:1], orstd[0:R, h:h + 1], ALU.subtract, ALU.mult)
                dve.drain()
                dve.tensor_tensor(ret[0:R, s, :], o[0:R, :], gate[0:R, :], ALU.mult).then_inc(ret_done.sem, 1)

            dve.memset(ret[:].rearrange("p s n -> p (s n)"), 0.0)
            dve.drain()
            with dve.Fori(0, PAIRS) as i:
                body((i, 0), P)
                body((i, 1), P)
            body(last, NS, sample=True)

        @block.gpsimd
        def _(pool):
            for s in (xn_done, rkd_done, gate_done, orstd_done):
                s.seed(pool)
            pool.memset(mhalf[:], -0.5)
            pool.wait_ge(consts, 48)
            pool.drain()

            def normalise(n):
                i, u = n
                s = u % 2
                pool.wait_ge(ssq_done.sem, ssq_done.at(n))
                pool.tensor_tensor(rstd[:, s:s + 1], ssq[:, s:s + 1], mhalf[:, 0:1], ALU.pow)
                pool.drain()
                pool.tensor_scalar(xn[:], x[:, s, :], rstd[:, s:s + 1], None, ALU.mult)
                pool.drain()
                pool.tensor_tensor(xn[:], xn[:], gmix[:], ALU.mult).then_inc(xn_done.sem, 1)

            def body(n, R, sample=False):
                i, u = n
                before = (i, u - 1)
                kdec = c[:, C_KDS:C_KDS + RH] if sample else c[:, C_KD:C_KD + RH]
                pool.wait_ge(roped.sem, roped.at(n, 2))
                pool.wait_ge(mixed.sem, mixed.at(before, 5))
                pool.tensor_tensor(heads(rkd[0:R, :]), heads(rk[0:R, :]), bc(kdec[0:R], 2, RD), ALU.mult).then_inc(rkd_done.sem, 1)
                if not sample:
                    normalise((i, u + 1))
                pool.wait_ge(taken.sem, taken.at(n, 2))
                pool.wait_ge(ret_done.sem, ret_done.at(before))
                pool.tensor_tensor(gate[:], rg[:], erg[:], ALU.mult)
                pool.drain()
                pool.tensor_tensor(gate[:], gate[:], gretn[:], ALU.mult).then_inc(gate_done.sem, 1)
                pool.wait_ge(var_done.sem, var_done.at(n))
                pool.wait_ge(ret_done.sem, ret_done.at(before))
                pool.tensor_tensor(orstd[0:R], mv[0:R, :, 1], mhalf[0:R], ALU.pow).then_inc(orstd_done.sem, 1)

            normalise((0, 0))
            with pool.Fori(0, PAIRS) as i:
                body((i, 0), P)
                body((i, 1), P)
            body(last, NS, sample=True)


NSTEP = 24
B_ID, B_CAUSAL, B_HALF, B_W = 0, 128, 256, 256 + NSTEP


def attention_table():
    c = np.zeros((P, B_W), np.float32)
    i = np.arange(P)
    c[:, B_ID:B_ID + P] = np.eye(P)
    c[:, B_CAUSAL:B_CAUSAL + P] = np.where(i[None, :] > i[:, None], -BIG, 0)
    c[:, B_HALF:B_HALF + NSTEP] = 2.0 ** -(np.arange(NSTEP) + 1.0)
    return c


def prompt_phase(nc, t):
    with ExitStack() as ctx:
        sb = lambda name, shape, dt=F32: ctx.enter_context(nc.sbuf_tensor("b_" + name, shape, dt))
        sem = lambda name: ctx.enter_context(nc.semaphore("b_" + name))

        c = sb("consts", [P, B_W])
        ident = c[:, B_ID:B_ID + P]
        kT = sb("kT", [P, NT * P])
        kiT = sb("kiT", [P, NT * P])
        v = sb("v", [P, NT, P])
        wi = sb("wi", [P, NT, IH])
        qT = sb("qT", [P, 2, AH, P])
        qiT = sb("qiT", [P, 2, IH, P])
        relu = sb("relu", [P, 4, 512])
        score = sb("score", [P, 3, SEQ])
        mask = sb("mask", [P, 2, SEQ])
        above = sb("above", [P, SEQ])
        band = sb("band", [P, SEQ])
        rank = sb("rank", [P, SEQ])
        lim = sb("lim", [P, 8])
        step = sb("step", [P, NSTEP])
        mid = sb("mid", [P, NSTEP])
        cnt = sb("cnt", [P, NSTEP])
        logit = sb("logit", [P, 2, SEQ])
        mx = sb("mx", [P, 2, 4])
        nb = sb("nb", [P, 4])
        rs = sb("rs", [P, 2, AH])
        rrs = sb("rrs", [P, AH])
        pT = sb("pT", [P, 2, SEQ])
        att = sb("att", [P, 2, AH, HD])
        pi = ctx.enter_context(nc.psum_tensor("b_pi", [P, 2, 512], F32))
        pl = ctx.enter_context(nc.psum_tensor("b_pl", [P, 3, 512], F32))
        pt = ctx.enter_context(nc.psum_tensor("b_pt", [P, 2, 512], F32))
        po = ctx.enter_context(nc.psum_tensor("b_po", [P, 512], F32))

        loaded = sem("loaded")
        q_in = [sem(f"q_in{s}") for s in range(2)]
        qi_in = [sem(f"qi_in{s}") for s in range(2)]
        att_out = [sem(f"att_out{s}") for s in range(2)]
        scored = sem("scored")
        relued = sem("relued")
        weighed = sem("weighed")
        logits = sem("logits")
        masked = sem("masked")
        max_done = sem("max_done")
        exp_done = sem("exp_done")
        turned = sem("turned")
        pT_done = sem("pT_done")
        pv = sem("pv")
        att_done = sem("att_done")
        zeroed = sem("zeroed")
        ranked = sem("ranked")

        def chunks(T):
            return [(a, min(512, (T + 1) * P - a)) for a in range(0, (T + 1) * P, 512)]

        FIRST = TOPK // P
        ibase = {T: IH * sum(len(chunks(x)) for x in range(FIRST, T)) for T in range(FIRST, NT + 1)}
        lbase = {T: AH * sum(len(chunks(x)) for x in range(T)) for T in range(NT + 1)}

        def icount(T, hh, k):
            return ibase[T] + hh * len(chunks(T)) + k + 1

        def lcount(T, hh, k):
            return lbase[T] + hh * len(chunks(T)) + k + 1

        def head(hh):
            return hh // 2, hh % 2, hh // 2 + 4 * (hh % 2)

        steps = [(T, hh) for T in range(FIRST - 2, NT) for hh in range(AH)]
        block = ctx.enter_context(nc.Block())

        @block.sync
        def _(sp):
            tr = t.tr[0:SEQ, :].rearrange("(n p) c -> p n c", p=P)
            kv = t.kiv[0:SEQ, :].rearrange("(n p) c -> p n c", p=P)

            def load_q(T):
                if T >= 2:
                    sp.wait_ge(logits, lcount(T - 2, AH - 1, len(chunks(T - 2)) - 1))
                for half in range(2):
                    rows = slice(half * HD, half * HD + HD)
                    sp.dma_start(qT[rows, T % 2, half::2, :], tr[rows, T, 0:4 * P].rearrange("p (j c) -> p j c", j=4)).then_inc(q_in[T % 2], 16)

            def load_qi(T):
                if T >= FIRST + 2:
                    sp.wait_ge(scored, icount(T - 2, IH - 1, len(chunks(T - 2)) - 1))
                for half in range(2):
                    rows = slice(half * HD, half * HD + HD)
                    sp.dma_start(qiT[rows, T % 2, half::2, :], tr[rows, T, 4 * P:8 * P].rearrange("p (j c) -> p j c", j=4)).then_inc(qi_in[T % 2], 16)

            load_qi(FIRST)
            sp.dma_start(kiT[:].rearrange("p (n c) -> p n c", n=NT), tr[:, :, 9 * P:10 * P]).then_inc(loaded, 16)
            sp.dma_start(wi[:], kv[:, :, 320:328]).then_inc(loaded, 16)
            load_q(0)
            sp.dma_start(kT[:].rearrange("p (n c) -> p n c", n=NT), tr[:, :, 8 * P:9 * P]).then_inc(loaded, 16)
            sp.dma_start(c[:], t.b_c).then_inc(loaded, 16)
            sp.dma_start(v[:], kv[:, :, 192:320]).then_inc(loaded, 16)
            load_q(1)
            load_qi(FIRST + 1)
            for T in range(NT):
                if T + 4 < NT:
                    load_qi(T + 4)
                if T + 2 < NT:
                    load_q(T + 2)
                sp.wait_ge(att_done, T + 1)
                sp.dma_start(t.cat[T * P:(T + 1) * P, 0:512], att[:, T % 2].rearrange("p h d -> p (h d)")).then_inc(att_out[T % 2], 16)
            for s in range(2):
                sp.wait_ge(att_out[s], 16 * (NT // 2))

        @block.tensor
        def _(pe):
            pe.wait_ge(loaded, 80)
            pe.wait_ge(zeroed, 1)

            def index(T, hh, k):
                a, w_ = chunks(T)[k]
                n = icount(T, hh, k)
                if k == 0:
                    pe.wait_ge(qi_in[T % 2], 32 * ((T - FIRST) // 2 + 1))
                if n > 2:
                    pe.wait_ge(relued, n - 2)
                pe.matmul(pi[:, n % 2, 0:w_], qiT[:, T % 2, hh, :], kiT[:, a:a + w_],
                          start=True, stop=True).then_inc(scored, 1)

            def logit_products(T, hh, k):
                a, w_ = chunks(T)[k]
                n = lcount(T, hh, k)
                if k == 0:
                    pe.wait_ge(q_in[T % 2], 32 * (T // 2 + 1))
                if n > 3:
                    pe.wait_ge(masked, n - 3)
                pe.matmul(pl[:, n % 3, 0:w_], qT[:, T % 2, hh, :], kT[:, a:a + w_],
                          start=True, stop=True).then_inc(logits, 1)

            def values(T, hh):
                _, half, hd = head(hh)
                g = T * AH + hh
                pe.wait_ge(exp_done, g + 1)
                for k, (a, w_) in enumerate(chunks(T)):
                    n = lcount(T, hh, k)
                    if n > 2:
                        pe.wait_ge(pT_done, n - 2)
                    for b in range(0, w_, P):
                        m = pe.transpose(pt[:, n % 2, b:b + P], logit[:, g % 2, a + b:a + b + P], ident)
                    m.then_inc(turned, 1)
                if hh == 0 and T >= 1:
                    pe.wait_ge(att_done, T)
                pe.wait_ge(pT_done, lcount(T, hh, len(chunks(T)) - 1))
                for b in range(T + 1):
                    m = pe.matmul(po[:, hd * HD:(hd + 1) * HD], pT[:, g % 2, b * P:(b + 1) * P],
                                  v[:, b, half * HD:half * HD + HD], start=(b == 0), stop=(b == T))
                m.then_inc(pv, 1)

            for T, hh in steps:
                for k in range(4):
                    if T >= 0 and k < len(chunks(T)):
                        logit_products(T, hh, k)
                    if T + 2 < NT and k < len(chunks(T + 2)):
                        index(T + 2, hh, k)
                if T * AH + hh >= 1:
                    values((T * AH + hh - 1) // AH, (hh - 1) % AH)
            values(NT - 1, AH - 1)

        @block.scalar
        def _(act):
            def relu_chunks(T, hh):
                for k, (a, w_) in enumerate(chunks(T)):
                    n = icount(T, hh, k)
                    act.wait_ge(scored, n)
                    if n > 4:
                        act.wait_ge(weighed, n - 4)
                    act.activation(relu[:, n % 4, 0:w_], pi[:, n % 2, 0:w_], ACT.Relu).then_inc(relued, 1)

            def copy_probs(T, hh):
                g = T * AH + hh
                if g >= 2:
                    act.wait_ge(pv, g - 1)
                for k, (a, w_) in enumerate(chunks(T)):
                    n = lcount(T, hh, k)
                    act.wait_ge(turned, n)
                    act.activation(pT[:, g % 2, a:a + w_], pt[:, n % 2, 0:w_], ACT.Copy).then_inc(pT_done, 1)

            def exponential(T, hh):
                g = T * AH + hh
                hd = head(hh)[2]
                act.wait_ge(max_done, g + 1)
                lg = logit[:, g % 2, 0:(T + 1) * P]
                act.activation(lg, lg, ACT.Exp, bias=nb[:, g % 4:g % 4 + 1], scale=HD ** -0.5,
                               accum_out=rs[:, T % 2, hd:hd + 1]).then_inc(exp_done, 1)

            for T, hh in steps:
                if T + 2 < NT:
                    relu_chunks(T + 2, hh)
                if T * AH + hh >= 1:
                    copy_probs((T * AH + hh - 1) // AH, (hh - 1) % AH)
                if T >= 0:
                    exponential(T, hh)
            copy_probs(NT - 1, AH - 1)

        @block.vector
        def _(dve):
            for half in range(2):
                rows = slice((1 - half) * HD, (1 - half) * HD + HD)
                dve.memset(qT[rows, :, half::2, :], 0.0)
                dve.memset(qiT[rows, :, half::2, :], 0.0)
            dve.memset(mask[:].rearrange("p s n -> p (s n)"), 0.0)
            dve.drain().then_inc(zeroed, 1)
            dve.wait_ge(loaded, 80)

            lo, hi, need, took = (lim[:, j:j + 1] for j in range(4))

            def open_range(T):
                dve.wait_ge(weighed, icount(T, IH - 1, len(chunks(T)) - 1))
                s = score[:, T % 3, 0:(T + 1) * P]
                diag = score[:, T % 3, T * P:(T + 1) * P]
                dve.tensor_reduce(lo, s, AX.X, ALU.min)
                dve.drain()
                dve.tensor_tensor(diag, diag, c[:, B_CAUSAL:B_CAUSAL + P], ALU.add)
                dve.drain()
                dve.tensor_reduce(hi, s, AX.X, ALU.max)
                dve.drain()
                dve.tensor_tensor(took, hi, lo, ALU.subtract)
                dve.drain()
                dve.tensor_scalar(step[:], c[:, B_HALF:B_HALF + NSTEP], took, None, ALU.mult)
                dve.drain()
                dve.tensor_tensor(mid[:, 0:1], lo, step[:, 0:1], ALU.add)
                dve.drain()

            def halve(T, k):
                s = score[:, T % 3, 0:(T + 1) * P]
                dve.tensor_scalar(above[:, 0:(T + 1) * P], s, mid[:, k:k + 1], None, ALU.is_ge, ALU.add,
                                  accum_out=cnt[:, k:k + 1])
                dve.drain()
                if k + 1 < NSTEP:
                    dve.tensor_scalar(took, cnt[:, k:k + 1], TOPK - 0.5, step[:, k:k + 1], ALU.is_ge, ALU.mult)
                    dve.drain()
                    dve.scalar_tensor_tensor(mid[:, k + 1:k + 2], mid[:, k:k + 1], step[:, k + 1:k + 2], took, ALU.subtract, ALU.add)
                    dve.drain()

            def close_range(T, part):
                n = (T + 1) * P
                s = score[:, T % 3, 0:n]
                if part == 0:
                    dve.tensor_scalar(cnt[:], cnt[:], TOPK - 0.5, BIG, ALU.is_ge, ALU.mult)
                    dve.drain()
                    dve.tensor_tensor(step[:], mid[:], cnt[:], ALU.add)
                    dve.scalar_tensor_tensor(mid[:], cnt[:], -BIG, mid[:], ALU.add, ALU.add)
                    dve.drain()
                    dve.tensor_reduce(took, step[:], AX.X, ALU.min)
                    dve.drain()
                    dve.tensor_tensor(hi, hi, took, ALU.min)
                    dve.tensor_reduce(need, mid[:], AX.X, ALU.max)
                    dve.drain()
                    dve.tensor_tensor(lo, lo, need, ALU.max)
                    dve.drain()
                    dve.tensor_scalar(above[:, 0:n], s, hi, None, ALU.is_gt, ALU.add, accum_out=need)
                    dve.drain()
                    dve.tensor_scalar(need, need, -1.0, float(TOPK), ALU.mult, ALU.add)
                elif part == 1:
                    dve.scalar_tensor_tensor(band[:, 0:n], s, lo, above[:, 0:n], ALU.is_ge, ALU.subtract)
                elif part == 2:
                    dve.tensor_tensor_scan(rank[:, 0:n], band[:, 0:n], band[:, 0:n], 0.0, ALU.add, ALU.max)
                elif part == 3:
                    dve.scalar_tensor_tensor(band[:, 0:n], rank[:, 0:n], need, band[:, 0:n], ALU.is_le, ALU.mult)
                elif part == 4:
                    dve.tensor_tensor(band[:, 0:n], band[:, 0:n], above[:, 0:n], ALU.add)
                elif part == 5:
                    dve.tensor_scalar(mask[:, T % 2, 0:n], band[:, 0:n], -1.0, BIG, ALU.add, ALU.mult)
                dve.drain()

            def threshold(T, x):
                if x == 0:
                    open_range(T)
                elif x <= NSTEP:
                    halve(T, x - 1)
                elif x <= NSTEP + 6:
                    close_range(T, x - 1 - NSTEP)

            def mask_logits(T, hh, k):
                g = T * AH + hh
                if k == 0 and g >= 2:
                    dve.wait_ge(turned, lcount((g - 2) // AH, (g - 2) % AH, len(chunks((g - 2) // AH)) - 1))
                a, w_ = chunks(T)[k]
                n = lcount(T, hh, k)
                dve.wait_ge(logits, n)
                dve.tensor_tensor_reduce(logit[:, g % 2, a:a + w_], pl[:, n % 3, 0:w_], mask[:, T % 2, a:a + w_],
                                         1.0, -3.0e38, ALU.add, ALU.max, accum_out=mx[:, g % 2, k:k + 1]).then_inc(masked, 1)
                if k + 1 < len(chunks(T)):
                    return
                dve.drain()
                m = mx[:, g % 2, 0:1]
                if len(chunks(T)) > 1:
                    dve.tensor_reduce(m, mx[:, g % 2, 0:len(chunks(T))], AX.X, ALU.max)
                    dve.drain()
                if g >= 4:
                    dve.wait_ge(exp_done, g - 3)
                dve.tensor_scalar(nb[:, g % 4:g % 4 + 1], m, -(HD ** -0.5), None, ALU.mult).then_inc(max_done, 1)

            def normalise(T):
                dve.wait_ge(pv, AH * (T + 1))
                dve.wait_ge(exp_done, AH * (T + 1))
                if T >= 2:
                    dve.wait_ge(att_out[T % 2], 16 * (T // 2))
                dve.reciprocal(rrs[:], rs[:, T % 2, :])
                dve.drain()
                dve.tensor_tensor(att[:, T % 2], po[:].rearrange("p (h d) -> p h d", h=AH), bc(rrs[:], 2, HD), ALU.mult).then_inc(att_done, 1)

            for T in range(FIRST):
                dve.tensor_copy(mask[:, T % 2, T * P:(T + 1) * P], c[:, B_CAUSAL:B_CAUSAL + P])
            dve.drain()
            for T, hh in steps:
                ks = len(chunks(T)) if T >= 0 else 1
                for k in range(ks):
                    if T >= 0:
                        mask_logits(T, hh, k)
                    if T >= 1 and hh == 1 and k == 0:
                        normalise(T - 1)
                    if FIRST <= T + 1 < NT:
                        for x in range(4 * k // ks, 4 * (k + 1) // ks):
                            threshold(T + 1, 4 * hh + x)
                if hh == AH - 1:
                    dve.drain().then_inc(ranked, 1)
            normalise(NT - 1)

        @block.gpsimd
        def _(pool):
            pool.wait_ge(loaded, 80)

            def weigh(T, hh):
                hd = head(hh)[2]
                if hh == 0 and T >= FIRST + 3:
                    pool.wait_ge(ranked, T - FIRST - 1)
                for k, (a, w_) in enumerate(chunks(T)):
                    n = icount(T, hh, k)
                    pool.wait_ge(relued, n)
                    out, r, w1 = score[:, T % 3, a:a + w_], relu[:, n % 4, 0:w_], wi[:, T, hd:hd + 1]
                    if hh == 0:
                        pool.tensor_scalar(out, r, w1, None, ALU.mult).then_inc(weighed, 1)
                    else:
                        pool.tensor_scalar(r, r, w1, None, ALU.mult)
                        pool.drain()
                        pool.tensor_tensor(out, out, r, ALU.add).then_inc(weighed, 1)

            for T in range(FIRST, NT):
                for hh in range(IH):
                    weigh(T, hh)


S_ID, S_PAIR, S_SAME, S_LOWER, S_NEW, S_SLOT, S_ROWBASE, S_IOTA = 0, 128, 144, 272, 400, 404, 406, 470
S_HALF = S_IOTA + TOPK
S_W = S_HALF + 24
CH = 4
CKEYS = PAST // CH
CPAGES = NPAGES // CH


def sample_table():
    c = np.zeros((P, S_W), np.float32)
    p = np.arange(P)
    c[:, S_ID:S_ID + P] = np.eye(P)
    b2, par, tok = p // 64, p // 32 % 2, p % TS
    c[p, S_PAIR + b2 * 8 + par * 4 + tok] = 1
    part, row = p // NS, p % NS
    c[:, S_SAME:S_SAME + P] = row[:, None] == row[None, :]
    c[:, S_LOWER:S_LOWER + P] = (row[:, None] == row[None, :]) & (part[:, None] < part[None, :])
    new = np.arange(TS)
    c[:, S_NEW:S_NEW + TS] = np.where((part[:, None] == CH - 1) & (new[None, :] <= row[:, None] % TS), 0, -BIG)
    for half in range(2):
        c[:, S_SLOT + half] = p + 1 + P * half
        c[:, S_ROWBASE + half:S_ROWBASE + 2 * NS:2] = np.arange(NS) * NPAGES
    c[:, S_IOTA:S_IOTA + TOPK] = np.arange(TOPK) + 1
    c[:, S_HALF:S_W] = 2.0 ** -(np.arange(NSTEP) + 1.0)
    return c


def sample_index_phase(nc, t):
    with ExitStack() as ctx:
        sb = lambda name, shape, dt=F32: ctx.enter_context(nc.sbuf_tensor("s_" + name, shape, dt))
        sem = lambda name: ctx.enter_context(nc.semaphore("s_" + name))
        Q = 4
        GROUPS_Q = 4
        G = Q * GROUPS_Q
        signal = lambda name, per: Signal(sem(name), per, tiles=1)
        PAIRS = NB // 2
        QW = PAGE // Q * HD

        c = sb("consts", [P, S_W])
        ident = c[:, S_ID:S_ID + P]
        pti = sb("pti", [P, NB], I32)
        ptf = sb("ptf", [P, NB])
        rowf = sb("rowf", [P, NB, Q])
        row = sb("row", [P, PAIRS, 2 * Q], U32)
        rown = sb("rown", [P, 2 * Q], U32)
        keys = sb("keys", [P, 2, 2, QW])
        kT = sb("kT", [P, 2, 2, 512])
        qd = sb("qd", [P, IH, NS])
        qb = sb("qb", [P, PAIRS, 2 * 64])
        qn = sb("qn", [P, 2 * 64])
        wv = sb("wv", [P, PAIRS])
        wb = sb("wb", [P, PAIRS, 16])
        wn = sb("wn", [P, 16])
        kin = sb("kin", [P, NS])
        relu = sb("relu", [P, 2, 512])
        out = sb("out", [16, NPAGES, PAGE // 2])
        rnew = sb("rnew", [P, PAIRS * TS])
        onew = sb("onew", [16, PAIRS * TS])
        pk = ctx.enter_context(nc.psum_tensor("s_pk", [P, 2, 2, 512], F32))
        p1 = ctx.enter_context(nc.psum_tensor("s_p1", [P, 2, 512], F32))
        p2 = ctx.enter_context(nc.psum_tensor("s_p2", [P, 2, 512], F32))

        loaded = sem("loaded")
        weights = sem("weights")
        pages = sem("pages")
        ready = sem("ready")
        rows_done = sem("rows_done")
        rown_done = signal("rown_done", 1)
        may_gather = sem("may_gather")
        landed = [sem(f"landed{s}") for s in range(2)]
        new1, new2, new3, new4 = sem("new1"), sem("new2"), sem("new3"), sem("new4")
        pair_ready = signal("pair_ready", 1)
        turned = signal("turned", G)
        kT0 = signal("kT0", G)
        kT1 = signal("kT1", G)
        prod = signal("prod", G)
        relued = signal("relued", G)
        summed = signal("summed", G)
        kept = signal("kept", G)
        stored = sem("stored")
        new_stored = sem("new_stored")

        block = ctx.enter_context(nc.Block())

        @block.sync
        def _(sp):
            sp.sem_inc(stored, 64)
            sp.dma_start(pti[:], t.page_table.rearrange("b p -> p b"), allow_slow_non_contiguous=True).then_inc(pages, 16)
            sp.dma_start(c[:], t.s_c).then_inc(loaded, 16)
            tr = t.tr[SEQ:SEQ + P, :]
            for par in range(2):
                for half in range(2):
                    sp.dma_start(qd[par * HD:(par + 1) * HD, half * 4:half * 4 + 4, :],
                                 tr[half * HD:(half + 1) * HD, 4 * P:8 * P].rearrange("p (j c) -> p j c", j=4)[:, :, 0:NS]).then_inc(loaded, 16)
            sp.dma_start(kin[:], tr[:, 9 * P:9 * P + NS]).then_inc(loaded, 16)
            w = t.kiv[SEQ:SEQ + NS, 320:328].rearrange("(a b t) h -> b h t a", b=2, t=TS)
            for b2 in range(2):
                for par in range(2):
                    for h in range(IH):
                        at = b2 * 64 + par * 32 + h * TS
                        sp.dma_start(wv[at:at + TS, :], w[b2, h], allow_slow_non_contiguous=True).then_inc(weights, 16)
            sp.wait_ge(new4, 1)
            sp.dma_start(t.snew.rearrange("(a r) k -> r a k", a=PAIRS),
                         onew[:].rearrange("r (a k) -> r a k", a=PAIRS)).then_inc(new_stored, 16)
            sp.wait_ge(new_stored, 16)
            sp.nop()
            with sp.Fori(0, PAIRS) as i:
                base = sp.snap(i * 2 * TS)
                dst = t.sscore[bass.ds(base, 2 * TS)].rearrange("(b t) g x k -> b x t g k", b=2)
                sp.wait_ge(kept.sem, kept.at((i, 0)))
                for b2 in range(2):
                    for par in range(2):
                        at = b2 * 8 + par * 4
                        sp.dma_start(dst[b2, par], out[at:at + TS]).then_inc(stored, 16)
            sp.wait_ge(stored, 64 * (PAIRS + 1))

        @block.gpsimd
        def _(pool):
            rown_done.seed(pool)
            src = t.cache_idx.rearrange("n (q w) -> (n q) w", q=Q)
            pool.wait_ge(rows_done, 1)
            with pool.Fori(0, PAIRS) as i:
                pool.tensor_copy(rown[:], row[:, bass.ds(i, 1), :].rearrange("p a n -> p (a n)")).then_inc(rown_done.sem, 1)
                pool.wait_ge(rown_done.sem, rown_done.at((i, 0)))
                for q in range(Q):
                    if q >= 2:
                        pool.wait_ge(turned.sem, turned.at((i, 0), GROUPS_Q * (q - 1)))
                    else:
                        pool.wait_ge(turned.sem, turned.at((i, -1), GROUPS_Q * (q + 3)))
                    pool.sem_inc(may_gather, 1)
                    for b2 in range(2):
                        pool.indirect_dma_start(out=keys[:, q % 2, b2, :], out_offset=None, in_=src,
                                                in_offset=bass.IndirectOffsetOnAxis(ap=rown[:, b2 * Q + q:b2 * Q + q + 1], axis=0)
                                                ).then_inc(landed[q % 2], 16)
                for s in range(2):
                    pool.wait_ge(landed[s], i * 64 + 64)

        @block.tensor
        def _(pe):
            for s in (turned, prod, summed):
                s.seed(pe)
            pe.wait_ge(loaded, 16 * 6)
            pe.wait_ge(ready, 1)
            for a in range(PAIRS):
                for b2 in range(2):
                    m = pe.matmul(p1[b2 * 64:b2 * 64 + 64, 0, a * TS:(a + 1) * TS], qb[:, a, b2 * 64:b2 * 64 + 64],
                                  kin[:, (2 * a + b2) * TS:(2 * a + b2 + 1) * TS], start=True, stop=True)
            m.then_inc(new1, 1)
            pe.wait_ge(new2, 1)
            for a in range(PAIRS):
                m = pe.matmul(p2[0:16, 0, a * TS:(a + 1) * TS], wb[:, a, :], rnew[:, a * TS:(a + 1) * TS], start=True, stop=True)
            m.then_inc(new3, 1)

            def turn(i, g):
                q, gq = divmod(g, GROUPS_Q)
                if gq == 0:
                    pe.wait_ge(landed[q % 2], i * 64 + 32 * (q // 2 + 1))
                for k in (kT0, kT1):
                    pe.wait_ge(k.sem, k.at((i, 0), g - 1))
                for b2 in range(2):
                    for j in range(4):
                        at = (gq * 4 + j) * 2 * HD
                        m = pe.transpose(pk[:, g % 2, b2, j * P:(j + 1) * P], keys[:, q % 2, b2, at:at + 2 * HD], ident)
                m.then_inc(turned.sem, 1)

            def products(i, g):
                pe.wait_ge(relued.sem, relued.at((i, 0), g - 1))
                for b2, k in enumerate((kT0, kT1)):
                    pe.wait_ge(k.sem, k.at((i, 0), g + 1))
                    m = pe.matmul(p1[b2 * 64:b2 * 64 + 64, g % 2, :], qn[:, b2 * 64:b2 * 64 + 64], kT[:, g % 2, b2, :],
                                  start=True, stop=True)
                m.then_inc(prod.sem, 1)

            def sums(i, g):
                pe.wait_ge(kept.sem, kept.at((i, 0), g - 1))
                pe.wait_ge(relued.sem, relued.at((i, 0), g + 1))
                pe.matmul(p2[0:16, g % 2, :], wn[:], relu[:, g % 2, :], start=True, stop=True).then_inc(summed.sem, 1)

            pe.wait_ge(new4, 1)
            with pe.Fori(0, PAIRS) as i:
                for g in range(G + 2):
                    if g < G:
                        turn(i, g)
                    if g == 1:
                        pe.wait_ge(pair_ready.sem, pair_ready.at((i, 0)))
                    if 1 <= g <= G:
                        products(i, g - 1)
                    if g >= 2:
                        sums(i, g - 2)

        @block.scalar
        def _(act):
            for s in (kT0, relued):
                s.seed(act)
            act.wait_ge(new1, 1)
            act.activation(rnew[:], p1[:, 0, 0:PAIRS * TS], ACT.Relu).then_inc(new2, 1)

            with act.Fori(0, PAIRS) as i:
                for g in range(G + 1):
                    if g < G:
                        act.wait_ge(turned.sem, turned.at((i, 0), g + 1))
                        act.wait_ge(prod.sem, prod.at((i, 0), g - 1))
                        act.activation(kT[:, g % 2, 0, :], pk[:, g % 2, 0, :], ACT.Copy).then_inc(kT0.sem, 1)
                    if g >= 1:
                        h = g - 1
                        act.wait_ge(prod.sem, prod.at((i, 0), h + 1))
                        act.wait_ge(summed.sem, summed.at((i, 0), h - 1))
                        act.activation(relu[:, h % 2, :], p1[:, h % 2, :], ACT.Relu).then_inc(relued.sem, 1)

        @block.vector
        def _(dve):
            for s in (pair_ready, kT1, kept):
                s.seed(dve)
            dve.memset(qb[:].rearrange("p a n -> p (a n)"), 0.0)
            dve.wait_ge(pages, 16)
            dve.tensor_copy(ptf[:], pti[:])
            dve.drain()
            for q in range(Q):
                dve.tensor_scalar(rowf[:, :, q], ptf[:], float(Q), float(q), ALU.mult, ALU.add)
            dve.drain()
            dve.tensor_copy(row[:].rearrange("p a n -> p (a n)"), rowf[:].rearrange("p b q -> p (b q)")).then_inc(rows_done, 1)
            dve.wait_ge(loaded, 16 * 6)
            dve.wait_ge(weights, 16 * 4 * IH)
            for par in range(2):
                rows = slice(par * HD, (par + 1) * HD)
                dst = qb[rows].rearrange("p a (b x h t) -> p (a b) x h t", b=2, x=2, h=IH)[:, :, par]
                dve.tensor_copy(dst, qd[rows].rearrange("p h (b t) -> p b h t", b=NB))
            for a in range(PAIRS):
                m = dve.tensor_scalar(wb[:, a, :], c[:, S_PAIR:S_PAIR + 16], wv[:, a:a + 1], None, ALU.mult)
            dve.drain().then_inc(ready, 1)
            dve.wait_ge(new3, 1)
            dve.tensor_copy(onew[:], p2[0:16, 0, 0:PAIRS * TS]).then_inc(new4, 1)

            with dve.Fori(0, PAIRS) as i:
                dve.wait_ge(summed.sem, summed.at((i, -1)))
                dve.wait_ge(stored, i * 64 + 64)
                dve.tensor_copy(qn[:], qb[:, bass.ds(i, 1), :].rearrange("p a n -> p (a n)"))
                dve.tensor_copy(wn[:], wb[:, bass.ds(i, 1), :].rearrange("p a n -> p (a n)"))
                dve.drain().then_inc(pair_ready.sem, 1)
                for g in range(G + 2):
                    if g < G:
                        dve.wait_ge(turned.sem, turned.at((i, 0), g + 1))
                        dve.wait_ge(prod.sem, prod.at((i, 0), g - 1))
                        dve.tensor_copy(kT[:, g % 2, 1, :], pk[:, g % 2, 1, :]).then_inc(kT1.sem, 1)
                    if g >= 2:
                        h = g - 2
                        dve.wait_ge(summed.sem, summed.at((i, 0), h + 1))
                        dve.tensor_copy(out[:, :, h * 4:h * 4 + 4].rearrange("r g k -> r k g"),
                                        p2[0:16, h % 2, :].rearrange("r (k g) -> r k g", k=4)).then_inc(kept.sem, 1)


TABW = PAGE + 1


def sample_select_phase(nc, t):
    with ExitStack() as ctx:
        sb = lambda name, shape, dt=F32: ctx.enter_context(nc.sbuf_tensor("k_" + name, shape, dt))
        sem = lambda name: ctx.enter_context(nc.semaphore("k_" + name))
        N = CKEYS + TS
        c = sb("consts", [P, S_W])
        ident = c[:, S_ID:S_ID + P]
        raw = sb("raw", [P, CKEYS])
        score = sb("score", [P, N])
        new = sb("new", [P, TS])
        above = sb("above", [P, N])
        band = sb("band", [P, N])
        rank = sb("rank", [P, N])
        table = sb("table", [P, CPAGES, TABW])
        phi = sb("phi", [P, CPAGES], I32)
        ends = sb("ends", [P, CPAGES])
        newmask = sb("newmask", [P, TS])
        ext = sb("ext", [P, 2])
        extr = sb("extr", [2, CH, NS])
        lim = sb("lim", [P, 8])
        pair = sb("pair", [P, 2])
        step = sb("step", [P, NSTEP])
        mid = sb("mid", [P, NSTEP])
        cnt = sb("cnt", [P, NSTEP])
        tot = sb("tot", [P, NSTEP])
        ps = ctx.enter_context(nc.psum_tensor("k_ps", [P, 2, 512], F32))
        lo, hi, took, need = (lim[:, j:j + 1] for j in range(4))

        loaded, new_in, pages_in = sem("loaded"), sem("new_in"), sem("pages_in")
        new_clear = sem("new_clear")
        asked = sem("asked")
        told = sem("told")
        done, stored = sem("done"), sem("stored")
        block = ctx.enter_context(nc.Block())

        @block.sync
        def _(sp):
            for a in range(CH):
                sp.dma_start(raw[a * NS:(a + 1) * NS, :],
                             t.sscore.rearrange("r (c g) x k -> c r (g x k)", c=CH)[a]).then_inc(loaded, 16)
            sp.dma_start(c[:], t.s_c).then_inc(loaded, 16)
            for a in range(CH):
                for b in range(NB):
                    at = a * NS + b * TS
                    sp.dma_start(phi[at:at + TS, :], t.page_table[b, a * CPAGES:(a + 1) * CPAGES].partition_broadcast(TS)
                                 ).then_inc(pages_in, 16)
            sp.wait_ge(new_clear, 1)
            sp.dma_start(new[(CH - 1) * NS:P, :], t.snew.rearrange("(b x t) k -> x b t k", x=2, t=TS)[0]).then_inc(new_in, 16)
            sp.wait_ge(done, 1)
            for a in range(CH):
                rows = slice(a * NS, (a + 1) * NS)
                sp.dma_start(t.table.rearrange("(r c g) n -> c r (g n)", r=NS, c=CH)[a],
                             table[rows].rearrange("p g n -> p (g n)")).then_inc(stored, 16)
                sp.dma_start(t.pagecum.rearrange("r (c g) -> c r g", c=CH)[a], ends[rows, :]).then_inc(stored, 16)
            sp.dma_start(t.newmask, newmask[(CH - 1) * NS:P, :]).then_inc(stored, 16)
            sp.wait_ge(stored, 16 * (2 * CH + 1))

        asks = ["turn", "back"] + ["same"] * NSTEP + ["same", "lower", "lower"]

        @block.tensor
        def _(pe):
            pe.wait_ge(loaded, 16 * (CH + 1))
            for n, kind in enumerate(asks):
                pe.wait_ge(asked, n + 1)
                out = ps[:, n % 2, :]
                if kind == "turn":
                    m = pe.transpose(out[0:2, 0:P], ext[:], ident)
                elif kind == "back":
                    m = pe.transpose(out[:, 0:2], extr[:].rearrange("x c r -> x (c r)"), ident[0:2, 0:2])
                elif kind == "same":
                    src = cnt[:, n - 2:n - 1] if n < 2 + NSTEP else pair[:, 0:1]
                    m = pe.matmul(out[:, 0:1], c[:, S_SAME:S_SAME + P], src, start=True, stop=True)
                else:
                    m = pe.matmul(out[:, 0:1], c[:, S_LOWER:S_LOWER + P], pair[:, 1:2], start=True, stop=True)
                m.then_inc(told, 1)

        @block.scalar
        def _(act):
            pass

        @block.vector
        def _(dve):
            asked_n = [0]

            def ask(ins):
                ins.then_inc(asked, 1)
                asked_n[0] += 1
                dve.wait_ge(told, asked_n[0])
                return ps[:, (asked_n[0] - 1) % 2, :]

            dve.memset(new[:], 0.0).then_inc(new_clear, 1)
            dve.wait_ge(loaded, 16 * (CH + 1))
            dve.tensor_copy(score[:, 0:CKEYS].rearrange("p (g k x) -> p g x k", g=CPAGES, x=2),
                            raw[:].rearrange("p (g x k) -> p g x k", g=CPAGES, x=2))
            dve.wait_ge(new_in, 16)
            dve.tensor_tensor(score[:, CKEYS:N], new[:], c[:, S_NEW:S_NEW + TS], ALU.add)
            dve.drain()
            dve.tensor_reduce(ext[:, 0:1], score[:], AX.X, ALU.max)
            dve.tensor_reduce(ext[:, 1:2], score[:, 0:CKEYS], AX.X, ALU.min)
            dve.drain()
            out = ask(dve.tensor_scalar(ext[:, 1:2], ext[:, 1:2], -1.0, None, ALU.mult))
            dve.tensor_reduce(extr[:, 0, :], out[0:2, 0:P].rearrange("x (c r) -> x r c", c=CH), AX.X, ALU.max)
            dve.drain()
            out = ask(dve.tensor_copy(extr[:, 1:CH, :], bc(extr[:, 0, :], 1, CH - 1)))
            dve.tensor_copy(hi, out[:, 0:1])
            dve.tensor_scalar(lo, out[:, 1:2], -1.0, None, ALU.mult)
            dve.drain()
            dve.tensor_tensor(took, hi, lo, ALU.subtract)
            dve.drain()
            dve.tensor_scalar(step[:], c[:, S_HALF:S_HALF + NSTEP], took, None, ALU.mult)
            dve.drain()
            dve.tensor_tensor(mid[:, 0:1], lo, step[:, 0:1], ALU.add)
            dve.drain()
            for k in range(NSTEP):
                out = ask(dve.tensor_scalar(above[:], score[:], mid[:, k:k + 1], None, ALU.is_ge, ALU.add,
                                            accum_out=cnt[:, k:k + 1]))
                dve.tensor_copy(tot[:, k:k + 1], out[:, 0:1])
                dve.tensor_scalar(took, out[:, 0:1], TOPK - 0.5, step[:, k:k + 1], ALU.is_ge, ALU.mult)
                dve.drain()
                if k + 1 < NSTEP:
                    dve.scalar_tensor_tensor(mid[:, k + 1:k + 2], lo, took, step[:, k + 1:k + 2], ALU.add, ALU.add)
                dve.tensor_tensor(lo, lo, took, ALU.add)
                dve.drain()
            dve.tensor_scalar(tot[:], tot[:], TOPK - 0.5, BIG, ALU.is_ge, ALU.mult)
            dve.drain()
            dve.tensor_tensor(mid[:], mid[:], tot[:], ALU.add)
            dve.drain()
            dve.tensor_reduce(took, mid[:], AX.X, ALU.min)
            dve.drain()
            dve.tensor_tensor(hi, hi, took, ALU.min)
            dve.drain()
            out = ask(dve.tensor_scalar(above[:], score[:], hi, None, ALU.is_gt, ALU.add, accum_out=pair[:, 0:1]))
            dve.tensor_scalar(need, out[:, 0:1], -1.0, float(TOPK), ALU.mult, ALU.add)
            dve.scalar_tensor_tensor(band[:], score[:], lo, above[:], ALU.is_ge, ALU.subtract)
            dve.drain()
            dve.tensor_tensor_scan(rank[:], band[:], band[:], 0.0, ALU.add, ALU.max)
            dve.drain()
            out = ask(dve.tensor_copy(pair[:, 1:2], rank[:, N - 1:N]))
            dve.tensor_tensor(need, need, out[:, 0:1], ALU.subtract)
            dve.drain()
            dve.scalar_tensor_tensor(band[:], rank[:], need, band[:], ALU.is_le, ALU.mult)
            dve.drain()
            dve.tensor_tensor(band[:], band[:], above[:], ALU.add)
            dve.drain()
            dve.tensor_scalar(newmask[:], band[:, CKEYS:N], -1.0, BIG, ALU.add, ALU.mult)
            dve.tensor_tensor_scan(rank[:, 0:CKEYS], band[:, 0:CKEYS], band[:, 0:CKEYS], 0.0, ALU.add, ALU.max)
            dve.drain()
            out = ask(dve.tensor_copy(pair[:, 1:2], rank[:, CKEYS - 1:CKEYS]))
            dve.tensor_copy(lo, out[:, 0:1])
            dve.drain()
            dve.tensor_scalar(table[:, :, 0:PAGE], rank[:, 0:CKEYS].rearrange("p (g n) -> p g n", g=CPAGES), lo, None, ALU.add)
            dve.wait_ge(pages_in, 16 * CH * NB)
            dve.tensor_copy(table[:, :, PAGE], phi[:])
            dve.drain()
            dve.tensor_copy(ends[:], table[:, :, PAGE - 1])
            dve.drain().then_inc(done, 1)


def sample_attend_phase(nc, t):
    with ExitStack() as ctx:
        sb = lambda name, shape, dt=F32: ctx.enter_context(nc.sbuf_tensor("g_" + name, shape, dt))
        sem = lambda name: ctx.enter_context(nc.semaphore("g_" + name))
        S2 = 2 * NS
        W = TOPK + TS
        HALFR = NS // 2

        c = sb("consts", [P, S_W])
        ident = c[:, S_ID:S_ID + P]
        cum = sb("cum", [P, NS, NPAGES])
        less = sb("less", [P, NS, NPAGES])
        page = sb("page", [P, NS, 2])
        rowt = sb("rowt", [P, S2], U32)
        pages = sb("pages", [P, S2, TABW])
        off = sb("off", [P, NS, 2])
        rowk = sb("rowk", [P, S2], U32)
        kg = sb("kg", [P, S2, P])
        vg = sb("vg", [P, S2, P])
        kT = sb("kT", [P, NS, W])
        kn = sb("kn", [P, NS])
        vn = sb("vn", [TS, NB, P])
        qT = sb("qT", [P, 4, NS])
        qz = sb("qz", [P, NS * P + 256])
        have = sb("have", [P, 2])
        mask = sb("mask", [P, 2, W])
        logit = sb("logit", [P, 2, W])
        mx = sb("mx", [P, 4])
        rs = sb("rs", [P, 2])
        pT = sb("pT", [P, 2, 2, P])
        pTn = sb("pTn", [TS, 2, P])
        at_ = sb("at", [P, 4, NS])
        att = sb("att", [NS, KVH, 4, HD])
        pk = ctx.enter_context(nc.psum_tensor("g_pk", [P, 4, 512], F32))
        pl = ctx.enter_context(nc.psum_tensor("g_pl", [P, 2, 512], F32))
        po = ctx.enter_context(nc.psum_tensor("g_po", [P, 512], F32))
        pf = ctx.enter_context(nc.psum_tensor("g_pf", [P, 512], F32))

        loaded, cum_in, q_in = sem("loaded"), sem("cum_in"), sem("q_in")
        rowt_done, rowk_done = sem("rowt_done"), sem("rowk_done")
        pages_in, k_in, v_in = sem("pages_in"), sem("k_in"), sem("v_in")
        q_ready = sem("q_ready")
        turned, kT_done = sem("turned"), sem("kT_done")
        logits, max_done, exp_done, normed = sem("logits"), sem("max_done"), sem("exp_done"), sem("normed")
        pturned, pT_done = sem("pturned"), sem("pT_done")
        pv, att_done, fturned, out_done, stored = sem("pv"), sem("att_done"), sem("fturned"), sem("out_done"), sem("stored")
        block = ctx.enter_context(nc.Block())

        @block.sync
        def _(sp):
            sp.dma_start(cum[:].rearrange("p r g -> p (r g)"),
                         t.pagecum.rearrange("r g -> (r g)").partition_broadcast(P)).then_inc(cum_in, 16)
            sp.dma_start(c[:], t.s_c).then_inc(loaded, 16)
            tr = t.tr[SEQ:SEQ + P, :]
            sp.dma_start(qT[:], tr[:, 0:4 * P].rearrange("p (j c) -> p j c", j=4)[:, :, 0:NS]).then_inc(q_in, 16)
            sp.dma_start(kn[:], tr[:, 8 * P:8 * P + NS]).then_inc(q_in, 16)
            sp.dma_start(vn[:], t.kiv[SEQ:SEQ + NS, 192:320].rearrange("(b t) d -> t b d", b=NB)).then_inc(q_in, 16)
            for g in range(2):
                for r in range(HALFR):
                    row = g * HALFR + r
                    sp.dma_start(have[r * AH:(r + 1) * AH, g:g + 1],
                                 t.pagecum[row, NPAGES - 1:NPAGES].partition_broadcast(AH)).then_inc(q_in, 16)
                    sp.dma_start(mask[r * AH:(r + 1) * AH, g, TOPK:W],
                                 t.newmask[row, :].partition_broadcast(AH)).then_inc(q_in, 16)
            sp.wait_ge(out_done, 1)
            sp.dma_start(t.cat[SEQ:SEQ + NS, 0:512], att[:].rearrange("p v j d -> p (v j d)")).then_inc(stored, 16)
            sp.wait_ge(stored, 16)

        @block.gpsimd
        def _(pool):
            pool.wait_ge(rowt_done, 1)
            for s in range(S2):
                pool.indirect_dma_start(out=pages[:, s, :], out_offset=None, in_=t.table,
                                        in_offset=bass.IndirectOffsetOnAxis(ap=rowt[:, s:s + 1], axis=0)).then_inc(pages_in, 16)
            pool.wait_ge(rowk_done, 1)
            for s in range(S2):
                pool.indirect_dma_start(out=kg[:, s, :], out_offset=None, in_=t.cache_k,
                                        in_offset=bass.IndirectOffsetOnAxis(ap=rowk[:, s:s + 1], axis=0)).then_inc(k_in, 16)
            for s in range(S2):
                pool.indirect_dma_start(out=vg[:, s, :], out_offset=None, in_=t.cache_v,
                                        in_offset=bass.IndirectOffsetOnAxis(ap=rowk[:, s:s + 1], axis=0)).then_inc(v_in, 16)
            pool.wait_ge(k_in, 16 * S2)
            pool.wait_ge(v_in, 16 * S2)

        KG = S2 // 4

        @block.tensor
        def _(pe):
            pe.wait_ge(loaded, 16)
            pe.wait_ge(k_in, 16 * S2)
            for n in range(KG):
                if n >= 4:
                    pe.wait_ge(kT_done, n - 3)
                for j in range(4):
                    m = pe.transpose(pk[:, n % 4, j * P:(j + 1) * P], kg[:, 4 * n + j, :], ident)
                m.then_inc(turned, 1)
            pe.wait_ge(q_ready, 1)
            pe.wait_ge(kT_done, KG)
            for g in range(2):
                for r in range(HALFR):
                    row = g * HALFR + r
                    m = pe.matmul(pl[:, g, 0:W], qz[:, row * P:(row + 1) * P], kT[:, row, :], start=(r == 0), stop=(r == HALFR - 1))
                m.then_inc(logits, 1)
            for g in range(2):
                pe.wait_ge(normed, g + 1)
                for half in range(2):
                    pe.transpose(pk[:, g, half * P:(half + 1) * P], logit[:, g, half * P:(half + 1) * P], ident)
                pe.transpose(pk[0:TS, g, 2 * P:3 * P], logit[:, g, TOPK:W], ident).then_inc(pturned, 1)
            pe.wait_ge(pT_done, 2)
            pe.wait_ge(v_in, 16 * S2)
            for row in range(NS):
                g, r = divmod(row, HALFR)
                cols = slice(r * AH, (r + 1) * AH)
                out = po[:, row * AH:(row + 1) * AH]
                for half in range(2):
                    pe.matmul(out, vg[:, 2 * row + half, :], pT[:, g, half, cols], start=(half == 0), stop=False)
                m = pe.matmul(out, vn[:, row // TS, :], pTn[:, g, cols], start=False, stop=True)
            m.then_inc(pv, 1)
            pe.wait_ge(att_done, 1)
            for j in range(4):
                m = pe.transpose(pf[0:NS, j * P:(j + 1) * P], at_[:, j, :], ident)
            m.then_inc(fturned, 1)

        @block.scalar
        def _(act):
            for n in range(KG):
                act.wait_ge(turned, n + 1)
                act.activation(kT[:, 2 * n:2 * n + 2, 0:TOPK], pk[:, n % 4, :].rearrange("p (r c) -> p r c", r=2), ACT.Copy).then_inc(kT_done, 1)
            for g in range(2):
                act.wait_ge(max_done, g + 1)
                act.activation(logit[:, g, :], logit[:, g, :], ACT.Exp, bias=mx[:, 2 + g:3 + g], scale=HD ** -0.5,
                               accum_out=rs[:, g:g + 1]).then_inc(exp_done, 1)

        @block.vector
        def _(dve):
            def slots_less(src, out, width):
                for half in range(2):
                    dve.tensor_scalar(less[:], src(half), c[:, S_SLOT + half:S_SLOT + half + 1], None, ALU.is_lt)
                    dve.drain()
                    dve.tensor_reduce(out[:, :, half], less[:], AX.X, ALU.add)
                    dve.drain()

            flat = lambda a: a[:].rearrange("p r h -> p (r h)")
            dve.wait_ge(loaded, 16)
            dve.wait_ge(cum_in, 16)
            slots_less(lambda half: cum[:], page, NPAGES)
            dve.tensor_scalar(flat(page), flat(page), NPAGES - 1.0, None, ALU.min)
            dve.drain()
            dve.tensor_tensor(flat(page), flat(page), c[:, S_ROWBASE:S_ROWBASE + S2], ALU.add)
            dve.drain()
            dve.tensor_copy(rowt[:], flat(page)).then_inc(rowt_done, 1)
            dve.memset(qz[:], 0.0)
            dve.drain()
            dve.wait_ge(q_in, 16 * (3 + 2 * NS))
            for kv in range(KVH):
                rows = slice(kv * HD, (kv + 1) * HD)
                for g in range(2):
                    at = g * HALFR * P + kv * 4
                    dst = qz[rows, at:at + HALFR * (P + AH)].rearrange("p (r x) -> p r x", x=P + AH)[:, :, 0:4]
                    m = dve.tensor_copy(dst, qT[rows, :, g * HALFR:(g + 1) * HALFR].rearrange("p j r -> p r j"))
            for g in range(2):
                dve.tensor_scalar(mask[:, g, 0:TOPK], c[:, S_IOTA:S_IOTA + TOPK], have[:, g:g + 1], -BIG, ALU.is_gt, ALU.mult)
            dve.tensor_copy(kT[:, :, TOPK:W].rearrange("p (b t) k -> p b t k", b=NB),
                            kn[:].rearrange("p (b k) -> p b k", b=NB).unsqueeze(2).broadcast_to([P, NB, TS, TS]))
            dve.drain().then_inc(q_ready, 1)
            dve.wait_ge(pages_in, 16 * S2)
            slots_less(lambda half: pages[:].rearrange("p (r h) n -> p r h n", h=2)[:, :, half, 0:PAGE], off, PAGE)
            dve.tensor_scalar(flat(off), flat(off), PAGE - 1.0, None, ALU.min)
            dve.drain()
            dve.scalar_tensor_tensor(flat(off), pages[:, :, PAGE], float(PAGE), flat(off), ALU.mult, ALU.add)
            dve.drain()
            dve.tensor_copy(rowk[:], flat(off)).then_inc(rowk_done, 1)
            for g in range(2):
                dve.wait_ge(logits, g + 1)
                dve.tensor_tensor_reduce(logit[:, g, :], pl[:, g, 0:W], mask[:, g, :], 1.0, -3.0e38, ALU.add, ALU.max,
                                         accum_out=mx[:, g:g + 1])
                dve.drain()
                dve.tensor_scalar(mx[:, 2 + g:3 + g], mx[:, g:g + 1], -(HD ** -0.5), None, ALU.mult).then_inc(max_done, 1)
            for g in range(2):
                dve.wait_ge(exp_done, g + 1)
                dve.reciprocal(rs[:, g:g + 1], rs[:, g:g + 1])
                dve.drain()
                dve.tensor_scalar(logit[:, g, :], logit[:, g, :], rs[:, g:g + 1], None, ALU.mult).then_inc(normed, 1)
            for g in range(2):
                dve.wait_ge(pturned, g + 1)
                dve.tensor_copy(pT[:, g].rearrange("p h c -> p (h c)"), pk[:, g, 0:2 * P])
                dve.tensor_copy(pTn[:, g, :], pk[0:TS, g, 2 * P:3 * P])
                dve.drain().then_inc(pT_done, 1)
            dve.wait_ge(pv, 1)
            for kv in range(KVH):
                rows = slice(kv * HD, (kv + 1) * HD)
                dve.tensor_copy(at_[rows], po[rows, 0:NS * AH].rearrange("p (r v j) -> p v j r", v=KVH, j=4)[:, kv])
            dve.drain().then_inc(att_done, 1)
            dve.wait_ge(fturned, 1)
            dve.tensor_copy(att[:], pf[0:NS, :].rearrange("p (j v d) -> p v j d", j=4, v=KVH)).then_inc(out_done, 1)


CK = 416
TT = 104
NCHUNK = (SEQ + NS) // CK
FB = DFF // P
KPL = PLE // P
F32R = mybir.dt.float32r


def dense_phase(nc, t):
    with ExitStack() as ctx:
        sb = lambda name, shape, dt=F32: ctx.enter_context(nc.sbuf_tensor("d_" + name, shape, dt))
        sem = lambda name: ctx.enter_context(nc.semaphore("d_" + name))
        signal = lambda name, per: Signal(sem(name), per, tiles=1)
        RING = 4
        ident = sb("ident", [P, P])[:]
        ones = sb("ones", [P, 1])
        gains = sb("gains", [P, 3, KD])
        raw = sb("raw", [P, RING, KD * P])
        wh = sb("wh", [P, RING, KD * P], F32R)
        wl = sb("wl", [P, RING, KD * P], F32R)
        catx = sb("catx", [TT, 2, 2, D])
        ple = sb("ple", [TT, 2, PLE])
        hT = sb("hT", [P, KD, CK])
        nh = sb("nh", [P, KD, CK], F32R)
        nl = sb("nl", [P, KD, CK], F32R)
        pTh = sb("pTh", [P, KPL, CK], F32R)
        pTl = sb("pTl", [P, KPL, CK], F32R)
        ah = sb("ah", [P, FB, CK], F32R)
        al = sb("al", [P, FB, CK], F32R)
        sq = sb("sq", [P, 2, CK])
        acc = sb("acc", [P, CK])
        ms = sb("ms", [TT, 4])
        rstd = sb("rstd", [TT, 4])
        mhalf = sb("mhalf", [TT, 4])
        factor = sb("factor", [P, CK])
        gate = sb("gate", [P, 2, CK])
        sig = sb("sig", [P, 2, CK])
        y = sb("y", [TT, 2, 512])
        pm = ctx.enter_context(nc.psum_tensor("d_pm", [P, 4, 512], F32))
        pt = ctx.enter_context(nc.psum_tensor("d_pt", [P, 2, 512], F32))
        pn = ctx.enter_context(nc.psum_tensor("d_pn", [P, 512], F32))
        pb = ctx.enter_context(nc.psum_tensor("d_pb", [P, 512], F32))

        FFN0, DOWN0, PLE0 = KD, KD + 2 * FB, 2 * KD + 2 * FB
        MM = PLE0 + 2 * KD
        PARTS = [range(0, 8), range(8, 15), range(15, FB)]
        NP = len(PARTS)
        ITEMS = PLE0 + (NP - 1) * KD + 2 * KD
        LEAD = RING - 1

        def first_item(p):
            return p if p < DOWN0 else DOWN0 + NP * (p - DOWN0) if p < PLE0 else DOWN0 + NP * KD + p - PLE0

        def item(m):
            m %= ITEMS
            if m < DOWN0:
                w_, col = (t.w_out, m) if m < FFN0 else (t.w_ffn_in, (m - FFN0) % 2 * FB + (m - FFN0) // 2)
                blocks = range(KD)
            elif m < DOWN0 + NP * KD:
                w_, (col, part) = t.w_ffn_out, divmod(m - DOWN0, NP)
                blocks = PARTS[part]
            else:
                col, g = divmod(m - DOWN0 - NP * KD, 2)
                w_, blocks = (t.w_ple_gate, range(KD)) if g else (t.w_ple_proj, range(KPL))
            return w_.rearrange("(k p) c -> p k c", p=P)[:, blocks[0]:blocks[-1] + 1, col * P:(col + 1) * P], len(blocks)

        def items_at(p):
            return range(first_item(p) + LEAD, first_item(p + 1) + LEAD)

        loaded = sem("loaded")
        in_landed = [sem(f"in_landed{s}") for s in range(2)]
        w_landed = [sem(f"w_landed{s}") for s in range(RING)]
        y_stored = [sem(f"y_stored{s}") for s in range(2)]
        ones_done = sem("ones_done")
        w_high = signal("w_high", ITEMS)
        w_split = signal("w_split", ITEMS)
        part_used = signal("part_used", (NP - 1) * KD)
        turned = signal("turned", 28)
        in_high = signal("in_high", 12)
        in_moved = signal("in_moved", 20)
        y_moved = signal("y_moved", 8)
        prod = signal("prod", MM)
        used = signal("used", MM)
        summed = signal("summed", 3 * KD)
        squared = signal("squared", 3 * KD)
        sq_added = signal("sq_added", 3 * KD)
        n_high = signal("n_high", 2 * KD)
        n_split = signal("n_split", 2 * KD)
        ms_psum = signal("ms_psum", 3)
        ms_done = signal("ms_done", 3)
        rstd_done = signal("rstd_done", 3)
        spread = signal("spread", 3)
        factor_done = signal("factor_done", 3)
        normed = signal("normed", KD)
        gated = signal("gated", KD)
        sig_done = signal("sig_done", FB + KD)
        a_ready = signal("a_ready", FB)
        a_high = signal("a_high", FB)
        a_split = signal("a_split", FB)
        block = ctx.enter_context(nc.Block())

        @block.sync
        def _(sp):
            sp.dma_start(ident, t.c[:, C_ID:C_ID + P]).then_inc(loaded, 16)
            for j, g in enumerate((t.g_ffn, t.g_ple, t.g_final)):
                sp.dma_start(gains[:, j, :], g.rearrange("(k p) -> p k", p=P), allow_slow_non_contiguous=True).then_inc(loaded, 16)

            def load(m):
                src, blocks = item(m)
                sp.dma_start(raw[:, m % RING, 0:blocks * P].rearrange("p (k c) -> p k c", c=P), src).then_inc(w_landed[m % RING], 16)

            for m in range(LEAD):
                load(m)
            with sp.Fori(0, NCHUNK) as i:
                n = (i, 0)
                rows = [sp.snap(i * CK + j * TT) for j in range(4)]

                def load_inputs(j):
                    sp.wait_ge(turned.sem, turned.at(n, 5 * (j - 1)) if j >= 2 else turned.at((i, -1), 5 * (j + 3)))
                    s = j % 2
                    sp.dma_start(catx[:, s, 0, :], t.cat[bass.ds(rows[j], TT), :]).then_inc(in_landed[s], 16)
                    sp.dma_start(catx[:, s, 1, :], t.x[bass.ds(rows[j], TT), :]).then_inc(in_landed[s], 16)
                    sp.dma_start(ple[:, s, :], t.p[bass.ds(rows[j], TT), :]).then_inc(in_landed[s], 16)

                for j in range(4):
                    load_inputs(j)
                for m in range(LEAD, LEAD + ITEMS):
                    sp.wait_ge(w_split.sem, w_split.at(n, m - RING + 1))
                    load(m)

        @block.tensor
        def _(pe):
            for s in (turned, prod, part_used, ms_psum, spread):
                s.seed(pe)
            pe.wait_ge(loaded, 16 * 4)
            pe.wait_ge(ones_done, 1)

            def turn_inputs(i, j):
                s = j % 2
                n = (i, 0)
                pe.wait_ge(in_landed[s], i * 96 + 48 * (j // 2 + 1))
                for b in range(5):
                    at = 5 * j + b
                    if at < 2:
                        pe.wait_ge(y_moved.sem, y_moved.at(n, at - 1))
                    else:
                        pe.wait_ge(in_moved.sem, in_moved.at(n, at - 1))
                    for k in range(4 if b < 4 else KPL):
                        col = (b // 2 * 4 + k) * P
                        src = catx[:, s, b % 2, col:col + P] if b < 4 else ple[:, s, k * P:(k + 1) * P]
                        m = pe.transpose(pt[:, at % 2, k * TT:(k + 1) * TT], src, ident[0:TT, 0:TT])
                    m.then_inc(turned.sem, 1)

            def product(i, p, operand, ready=None):
                n = (i, 0)
                pe.wait_ge(used.sem, used.at(n, p - 3))
                items = range(first_item(p), first_item(p + 1))
                k = 0
                for m in items:
                    pe.wait_ge(w_split.sem, w_split.at(n, m + 1))
                    blocks = item(m)[1]
                    for b in range(blocks):
                        if ready:
                            ready(k)
                        high, low = operand(k)
                        cols = slice(b * P, (b + 1) * P)
                        out = pm[:, p % 4, 0:CK]
                        last = m == items[-1] and b == blocks - 1
                        pe.matmul(out, wl[:, m % RING, cols], high, start=(k == 0), stop=False)
                        pe.matmul(out, wh[:, m % RING, cols], low, start=False, stop=False)
                        ins = pe.matmul(out, wh[:, m % RING, cols], high, start=False, stop=last)
                        k += 1
                    if not last:
                        ins.then_inc(part_used.sem, 1)
                ins.then_inc(prod.sem, 1)

            def square_sums(i, j):
                pe.wait_ge(sq_added.sem, sq_added.at((i, 0), (j + 1) * KD))
                pe.wait_ge(ms_done.sem, ms_done.at((i, 0), j))
                for b in range(4):
                    m = pe.matmul(pn[0:TT, b:b + 1], acc[:, b * TT:(b + 1) * TT], ones[:], start=True, stop=True)
                m.then_inc(ms_psum.sem, 1)

            def spread_factor(i, j):
                pe.wait_ge(rstd_done.sem, rstd_done.at((i, 0), j + 1))
                pe.wait_ge(factor_done.sem, factor_done.at((i, 0), j))
                for b in range(4):
                    m = pe.matmul(pb[:, b * TT:(b + 1) * TT], rstd[:, b:b + 1].broadcast_to([TT, P]), ident[0:TT, 0:TT],
                                  start=True, stop=True)
                m.then_inc(spread.sem, 1)

            a_part = lambda k: (ah[:, k, :], al[:, k, :])
            n_part = lambda k: (nh[:, k, :], nl[:, k, :])
            p_part = lambda k: (pTh[:, k, :], pTl[:, k, :])
            with pe.Fori(0, NCHUNK) as i:
                n = (i, 0)
                for j in range(4):
                    turn_inputs(i, j)
                pe.wait_ge(in_moved.sem, in_moved.at(n))
                for d in range(KD):
                    product(i, d, a_part)
                for q in range(2 * FB):
                    product(i, FFN0 + q, n_part, (lambda k: pe.wait_ge(n_split.sem, n_split.at(n, k + 1))) if q == 0 else None)
                    if q == 0:
                        square_sums(i, 0)
                    if q == 1:
                        spread_factor(i, 0)
                for d in range(KD):
                    product(i, DOWN0 + d, a_part, (lambda k: pe.wait_ge(a_split.sem, a_split.at(n, k + 1))) if d == 0 else None)
                for d in range(KD):
                    product(i, PLE0 + 2 * d, p_part)
                    product(i, PLE0 + 2 * d + 1, n_part, (lambda k: pe.wait_ge(n_split.sem, n_split.at(n, KD + k + 1))) if d == 0 else None)
                    if d == 0:
                        square_sums(i, 1)
                    if d == 1:
                        spread_factor(i, 1)
                square_sums(i, 2)
                spread_factor(i, 2)
                for b in range(8):
                    at = 20 + b
                    if b < 2:
                        pe.wait_ge(in_moved.sem, in_moved.at(n))
                    else:
                        pe.wait_ge(y_moved.sem, y_moved.at(n, b - 1))
                    j, half = divmod(b, 2)
                    for k in range(4):
                        pe.wait_ge(normed.sem, normed.at(n, half * 4 + k + 1))
                        m = pe.transpose(pt[0:TT, at % 2, k * P:(k + 1) * P], hT[:, half * 4 + k, j * TT:(j + 1) * TT], ident)
                    m.then_inc(turned.sem, 1)

        @block.scalar
        def _(act):
            for s in (in_high, squared, n_high, ms_done, sig_done, a_high, w_high):
                s.seed(act)
            for s in range(2):
                act.sem_inc(y_stored[s], 16)
            act.wait_ge(loaded, 16 * 4)

            def high_part(i, m):
                n = (i, 0)
                cols = slice(0, item(m)[1] * P)
                act.wait_ge(w_landed[m % RING], i * (16 * ITEMS // RING) + 16 * (m // RING + 1))
                back, before = divmod(m - RING, ITEMS)
                d, part = divmod(before - DOWN0, NP)
                if 0 <= d < KD and part < NP - 1:
                    act.wait_ge(part_used.sem, part_used.at((i, back), d * (NP - 1) + part + 1))
                else:
                    p = before if d < 0 else DOWN0 + d if d < KD else before - (NP - 1) * KD
                    act.wait_ge(prod.sem, prod.at((i, back), p + 1))
                act.activation(wh[:, m % RING, cols], raw[:, m % RING, cols], ACT.Copy).then_inc(w_high.sem, 1)

            def high_parts(i, p):
                for m in items_at(p):
                    high_part(i, m)

            def squares(i, j, d):
                n = (i, 0)
                act.wait_ge(summed.sem, summed.at(n, j * KD + d + 1))
                if d == 0:
                    act.wait_ge(ms_psum.sem, ms_psum.at(n, j))
                    act.activation(acc[:], hT[:, 0, :], ACT.Square).then_inc(squared.sem, 1)
                else:
                    act.wait_ge(sq_added.sem, sq_added.at(n, j * KD + d - 1))
                    act.activation(sq[:, d % 2, :], hT[:, d, :], ACT.Square).then_inc(squared.sem, 1)

            def scaled(i, j, d):
                act.activation(nh[:, d, :], hT[:, d, :], ACT.Copy, scale=gains[:, j, d:d + 1]).then_inc(n_high.sem, 1)

            def mean(i, j):
                n = (i, 0)
                act.wait_ge(ms_psum.sem, ms_psum.at(n, j + 1))
                act.wait_ge(rstd_done.sem, rstd_done.at(n, j))
                act.activation(ms[:], pn[0:TT, 0:4], ACT.Copy, scale=1.0 / D, bias=EPS).then_inc(ms_done.sem, 1)

            for m in range(LEAD):
                high_part(0, m)
            with act.Fori(0, NCHUNK) as i:
                n = (i, 0)
                rows = [act.snap(i * CK + j * TT) for j in range(4)]
                for j in range(4):
                    cols = slice(j * TT, (j + 1) * TT)
                    for b in (0, 2, 4):
                        at = 5 * j + b
                        act.wait_ge(turned.sem, turned.at(n, at + 1))
                        if b == 4:
                            dst, src = pTh[:, :, cols], pt[:, at % 2, 0:KPL * TT].rearrange("p (k c) -> p k c", k=KPL)
                        else:
                            dst, src = ah[:, b // 2 * 4:b // 2 * 4 + 4, cols], pt[:, at % 2, 0:4 * TT].rearrange("p (k c) -> p k c", k=4)
                        act.activation(dst, src, ACT.Copy).then_inc(in_high.sem, 1)
                for d in range(KD):
                    high_parts(i, d)
                    squares(i, 0, d)
                    scaled(i, 0, d)
                for f in range(FB):
                    p = FFN0 + 2 * f
                    high_parts(i, p)
                    if f == 0:
                        mean(i, 0)
                    act.wait_ge(used.sem, used.at(n, p + 1))
                    act.activation(sig[:, f % 2, :], gate[:, f % 2, :], ACT.Sigmoid).then_inc(sig_done.sem, 1)
                    high_parts(i, p + 1)
                    act.wait_ge(a_ready.sem, a_ready.at(n, f + 1))
                    act.activation(ah[:, f, :], sq[:, f % 2, :], ACT.Copy).then_inc(a_high.sem, 1)
                for d in range(KD):
                    high_parts(i, DOWN0 + d)
                    squares(i, 1, d)
                    scaled(i, 1, d)
                for d in range(KD):
                    p = PLE0 + 2 * d
                    high_parts(i, p)
                    high_parts(i, p + 1)
                    if d == 0:
                        mean(i, 1)
                    act.wait_ge(gated.sem, gated.at(n, d + 1))
                    act.activation(sig[:, d % 2, :], gate[:, d % 2, :], ACT.Sigmoid).then_inc(sig_done.sem, 1)
                    if d:
                        squares(i, 2, d - 1)
                squares(i, 2, KD - 1)
                mean(i, 2)
                for b in range(8):
                    j, half = divmod(b, 2)
                    act.wait_ge(y_moved.sem, y_moved.at(n, b + 1))
                    act.dma_start(t.y[bass.ds(rows[j], TT), half * 512:(half + 1) * 512], y[:, b % 2, :]).then_inc(y_stored[b % 2], 16)
            for s in range(2):
                act.wait_ge(y_stored[s], 16 + 64 * NCHUNK)

        @block.vector
        def _(dve):
            for s in (in_moved, y_moved, used, summed, n_split, factor_done, normed, gated, a_ready, a_split):
                s.seed(dve)
            dve.memset(ones[:], 1.0).then_inc(ones_done, 1)
            dve.wait_ge(loaded, 16 * 4)

            def add_block(i, p, d):
                dve.wait_ge(prod.sem, prod.at((i, 0), p + 1))
                dve.tensor_tensor(hT[:, d, :], pm[:, p % 4, 0:CK], hT[:, d, :], ALU.add).then_inc(used.sem, 1)
                dve.drain().then_inc(summed.sem, 1)

            def low_part(i, j, d):
                dve.wait_ge(n_high.sem, n_high.at((i, 0), j * KD + d + 1))
                dve.scalar_tensor_tensor(nl[:, d, :], hT[:, d, :], gains[:, j, d:d + 1], nh[:, d, :].bitcast(F32), ALU.mult, ALU.subtract
                                         ).then_inc(n_split.sem, 1)

            def take_factor(i, j):
                dve.wait_ge(spread.sem, spread.at((i, 0), j + 1))
                dve.tensor_copy(factor[:], pb[:, 0:CK]).then_inc(factor_done.sem, 1)
                dve.drain()

            def low_activation(i, f):
                dve.wait_ge(a_high.sem, a_high.at((i, 0), f + 1))
                dve.tensor_tensor(al[:, f, :], sq[:, f % 2, :], ah[:, f, :].bitcast(F32), ALU.subtract).then_inc(a_split.sem, 1)

            with dve.Fori(0, NCHUNK) as i:
                n = (i, 0)
                for j in range(4):
                    cols = slice(j * TT, (j + 1) * TT)
                    for b in range(5):
                        at = 5 * j + b
                        k = 4 if b < 4 else KPL
                        src = pt[:, at % 2, 0:k * TT].rearrange("p (k c) -> p k c", k=k)
                        blocks = slice(b // 2 * 4, b // 2 * 4 + 4)
                        if b in (1, 3):
                            dve.wait_ge(turned.sem, turned.at(n, at + 1))
                            dve.tensor_copy(hT[:, blocks, cols], src).then_inc(in_moved.sem, 1)
                        else:
                            dve.wait_ge(in_high.sem, in_high.at(n, 3 * j + b // 2 + 1))
                            high, low = (pTh[:, :, cols], pTl[:, :, cols]) if b == 4 else (ah[:, blocks, cols], al[:, blocks, cols])
                            dve.tensor_tensor(low, src, high.bitcast(F32), ALU.subtract).then_inc(in_moved.sem, 1)
                dve.drain()
                for d in range(KD):
                    add_block(i, d, d)
                    if d:
                        low_part(i, 0, d - 1)
                low_part(i, 0, KD - 1)
                take_factor(i, 0)
                for f in range(FB):
                    p = FFN0 + 2 * f
                    dve.wait_ge(prod.sem, prod.at(n, p + 1))
                    dve.tensor_tensor(gate[:, f % 2, :], pm[:, p % 4, 0:CK], factor[:], ALU.mult).then_inc(used.sem, 1)
                    if f:
                        low_activation(i, f - 1)
                    dve.drain()
                    dve.wait_ge(sig_done.sem, sig_done.at(n, f + 1))
                    dve.tensor_tensor(sig[:, f % 2, :], gate[:, f % 2, :], sig[:, f % 2, :], ALU.mult)
                    dve.drain()
                    dve.tensor_tensor(sig[:, f % 2, :], sig[:, f % 2, :], factor[:], ALU.mult)
                    dve.drain()
                    dve.wait_ge(prod.sem, prod.at(n, p + 2))
                    dve.tensor_tensor(sq[:, f % 2, :], pm[:, (p + 1) % 4, 0:CK], sig[:, f % 2, :], ALU.mult).then_inc(used.sem, 1)
                    dve.drain().then_inc(a_ready.sem, 1)
                low_activation(i, FB - 1)
                for d in range(KD):
                    add_block(i, DOWN0 + d, d)
                    if d:
                        low_part(i, 1, d - 1)
                low_part(i, 1, KD - 1)
                take_factor(i, 1)
                for d in range(KD):
                    p = PLE0 + 2 * d
                    dve.wait_ge(prod.sem, prod.at(n, p + 2))
                    dve.tensor_tensor(gate[:, d % 2, :], pm[:, (p + 1) % 4, 0:CK], factor[:], ALU.mult).then_inc(gated.sem, 1)
                    dve.wait_ge(sig_done.sem, sig_done.at(n, FB + d + 1))
                    dve.tensor_tensor(sig[:, d % 2, :], pm[:, p % 4, 0:CK], sig[:, d % 2, :], ALU.mult).then_inc(used.sem, 1)
                    dve.drain()
                    dve.tensor_tensor(hT[:, d, :], hT[:, d, :], sig[:, d % 2, :], ALU.add).then_inc(used.sem, 1)
                    dve.drain().then_inc(summed.sem, 1)
                take_factor(i, 2)
                for d in range(KD):
                    dve.scalar_tensor_tensor(hT[:, d, :], hT[:, d, :], gains[:, 2, d:d + 1], factor[:], ALU.mult, ALU.mult
                                             ).then_inc(normed.sem, 1)
                for b in range(8):
                    dve.wait_ge(turned.sem, turned.at(n, 21 + b))
                    dve.wait_ge(y_stored[b % 2], i * 64 + 16 * (b // 2 + 1))
                    dve.tensor_copy(y[:, b % 2, :], pt[0:TT, b % 2, :]).then_inc(y_moved.sem, 1)

        @block.gpsimd
        def _(pool):
            for s in (rstd_done, sq_added, w_split):
                s.seed(pool)
            pool.memset(mhalf[:], -0.5)
            pool.drain()

            def low_part(i, m):
                cols = slice(0, item(m)[1] * P)
                pool.wait_ge(w_high.sem, w_high.at((i, 0), m + 1))
                pool.tensor_tensor(wl[:, m % RING, cols], raw[:, m % RING, cols], wh[:, m % RING, cols].bitcast(F32), ALU.subtract
                                   ).then_inc(w_split.sem, 1)

            def low_parts(i, p):
                for m in items_at(p):
                    low_part(i, m)

            def add_square(i, j, d):
                pool.wait_ge(squared.sem, squared.at((i, 0), j * KD + d + 1))
                if d == 0:
                    pool.sem_inc(sq_added.sem, 1)
                else:
                    pool.tensor_tensor(acc[:], acc[:], sq[:, d % 2, :], ALU.add).then_inc(sq_added.sem, 1)
                    pool.drain()

            def inverse_root(i, j):
                pool.wait_ge(ms_done.sem, ms_done.at((i, 0), j + 1))
                pool.wait_ge(spread.sem, spread.at((i, 0), j))
                pool.tensor_tensor(rstd[:], ms[:], mhalf[:], ALU.pow).then_inc(rstd_done.sem, 1)

            for m in range(LEAD):
                low_part(0, m)
            with pool.Fori(0, NCHUNK) as i:
                for p in range(MM):
                    low_parts(i, p)
                    if p < FFN0:
                        add_square(i, 0, p)
                    elif p == FFN0:
                        inverse_root(i, 0)
                    elif DOWN0 <= p < PLE0:
                        add_square(i, 1, p - DOWN0)
                    elif p == PLE0 + 1:
                        inverse_root(i, 1)
                    elif p > PLE0 + 1 and (p - PLE0) % 2:
                        add_square(i, 2, (p - PLE0) // 2 - 1)
                add_square(i, 2, KD - 1)
                inverse_root(i, 2)


def build(nc, t):
    project_phase(nc, t)
    prompt_phase(nc, t)
    sample_index_phase(nc, t)
    sample_select_phase(nc, t)
    sample_attend_phase(nc, t)
    dense_phase(nc, t)


class Tensors:
    pass


SCRATCH = {
    "tr": (ROWS, TRW), "cat": (ROWS, D), "sscore": (NS, NPAGES, 2, PAGE // 2), "snew": (NB // 2 * 16, TS),
    "table": (NS * NPAGES, TABW), "pagecum": (NS, NPAGES), "newmask": (NS, TS),
}
OUTPUTS = {"y": (ROWS, D), "kiv": (ROWS, KIV), "retn_prompt": (RH, RD, RD), "retn_sample": (NB, RH, RD, RD)}


def kernel(x_prompt, x_sample, cache_k, cache_v, cache_idx_k, state_retn, page_table, p_prompt, p_sample,
           g_mix, w_in, g_retn, w_out, g_ffn, w_ffn_in, w_ffn_out, g_ple, w_ple_gate, w_ple_proj, g_final):
    import concourse.bacc as bacc
    from concourse.bass_utils import run_bass_kernel_spmd

    def rows(prompt, sample, width):
        a = np.asarray(prompt).reshape(SEQ, width)
        b = np.asarray(sample).reshape(NS, width)
        return np.concatenate([a, b, np.zeros((ROWS - SEQ - NS, width), a.dtype)])

    arr = np.asarray
    ins = {
        "x": rows(x_prompt, x_sample, D), "p": rows(p_prompt, p_sample, PLE),
        "cache_k": arr(cache_k).reshape(-1, KVH * HD), "cache_v": arr(cache_v).reshape(-1, KVH * HD),
        "cache_idx": arr(cache_idx_k).reshape(-1, PAGE * HD), "state_retn": arr(state_retn).reshape(NB, RH, RD, RD),
        "page_table": arr(page_table), "g_mix": arr(g_mix)[0], "w_in": arr(w_in)[0], "g_retn": arr(g_retn)[0],
        "w_out": arr(w_out)[0], "g_ffn": arr(g_ffn)[0], "w_ffn_in": arr(w_ffn_in)[0], "w_ffn_out": arr(w_ffn_out)[0],
        "g_ple": arr(g_ple)[0], "w_ple_gate": arr(w_ple_gate)[0], "w_ple_proj": arr(w_ple_proj)[0],
        "g_final": arr(g_final), "rope": rope_table(), "c": constant_table(), "b_c": attention_table(), "s_c": sample_table(),
    }
    nc = bacc.Bacc("TRN2", target_bir_lowering=False, num_devices=1)
    t = Tensors()
    for name, a in ins.items():
        t.__dict__[name] = nc.dram_tensor(name, a.shape, mybir.dt.from_np(a.dtype), kind="ExternalInput").ap()
    for name, shape in SCRATCH.items():
        t.__dict__[name] = nc.dram_tensor(name, shape, F32, kind="Internal").ap()
    for name, shape in OUTPUTS.items():
        t.__dict__[name] = nc.dram_tensor(name, shape, F32, kind="ExternalOutput").ap()
    build(nc, t)
    r = run_bass_kernel_spmd(nc, [{n: np.ascontiguousarray(a) for n, a in ins.items()}], core_ids=[0]).results[0]
    y, kiv = r["y"], r["kiv"]
    k, ki, v = kiv[:, 0:128], kiv[:, 128:192], kiv[:, 192:320]
    past, new = slice(0, SEQ), slice(SEQ, SEQ + NS)
    return (y[past].reshape(1, SEQ, D), y[new].reshape(NB, TS, D),
            k[past].reshape(1, 1, SEQ, KVH, HD), v[past].reshape(1, 1, SEQ, KVH, HD), ki[past].reshape(1, 1, SEQ, HD),
            r["retn_prompt"].reshape(1, 1, RH, RD, RD),
            k[new].reshape(1, NB, TS, KVH, HD), v[new].reshape(1, NB, TS, KVH, HD), ki[new].reshape(1, NB, TS, HD),
            r["retn_sample"].reshape(1, NB, RH, RD, RD))
```

```python
from contextlib import ExitStack

import numpy as np

import concourse.bass as bass
from concourse import mybir

F32 = mybir.dt.float32
I32 = mybir.dt.int32
U32 = mybir.dt.uint32
ALU = mybir.AluOpType
ACT = mybir.ActivationFunctionType
AX = mybir.AxisListType

P = 128
D = 1024
KD = D // P
SEQ = 2048
NB, TS = 8, 4
NS = NB * TS
PAST = 16384
PAGE = 128
NPAGES = PAST // PAGE
HD = 64
AH, KVH, GRP = 8, 2, 4
IH = 8
TOPK = 256
RH, RD = 4, 128
DFF = 2816
PLE = 256
NT = SEQ // P
ROWS = (NT + 1) * P
EPS, GN_EPS = 1e-6, 1e-5
BIG = 1.0e30

GROUPS = {
    "rq": [(1352, 512)], "rk": [(1864, 512)], "rv": [(2376, 512)], "rg": [(2888, 512)],
    "q": [(0, 512)], "qi": [(768, 512)], "kiv": [(512, 128), (1280, 64), (640, 128), (1344, 8)],
}
ORDER = ["rq", "rk", "rv", "rg", "q", "qi", "kiv"]
WIDTH = {g: sum(w for _, w in GROUPS[g]) for g in ORDER}
START = {g: sum(WIDTH[x] for x in ORDER[:n]) for n, g in enumerate(ORDER)}
WIN = sum(WIDTH.values())
KIV = WIDTH["kiv"]
TRW = 10 * P


def log_gamma():
    return np.log1p(-np.exp2(-5.0 - np.arange(RH, dtype=np.float64)))


def rope_table():
    pos = np.concatenate([np.arange(SEQ), np.tile(PAST + np.arange(TS), NB), np.zeros(ROWS - SEQ - NS, int)])
    cols = []
    for half in (32, 64):
        inv = 10000.0 ** (-np.arange(half, dtype=np.float64) / half)
        ang = pos.astype(np.float32)[:, None] * inv[None, :].astype(np.float32)
        cols += [np.cos(ang), np.sin(ang)]
    return np.concatenate(cols, 1).astype(np.float32)


C_ID, C_DEC, C_DECS, C_QD, C_KD, C_QDS, C_KDS, C_BLK = 0, 128, 640, 768, 772, 776, 780, 784
C_BLKR = C_BLK + NB * NS
C_W = C_BLKR + NB


def constant_table():
    c = np.zeros((P, C_W), np.float64)
    c[:, C_ID:C_ID + P] = np.eye(P)
    i = np.arange(P)
    s = RD ** -0.5
    for h, lg in enumerate(log_gamma()):
        c[:, C_DEC + h * P:C_DEC + (h + 1) * P] = np.where(i[None, :] >= i[:, None], s * np.exp(-lg * (i[:, None] + 1.0)), 0)
        r = np.arange(NS)
        same = (r[:, None] // TS == r[None, :] // TS) & (r[None, :] >= r[:, None])
        c[:NS, C_DECS + h * NS:C_DECS + (h + 1) * NS] = np.where(same, s * np.exp(-lg * (r[:, None] % TS + 1.0)), 0)
        c[:, C_QD + h] = np.exp(lg * (i + 1.0))
        c[:, C_KD + h] = s * np.exp(lg * (P - 1.0 - i))
        c[:NS, C_QDS + h] = np.exp(lg * (r % TS + 1.0))
        c[:NS, C_KDS + h] = s * np.exp(lg * (TS - 1.0 - r % TS))
    for b in range(NB):
        c[:, C_BLK + b * NS + b * TS:C_BLK + b * NS + (b + 1) * TS] = 1
        c[b * TS:(b + 1) * TS, C_BLKR + b] = 1
    return c.astype(np.float32)


class Signal:

    def __init__(self, sem, per, tiles=2):
        self.sem, self.per, self.tiles = sem, per, tiles

    def seed(self, eng):
        eng.sem_inc(self.sem, 2 * self.per)

    def at(self, n, k=None):
        i, u = n
        return i * (self.tiles * self.per) + (u + 2) * self.per + (self.per if k is None else k)


def bc(ap, axis, n):
    v = ap.unsqueeze(axis)
    shape = list(v.shape)
    shape[axis] = n
    return v.broadcast_to(shape)


def project_phase(nc, t):
    with ExitStack() as ctx:
        sb = lambda name, shape, dt=F32: ctx.enter_context(nc.sbuf_tensor("a_" + name, shape, dt))
        sem = lambda name: ctx.enter_context(nc.semaphore("a_" + name))
        signal = lambda name, per: Signal(sem(name), per)

        w = sb("w", [P, KD, WIN])
        c = sb("c", [P, C_W])
        ident = c[:, C_ID:C_ID + P]
        gmix = sb("gmix", [P, D])
        gretn = sb("gretn", [P, RH * RD])
        x = sb("x", [P, 2, D])
        rope = sb("rope", [P, 2, 192])
        ssq = sb("ssq", [P, 2])
        rstd = sb("rstd", [P, 2])
        mhalf = sb("mhalf", [P, RH])
        xn = sb("xn", [P, D])
        xT = sb("xT", [P, 2, KD, P])
        ta = sb("ta", [P, 512])
        tb = sb("tb", [P, 512])
        rq = sb("rq", [P, 512])
        rk = sb("rk", [P, 512])
        rkd = sb("rkd", [P, 512])
        rv = sb("rv", [P, 512])
        rg = sb("rg", [P, 512])
        erg = sb("erg", [P, 512])
        gate = sb("gate", [P, 512])
        q = sb("q", [P, 4, KVH, HD])
        qi = sb("qi", [P, 4, KVH, HD])
        kiv = sb("kiv", [P, 2, KIV])
        kid = sb("kid", [P, 2, HD])
        rqT = sb("rqT", [P, 512])
        rkT = sb("rkT", [P, 512])
        innT = sb("innT", [P, 512])
        o = sb("o", [P, 512])
        stats = sb("stats", [P, RH, 6])
        mv = sb("mv", [P, RH, 2])
        orstd = sb("orstd", [P, RH])
        ret = sb("ret", [P, 2, 512])
        state = sb("state", [P, RH * RD])
        trs = sb("trs", [P, 2, TRW])

        pxT = ctx.enter_context(nc.psum_tensor("a_pxT", [P, 2, 512], F32))
        pproj = ctx.enter_context(nc.psum_tensor("a_pproj", [P, 4, 512], F32))
        pr = ctx.enter_context(nc.psum_tensor("a_pr", [P, 2, 512], F32))

        consts = sem("consts")
        w_landed = [sem(f"w_{g}") for g in ORDER]
        x_landed = [sem(f"x_landed{u}") for u in range(2)]
        stored = [sem(f"stored{u}") for u in range(2)]
        state_out = sem("state_out")
        sstate_in = sem("sstate_in")
        ssq_done = signal("ssq_done", 1)
        xn_done = signal("xn_done", 1)
        xT_done = signal("xT_done", 2)
        xT_copied = signal("xT_copied", 2)
        proj = signal("proj", 7)
        roped = signal("roped", 5)
        taken = signal("taken", 2)
        mixed = signal("mixed", 8)
        moved = signal("moved", 5)
        folded = signal("folded", 3)
        rkd_done = signal("rkd_done", 1)
        gate_done = signal("gate_done", 1)
        var_done = signal("var_done", 1)
        orstd_done = signal("orstd_done", 1)
        ret_done = signal("ret_done", 1)
        blk_done = sem("blk_done")
        snew_done = sem("snew_done")
        snew_taken = sem("snew_taken")

        zeroed = sem("zeroed")

        wflat = w[:].rearrange("p k n -> p (k n)")
        sst = wflat[:, 0:4096].rearrange("p (h b e) -> p h b e", h=RH, b=NB)
        rqb = wflat[:, 4096:5120].rearrange("p (h b r) -> p h b r", h=RH, b=NB)
        rvb = wflat[0:NS, 5120:9216].rearrange("p (h b e) -> p h b e", h=RH, b=NB)

        block = ctx.enter_context(nc.Block())
        last = (NT // 2, 0)
        PAIRS = NT // 2

        def heads(ap, n=RH):
            return ap.rearrange("p (h e) -> p h e", h=n)

        @block.sync
        def _(sp):
            sp.sem_inc(stored[0], 48)
            sp.sem_inc(stored[1], 48)

            def load(row, i, u):
                sp.dma_start(x[:, u, :], t.x[bass.ds(row, P), :]).then_inc(x_landed[u], 16)
                sp.dma_start(rope[:, u, :], t.rope[bass.ds(row, P), :]).then_inc(x_landed[u], 16)

            def store(row, n):
                i, u = n
                sp.wait_ge(moved.sem, moved.at(n))
                sp.dma_start(t.tr[bass.ds(row, P), :], trs[:, u, :]).then_inc(stored[u], 16)
                sp.dma_start(t.kiv[bass.ds(row, P), :], kiv[:, u, :]).then_inc(stored[u], 16)
                sp.wait_ge(ret_done.sem, ret_done.at(n))
                sp.dma_start(t.cat[bass.ds(row, P), 512:D], ret[:, u, :]).then_inc(stored[u], 16)

            load(0, 0, 0)
            sp.dma_start(c[:], t.c).then_inc(consts, 16)
            sp.dma_start(gmix[:], t.g_mix.partition_broadcast(P)).then_inc(consts, 16)
            sp.dma_start(gretn[:], t.g_retn.partition_broadcast(P)).then_inc(consts, 16)
            for g, landed in zip(ORDER, w_landed):
                at = START[g]
                for src, width in GROUPS[g]:
                    sp.dma_start(w[:, :, at:at + width],
                                 t.w_in[:, src:src + width].rearrange("(k p) n -> p k n", p=P)).then_inc(landed, 16)
                    at += width
            with sp.Fori(0, PAIRS) as i:
                rows = [sp.snap((i * 2 + v) * P) for v in range(3)]
                for u in range(2):
                    sp.wait_ge(xn_done.sem, xn_done.at((i, u - 1)))
                    sp.wait_ge(roped.sem, roped.at((i, u - 1)))
                    load(rows[u + 1], i, (u + 1) % 2)
                    store(rows[u], (i, u))
            for h in range(RH):
                if h == 0:
                    sp.wait_ge(proj.sem, proj.at(last))
                sp.dma_start(sst[:, h], t.state_retn[:, h].rearrange("b d e -> d b e")).then_inc(sstate_in, 16)
            store(NT * P, last)
            sp.wait_ge(folded.sem, folded.at((PAIRS - 1, 1)))
            sp.dma_start(t.retn_prompt.rearrange("h d e -> d h e"), heads(state[:])).then_inc(state_out, 16)
            for h in range(RH):
                sp.wait_ge(snew_taken, 2 * h + 2)
                sp.dma_start(t.retn_sample[:, h].rearrange("b d e -> d b e"), sst[:, h]).then_inc(state_out, 16)
            sp.wait_ge(state_out, 16 * (1 + RH))
            for u, tiles in ((0, PAIRS + 1), (1, PAIRS)):
                sp.wait_ge(stored[u], 48 * (tiles + 1))

        @block.tensor
        def _(pe):
            for s in (xT_done, proj, mixed):
                s.seed(pe)
            pe.wait_ge(consts, 48)

            def transpose_x(n):
                i, u = n
                pe.wait_ge(xn_done.sem, xn_done.at(n))
                pe.wait_ge(xT_copied.sem, xT_copied.at((i, u - 1)))
                for half in range(2):
                    for k in range(4):
                        at = (half * 4 + k) * P
                        m = pe.transpose(pxT[:, half, k * P:(k + 1) * P], xn[:, at:at + P], ident)
                    m.then_inc(xT_done.sem, 1)

            def project(n, g):
                i, u = n
                s = ORDER.index(g)
                pe.wait_ge(w_landed[s], 16 * len(GROUPS[g]))
                if g == "rq":
                    pe.wait_ge(xT_copied.sem, xT_copied.at(n))
                before = {"rq": (roped, (i, u - 1), 3), "rk": (roped, (i, u - 1), 4), "rv": (roped, (i, u - 1), 5),
                          "rg": (taken, (i, u - 1), 2), "q": (roped, n, 1), "qi": (roped, n, 2), "kiv": (taken, n, 1)}[g]
                pe.wait_ge(before[0].sem, before[0].at(before[1], before[2]))
                for k in range(KD):
                    m = pe.matmul(pproj[:, s % 4, 0:WIDTH[g]], xT[:, u % 2, k, :], w[:, k, START[g]:START[g] + WIDTH[g]],
                                  start=(k == 0), stop=(k == KD - 1))
                m.then_inc(proj.sem, 1)

            def body(n, m_rows, sample=False):
                i, u = n
                R = m_rows
                for g in ("rq", "rk", "rv", "rg", "q"):
                    project(n, g)
                for j, (src, before) in enumerate(((rq, 4), (rk, 5))):
                    pe.wait_ge(roped.sem, roped.at(n, j + 1))
                    pe.wait_ge(moved.sem, moved.at((i, u - 1), before))
                    for h in range(RH):
                        m = pe.transpose(pr[:, j, h * P:h * P + R], src[0:R, h * P:(h + 1) * P], ident[0:R, 0:R])
                    m.then_inc(mixed.sem, 1)
                project(n, "qi")
                pe.wait_ge(moved.sem, moved.at(n, 2))
                for h in range(RH):
                    m = pe.matmul(pr[0:R, 0, h * R:(h + 1) * R], rkT[:, h * P:h * P + R], rqT[:, h * P:h * P + R],
                                  start=True, stop=True)
                m.then_inc(mixed.sem, 1)
                project(n, "kiv")
                if not sample:
                    transpose_x((i, u + 1))
                pe.wait_ge(folded.sem, folded.at(n, 1))
                pe.wait_ge(taken.sem, taken.at(n, 1))
                pe.wait_ge(folded.sem, folded.at((i, u - 1), 3))
                if sample:
                    pe.wait_ge(blk_done, 2)
                    pe.wait_ge(sstate_in, 16 * RH)
                for h in range(RH):
                    out = pr[0:R, 1, h * P:(h + 1) * P]
                    pe.matmul(out, innT[0:R, h * R:(h + 1) * R], rv[0:R, h * P:(h + 1) * P], start=True, stop=False)
                    if sample:
                        for b in range(NB):
                            m = pe.matmul(out, rqb[:, h, b, :], sst[:, h, b, :], start=False, stop=(b == NB - 1))
                    else:
                        m = pe.matmul(out, rqT[:, h * P:(h + 1) * P], state[:, h * P:(h + 1) * P], start=False, stop=True)
                m.then_inc(mixed.sem, 1)
                pe.wait_ge(rkd_done.sem, rkd_done.at(n))
                if sample:
                    m = None
                    for h in range(RH):
                        for half in range(2):
                            pos = h * 2 + half
                            pe.wait_ge(snew_taken, pos - 1) if pos > 1 else None
                            m = pe.matmul(pxT[:, half, :], rkd[0:NS, h * P:(h + 1) * P],
                                          rvb[:, h, half * 4:half * 4 + 4, :].rearrange("p b e -> p (b e)"),
                                          start=True, stop=True)
                            if pos < 2 * RH - 1:
                                m.then_inc(snew_done, 1)
                    m.then_inc(snew_done, 1)
                    pe.transpose(pr[0:1, 0, 0:1], ident[0:1, 0:1], ident[0:1, 0:1]).then_inc(mixed.sem, 1)
                else:
                    for h in range(RH):
                        m = pe.matmul(pr[:, 0, h * P:(h + 1) * P], rkd[:, h * P:(h + 1) * P], rv[:, h * P:(h + 1) * P],
                                      start=True, stop=True)
                    m.then_inc(mixed.sem, 1)
                pe.wait_ge(roped.sem, roped.at(n, 3))
                pe.wait_ge(folded.sem, folded.at(n, 2))
                for j in range(4):
                    m = pe.transpose(pr[:, 1, j * P:j * P + R], q[0:R, j].rearrange("p a d -> p (a d)"), ident[0:R, 0:R])
                m.then_inc(mixed.sem, 1)
                pe.wait_ge(roped.sem, roped.at(n, 4))
                pe.wait_ge(folded.sem, folded.at(n, 3))
                for j in range(4):
                    m = pe.transpose(pr[:, 0, j * P:j * P + R], qi[0:R, j].rearrange("p a d -> p (a d)"), ident[0:R, 0:R])
                m.then_inc(mixed.sem, 1)
                pe.wait_ge(roped.sem, roped.at(n, 5))
                pe.wait_ge(moved.sem, moved.at(n, 3))
                pe.transpose(pr[:, 1, 0:R], kiv[0:R, u % 2, 0:P], ident[0:R, 0:R])
                pe.transpose(pr[:, 1, P:P + R], kid[0:R].rearrange("p a d -> p (a d)"), ident[0:R, 0:R]).then_inc(mixed.sem, 1)

            transpose_x((0, 0))
            with pe.Fori(0, PAIRS) as i:
                body((i, 0), P)
                body((i, 1), P)
            body(last, NS, sample=True)

        @block.scalar
        def _(act):
            for s in (ssq_done, xT_copied, taken, moved):
                s.seed(act)

            def square(n):
                i, u = n
                act.wait_ge(x_landed[u % 2], i * 32 + 32 * (u // 2 + 1))
                act.wait_ge(xn_done.sem, xn_done.at((i, u - 1)))
                act.activation(xn[:], x[:, u % 2, :], ACT.Square, accum_out=ssq[:, u % 2:u % 2 + 1])
                act.drain()
                act.activation(ssq[:, u % 2:u % 2 + 1], ssq[:, u % 2:u % 2 + 1], ACT.Copy, scale=1.0 / D, bias=EPS).then_inc(ssq_done.sem, 1)

            def copy_xT(n):
                i, u = n
                act.wait_ge(proj.sem, proj.at((i, u - 2)))
                for half in range(2):
                    act.wait_ge(xT_done.sem, xT_done.at(n, half + 1))
                    act.activation(xT[:, u % 2, half * 4:half * 4 + 4, :].rearrange("p k c -> p (k c)"), pxT[:, half, :],
                                   ACT.Copy).then_inc(xT_copied.sem, 1)

            def body(n, R, sample=False):
                i, u = n
                s = u % 2
                act.wait_ge(proj.sem, proj.at(n, 3))
                act.wait_ge(mixed.sem, mixed.at((i, u - 1), 5))
                act.activation(rv[:], pproj[:, 2, :], ACT.Copy).then_inc(taken.sem, 1)
                act.wait_ge(proj.sem, proj.at(n, 4))
                act.wait_ge(gate_done.sem, gate_done.at((i, u - 1)))
                act.activation(erg[:], pproj[:, 3, :], ACT.Sigmoid)
                act.activation(rg[:], pproj[:, 3, :], ACT.Copy)
                act.drain().then_inc(taken.sem, 1)
                for j, dst in enumerate((rqT, rkT)):
                    act.wait_ge(mixed.sem, mixed.at(n, j + 1))
                    act.activation(heads(dst[:])[:, :, 0:R], heads(pr[:, j, :])[:, :, 0:R], ACT.Copy).then_inc(moved.sem, 1)
                if not sample:
                    act.wait_ge(xT_done.sem, xT_done.at(n))
                    square((i, u + 1))
                    copy_xT((i, u + 1))
                act.wait_ge(stored[s], (u // 2 + 1) * 48 + i * 48)
                for j, (bank, width, at) in enumerate(((1, 4, 0), (0, 4, 4), (1, 2, 8))):
                    act.wait_ge(mixed.sem, mixed.at(n, 6 + j))
                    act.activation(heads(trs[:, s, at * P:(at + width) * P], width)[:, :, 0:R],
                                   heads(pr[:, bank, 0:width * P], width)[:, :, 0:R], ACT.Copy).then_inc(moved.sem, 1)

            act.wait_ge(zeroed, 2)
            square((0, 0))
            copy_xT((0, 0))
            with act.Fori(0, PAIRS) as i:
                body((i, 0), P)
                body((i, 1), P)
            body(last, NS, sample=True)

        @block.vector
        def _(dve):
            for s in (roped, folded, var_done, ret_done):
                s.seed(dve)
            dve.memset(state[:], 0.0).then_inc(zeroed, 1)
            dve.memset(trs[:].rearrange("p s n -> p (s n)"), 0.0).then_inc(zeroed, 1)
            dve.wait_ge(zeroed, 2)
            dve.wait_ge(consts, 48)

            def rotate(src, s, half, n, outs):
                base = 0 if half == 32 else 64
                width = 2 * n * half
                view = lambda a: a.rearrange("p (m d) -> p m d", d=half)
                cos = bc(rope[:, s, base:base + half], 1, 2 * n)
                sin = bc(rope[:, s, base + half:base + 2 * half], 1, 2 * n)
                dve.tensor_tensor(view(ta[:, 0:width]), view(src), cos, ALU.mult)
                m = dve.tensor_tensor(view(tb[:, 0:width]), view(src), sin, ALU.mult)
                dve.drain()
                a = ta[:, 0:width].rearrange("p (n s d) -> p n s d", s=2, d=half)
                b = tb[:, 0:width].rearrange("p (n s d) -> p n s d", s=2, d=half)
                return a, b

            def rotate_heads(src, s, dst, order):
                a, b = rotate(src, s, 32, 8, None)
                re = lambda v, s_: v[:, :, s_, :].rearrange("p (v j) d -> p v j d", v=KVH)
                out = lambda s_: dst[:, :, :, s_ * 32:s_ * 32 + 32].rearrange("p j v d -> p v j d")
                dve.tensor_tensor(out(0), re(a, 0), re(b, 1), ALU.subtract)
                return dve.tensor_tensor(out(1), re(a, 1), re(b, 0), ALU.add)

            def rotate_plain(src, s, half, n, dst):
                a, b = rotate(src, s, half, n, None)
                o_ = dst.rearrange("p (n s d) -> p n s d", s=2, d=half)
                dve.tensor_tensor(o_[:, :, 0, :], a[:, :, 0, :], b[:, :, 1, :], ALU.subtract)
                return dve.tensor_tensor(o_[:, :, 1, :], a[:, :, 1, :], b[:, :, 0, :], ALU.add)

            def body(n, R, sample=False):
                i, u = n
                s = u % 2
                before = (i, u - 1)
                decay = c[0:R, C_DECS:C_DECS + RH * NS] if sample else c[:, C_DEC:C_DEC + RH * P]
                qdec = c[:, C_QDS:C_QDS + RH] if sample else c[:, C_QD:C_QD + RH]
                for j, (g, dst) in enumerate((("rq", rq), ("rk", rk))):
                    dve.wait_ge(proj.sem, proj.at(n, ORDER.index(g) + 1))
                    dve.wait_ge(mixed.sem, mixed.at(before, j + 1))
                    if g == "rk":
                        dve.wait_ge(rkd_done.sem, rkd_done.at(before))
                    if g == "rq":
                        dve.wait_ge(x_landed[s], i * 32 + 32 * (u // 2 + 1))
                    rotate_plain(pproj[:, j, :], s, 64, RH, dst[:]).then_inc(roped.sem, 1)
                    dve.drain()
                for j, (g, dst) in enumerate((("q", q), ("qi", qi))):
                    dve.wait_ge(proj.sem, proj.at(n, ORDER.index(g) + 1))
                    dve.wait_ge(mixed.sem, mixed.at(before, 6 + j))
                    rotate_heads(pproj[:, j, :], s, dst[:], None).then_inc(roped.sem, 1)
                    dve.drain()
                dve.wait_ge(mixed.sem, mixed.at(n, 3))
                dve.tensor_tensor(innT[0:R, 0:RH * R], pr[0:R, 0, 0:RH * R], decay, ALU.mult).then_inc(folded.sem, 1)
                dve.wait_ge(proj.sem, proj.at(n, 7))
                dve.wait_ge(stored[s], (u // 2 + 1) * 48 + i * 48)
                dve.wait_ge(mixed.sem, mixed.at(before, 8))
                kv = kiv[:, s, :]
                rotate_plain(pproj[:, 2, 0:192], s, 32, 3, kv[:, 0:192])
                dve.tensor_copy(kv[:, 192:KIV], pproj[:, 2, 192:KIV])
                dve.drain()
                dve.tensor_copy(kid[:], bc(kv[:, P:P + HD], 1, 2)).then_inc(roped.sem, 1)
                if sample:
                    r4 = heads(rqT[:])[:, :, 0:NS].unsqueeze(2).broadcast_to([P, RH, NB, NS])
                    blk = c[:, C_BLK:C_BLK + NB * NS].rearrange("p (b r) -> p b r", b=NB)
                    dve.wait_ge(moved.sem, moved.at(n, 2))
                    dve.wait_ge(proj.sem, proj.at(n))
                    dve.tensor_tensor(rqb, r4, blk.unsqueeze(1).broadcast_to([P, RH, NB, NS]), ALU.mult).then_inc(blk_done, 1)
                    dve.wait_ge(taken.sem, taken.at(n, 1))
                    for b in range(NB):
                        m = dve.tensor_scalar(rvb[:, :, b, :], heads(rv[0:NS, :]), c[0:NS, C_BLKR + b:C_BLKR + b + 1], None, ALU.mult)
                    m.then_inc(blk_done, 1)
                dve.wait_ge(mixed.sem, mixed.at(n, 4))
                dve.tensor_tensor(heads(o[0:R, :]), heads(pr[0:R, 1, :]), bc(qdec[0:R], 2, RD), ALU.mult).then_inc(folded.sem, 1)
                if sample:
                    for h in range(RH):
                        for half in range(2):
                            dve.wait_ge(snew_done, 2 * h + half + 1)
                            st = sst[:, h, half * 4:half * 4 + 4, :].rearrange("p b e -> p (b e)")
                            dve.scalar_tensor_tensor(st, st, float(np.exp(log_gamma()[h] * TS)), pxT[:, half, :],
                                                     ALU.mult, ALU.add).then_inc(snew_taken, 1)
                    dve.wait_ge(mixed.sem, mixed.at(n, 5))
                    dve.memset(stats[0:1, 0, 0:1], 0.0).then_inc(folded.sem, 1)
                    dve.drain()
                else:
                    dve.wait_ge(mixed.sem, mixed.at(n, 5))
                    for h in range(RH):
                        st = state[:, h * P:(h + 1) * P]
                        m = dve.scalar_tensor_tensor(st, st, float(np.exp(log_gamma()[h] * P)), pr[:, 0, h * P:(h + 1) * P],
                                                     ALU.mult, ALU.add)
                    m.then_inc(folded.sem, 1)
                    dve.drain()
                for h in range(RH):
                    dve.bn_stats(stats[0:R, h, :], o[0:R, h * P:(h + 1) * P])
                dve.drain()
                for h in range(RH):
                    dve.bn_aggr(mv[0:R, h, :], stats[0:R, h, :])
                dve.drain()
                dve.tensor_scalar(mv[0:R, :, 1], mv[0:R, :, 1], GN_EPS, None, ALU.add).then_inc(var_done.sem, 1)
                dve.wait_ge(orstd_done.sem, orstd_done.at(n))
                dve.wait_ge(var_done.sem, var_done.at(n))
                dve.wait_ge(gate_done.sem, gate_done.at(n))
                for h in range(RH):
                    oh = o[0:R, h * P:(h + 1) * P]
                    dve.tensor_scalar(oh, oh, mv[0:R, h, 0:1], orstd[0:R, h:h + 1], ALU.subtract, ALU.mult)
                dve.drain()
                dve.tensor_tensor(ret[0:R, s, :], o[0:R, :], gate[0:R, :], ALU.mult).then_inc(ret_done.sem, 1)

            dve.memset(ret[:].rearrange("p s n -> p (s n)"), 0.0)
            dve.drain()
            with dve.Fori(0, PAIRS) as i:
                body((i, 0), P)
                body((i, 1), P)
            body(last, NS, sample=True)

        @block.gpsimd
        def _(pool):
            for s in (xn_done, rkd_done, gate_done, orstd_done):
                s.seed(pool)
            pool.memset(mhalf[:], -0.5)
            pool.wait_ge(consts, 48)
            pool.drain()

            def normalise(n):
                i, u = n
                s = u % 2
                pool.wait_ge(ssq_done.sem, ssq_done.at(n))
                pool.tensor_tensor(rstd[:, s:s + 1], ssq[:, s:s + 1], mhalf[:, 0:1], ALU.pow)
                pool.drain()
                pool.tensor_scalar(xn[:], x[:, s, :], rstd[:, s:s + 1], None, ALU.mult)
                pool.drain()
                pool.tensor_tensor(xn[:], xn[:], gmix[:], ALU.mult).then_inc(xn_done.sem, 1)

            def body(n, R, sample=False):
                i, u = n
                before = (i, u - 1)
                kdec = c[:, C_KDS:C_KDS + RH] if sample else c[:, C_KD:C_KD + RH]
                pool.wait_ge(roped.sem, roped.at(n, 2))
                pool.wait_ge(mixed.sem, mixed.at(before, 5))
                pool.tensor_tensor(heads(rkd[0:R, :]), heads(rk[0:R, :]), bc(kdec[0:R], 2, RD), ALU.mult).then_inc(rkd_done.sem, 1)
                if not sample:
                    normalise((i, u + 1))
                pool.wait_ge(taken.sem, taken.at(n, 2))
                pool.wait_ge(ret_done.sem, ret_done.at(before))
                pool.tensor_tensor(gate[:], rg[:], erg[:], ALU.mult)
                pool.drain()
                pool.tensor_tensor(gate[:], gate[:], gretn[:], ALU.mult).then_inc(gate_done.sem, 1)
                pool.wait_ge(var_done.sem, var_done.at(n))
                pool.wait_ge(ret_done.sem, ret_done.at(before))
                pool.tensor_tensor(orstd[0:R], mv[0:R, :, 1], mhalf[0:R], ALU.pow).then_inc(orstd_done.sem, 1)

            normalise((0, 0))
            with pool.Fori(0, PAIRS) as i:
                body((i, 0), P)
                body((i, 1), P)
            body(last, NS, sample=True)


NSTEP = 24
B_ID, B_CAUSAL, B_HALF, B_W = 0, 128, 256, 256 + NSTEP


def attention_table():
    c = np.zeros((P, B_W), np.float32)
    i = np.arange(P)
    c[:, B_ID:B_ID + P] = np.eye(P)
    c[:, B_CAUSAL:B_CAUSAL + P] = np.where(i[None, :] > i[:, None], -BIG, 0)
    c[:, B_HALF:B_HALF + NSTEP] = 2.0 ** -(np.arange(NSTEP) + 1.0)
    return c


def prompt_phase(nc, t):
    with ExitStack() as ctx:
        sb = lambda name, shape, dt=F32: ctx.enter_context(nc.sbuf_tensor("b_" + name, shape, dt))
        sem = lambda name: ctx.enter_context(nc.semaphore("b_" + name))

        c = sb("consts", [P, B_W])
        ident = c[:, B_ID:B_ID + P]
        kT = sb("kT", [P, NT * P])
        kiT = sb("kiT", [P, NT * P])
        v = sb("v", [P, NT, P])
        wi = sb("wi", [P, NT, IH])
        qT = sb("qT", [P, 2, AH, P])
        qiT = sb("qiT", [P, 2, IH, P])
        relu = sb("relu", [P, 4, 512])
        score = sb("score", [P, 3, SEQ])
        mask = sb("mask", [P, 2, SEQ])
        above = sb("above", [P, SEQ])
        band = sb("band", [P, SEQ])
        rank = sb("rank", [P, SEQ])
        lim = sb("lim", [P, 8])
        step = sb("step", [P, NSTEP])
        mid = sb("mid", [P, NSTEP])
        cnt = sb("cnt", [P, NSTEP])
        logit = sb("logit", [P, 2, SEQ])
        mx = sb("mx", [P, 2, 4])
        nb = sb("nb", [P, 4])
        rs = sb("rs", [P, 2, AH])
        rrs = sb("rrs", [P, AH])
        pT = sb("pT", [P, 2, SEQ])
        att = sb("att", [P, 2, AH, HD])
        pi = ctx.enter_context(nc.psum_tensor("b_pi", [P, 2, 512], F32))
        pl = ctx.enter_context(nc.psum_tensor("b_pl", [P, 3, 512], F32))
        pt = ctx.enter_context(nc.psum_tensor("b_pt", [P, 2, 512], F32))
        po = ctx.enter_context(nc.psum_tensor("b_po", [P, 512], F32))

        loaded = sem("loaded")
        q_in = [sem(f"q_in{s}") for s in range(2)]
        qi_in = [sem(f"qi_in{s}") for s in range(2)]
        att_out = [sem(f"att_out{s}") for s in range(2)]
        scored = sem("scored")
        relued = sem("relued")
        weighed = sem("weighed")
        logits = sem("logits")
        masked = sem("masked")
        max_done = sem("max_done")
        exp_done = sem("exp_done")
        turned = sem("turned")
        pT_done = sem("pT_done")
        pv = sem("pv")
        att_done = sem("att_done")
        zeroed = sem("zeroed")
        ranked = sem("ranked")

        def width(T):
            return (TILES[T] + 1) * P

        def chunks(T):
            return [(a, min(512, width(T) - a)) for a in range(0, width(T), 512)]

        FIRST = TOPK // P
        TILES = [*range(FIRST), *range(FIRST, NT, 2), *reversed(range(FIRST + 1, NT, 2))]
        ibase = {T: IH * sum(len(chunks(x)) for x in range(FIRST, T)) for T in range(FIRST, NT + 1)}
        lbase = {T: AH * sum(len(chunks(x)) for x in range(T)) for T in range(NT + 1)}

        def icount(T, hh, k):
            return ibase[T] + hh * len(chunks(T)) + k + 1

        def lcount(T, hh, k):
            return lbase[T] + hh * len(chunks(T)) + k + 1

        def head(hh):
            return hh // 2, hh % 2, hh // 2 + 4 * (hh % 2)

        steps = [(T, hh) for T in range(FIRST - 2, NT) for hh in range(AH)]
        block = ctx.enter_context(nc.Block())

        @block.sync
        def _(sp):
            tr = t.tr[0:SEQ, :].rearrange("(n p) c -> p n c", p=P)
            kv = t.kiv[0:SEQ, :].rearrange("(n p) c -> p n c", p=P)

            def load_q(T):
                if T >= 2:
                    sp.wait_ge(logits, lcount(T - 2, AH - 1, len(chunks(T - 2)) - 1))
                for half in range(2):
                    rows = slice(half * HD, half * HD + HD)
                    sp.dma_start(qT[rows, T % 2, half::2, :], tr[rows, TILES[T], 0:4 * P].rearrange("p (j c) -> p j c", j=4)).then_inc(q_in[T % 2], 16)

            def load_qi(T):
                if T >= FIRST + 2:
                    sp.wait_ge(scored, icount(T - 2, IH - 1, len(chunks(T - 2)) - 1))
                for half in range(2):
                    rows = slice(half * HD, half * HD + HD)
                    sp.dma_start(qiT[rows, T % 2, half::2, :], tr[rows, TILES[T], 4 * P:8 * P].rearrange("p (j c) -> p j c", j=4)).then_inc(qi_in[T % 2], 16)

            load_qi(FIRST)
            sp.dma_start(kiT[:].rearrange("p (n c) -> p n c", n=NT), tr[:, :, 9 * P:10 * P]).then_inc(loaded, 16)
            sp.dma_start(wi[:], kv[:, :, 320:328]).then_inc(loaded, 16)
            load_q(0)
            sp.dma_start(kT[:].rearrange("p (n c) -> p n c", n=NT), tr[:, :, 8 * P:9 * P]).then_inc(loaded, 16)
            sp.dma_start(c[:], t.b_c).then_inc(loaded, 16)
            sp.dma_start(v[:], kv[:, :, 192:320]).then_inc(loaded, 16)
            load_q(1)
            load_qi(FIRST + 1)
            for T in range(NT):
                if T + 4 < NT:
                    load_qi(T + 4)
                if T + 2 < NT:
                    load_q(T + 2)
                sp.wait_ge(att_done, T + 1)
                sp.dma_start(t.cat[width(T) - P:width(T), 0:512], att[:, T % 2].rearrange("p h d -> p (h d)")).then_inc(att_out[T % 2], 16)
            for s in range(2):
                sp.wait_ge(att_out[s], 16 * (NT // 2))

        @block.tensor
        def _(pe):
            pe.wait_ge(loaded, 80)
            pe.wait_ge(zeroed, 1)

            def index(T, hh, k):
                a, w_ = chunks(T)[k]
                n = icount(T, hh, k)
                if k == 0:
                    pe.wait_ge(qi_in[T % 2], 32 * ((T - FIRST) // 2 + 1))
                if n > 2:
                    pe.wait_ge(relued, n - 2)
                pe.matmul(pi[:, n % 2, 0:w_], qiT[:, T % 2, hh, :], kiT[:, a:a + w_],
                          start=True, stop=True).then_inc(scored, 1)

            def logit_products(T, hh, k):
                a, w_ = chunks(T)[k]
                n = lcount(T, hh, k)
                if k == 0:
                    pe.wait_ge(q_in[T % 2], 32 * (T // 2 + 1))
                if n > 3:
                    pe.wait_ge(masked, n - 3)
                pe.matmul(pl[:, n % 3, 0:w_], qT[:, T % 2, hh, :], kT[:, a:a + w_],
                          start=True, stop=True).then_inc(logits, 1)

            def values(T, hh):
                _, half, hd = head(hh)
                g = T * AH + hh
                pe.wait_ge(exp_done, g + 1)
                for k, (a, w_) in enumerate(chunks(T)):
                    n = lcount(T, hh, k)
                    if n > 2:
                        pe.wait_ge(pT_done, n - 2)
                    for b in range(0, w_, P):
                        m = pe.transpose(pt[:, n % 2, b:b + P], logit[:, g % 2, a + b:a + b + P], ident)
                    m.then_inc(turned, 1)
                if hh == 0 and T >= 1:
                    pe.wait_ge(att_done, T)
                pe.wait_ge(pT_done, lcount(T, hh, len(chunks(T)) - 1))
                for b in range(TILES[T] + 1):
                    m = pe.matmul(po[:, hd * HD:(hd + 1) * HD], pT[:, g % 2, b * P:(b + 1) * P],
                                  v[:, b, half * HD:half * HD + HD], start=(b == 0), stop=(b == TILES[T]))
                m.then_inc(pv, 1)

            for T, hh in steps:
                for k in range(4):
                    if T >= 0 and k < len(chunks(T)):
                        logit_products(T, hh, k)
                    if T + 2 < NT and k < len(chunks(T + 2)):
                        index(T + 2, hh, k)
                if T * AH + hh >= 1:
                    values((T * AH + hh - 1) // AH, (hh - 1) % AH)
            values(NT - 1, AH - 1)

        @block.scalar
        def _(act):
            def relu_chunks(T, hh):
                for k, (a, w_) in enumerate(chunks(T)):
                    n = icount(T, hh, k)
                    act.wait_ge(scored, n)
                    if n > 4:
                        act.wait_ge(weighed, n - 4)
                    act.activation(relu[:, n % 4, 0:w_], pi[:, n % 2, 0:w_], ACT.Relu).then_inc(relued, 1)

            def copy_probs(T, hh):
                g = T * AH + hh
                if g >= 2:
                    act.wait_ge(pv, g - 1)
                for k, (a, w_) in enumerate(chunks(T)):
                    n = lcount(T, hh, k)
                    act.wait_ge(turned, n)
                    act.activation(pT[:, g % 2, a:a + w_], pt[:, n % 2, 0:w_], ACT.Copy).then_inc(pT_done, 1)

            def exponential(T, hh):
                g = T * AH + hh
                hd = head(hh)[2]
                act.wait_ge(max_done, g + 1)
                lg = logit[:, g % 2, 0:width(T)]
                act.activation(lg, lg, ACT.Exp, bias=nb[:, g % 4:g % 4 + 1], scale=HD ** -0.5,
                               accum_out=rs[:, T % 2, hd:hd + 1]).then_inc(exp_done, 1)

            for T, hh in steps:
                if T + 2 < NT:
                    relu_chunks(T + 2, hh)
                if T * AH + hh >= 1:
                    copy_probs((T * AH + hh - 1) // AH, (hh - 1) % AH)
                if T >= 0:
                    exponential(T, hh)
            copy_probs(NT - 1, AH - 1)

        @block.vector
        def _(dve):
            for half in range(2):
                rows = slice((1 - half) * HD, (1 - half) * HD + HD)
                dve.memset(qT[rows, :, half::2, :], 0.0)
                dve.memset(qiT[rows, :, half::2, :], 0.0)
            dve.memset(mask[:].rearrange("p s n -> p (s n)"), 0.0)
            dve.drain().then_inc(zeroed, 1)
            dve.wait_ge(loaded, 80)

            lo, hi, need, took = (lim[:, j:j + 1] for j in range(4))

            def open_range(T):
                dve.wait_ge(weighed, icount(T, IH - 1, len(chunks(T)) - 1))
                s = score[:, T % 3, 0:width(T)]
                diag = score[:, T % 3, width(T) - P:width(T)]
                dve.tensor_reduce(lo, s, AX.X, ALU.min)
                dve.drain()
                dve.tensor_tensor(diag, diag, c[:, B_CAUSAL:B_CAUSAL + P], ALU.add)
                dve.drain()
                dve.tensor_reduce(hi, s, AX.X, ALU.max)
                dve.drain()
                dve.tensor_tensor(took, hi, lo, ALU.subtract)
                dve.drain()
                dve.tensor_scalar(step[:], c[:, B_HALF:B_HALF + NSTEP], took, None, ALU.mult)
                dve.drain()
                dve.tensor_tensor(mid[:, 0:1], lo, step[:, 0:1], ALU.add)
                dve.drain()

            def halve(T, k):
                s = score[:, T % 3, 0:width(T)]
                dve.tensor_scalar(above[:, 0:width(T)], s, mid[:, k:k + 1], None, ALU.is_ge, ALU.add,
                                  accum_out=cnt[:, k:k + 1])
                dve.drain()
                if k + 1 < NSTEP:
                    dve.tensor_scalar(took, cnt[:, k:k + 1], TOPK - 0.5, step[:, k:k + 1], ALU.is_ge, ALU.mult)
                    dve.drain()
                    dve.scalar_tensor_tensor(mid[:, k + 1:k + 2], mid[:, k:k + 1], step[:, k + 1:k + 2], took, ALU.subtract, ALU.add)
                    dve.drain()

            def close_range(T, part):
                n = width(T)
                s = score[:, T % 3, 0:n]
                if part == 0:
                    dve.tensor_scalar(cnt[:], cnt[:], TOPK - 0.5, BIG, ALU.is_ge, ALU.mult)
                    dve.drain()
                    dve.tensor_tensor(step[:], mid[:], cnt[:], ALU.add)
                    dve.scalar_tensor_tensor(mid[:], cnt[:], -BIG, mid[:], ALU.add, ALU.add)
                    dve.drain()
                    dve.tensor_reduce(took, step[:], AX.X, ALU.min)
                    dve.drain()
                    dve.tensor_tensor(hi, hi, took, ALU.min)
                    dve.tensor_reduce(need, mid[:], AX.X, ALU.max)
                    dve.drain()
                    dve.tensor_tensor(lo, lo, need, ALU.max)
                    dve.drain()
                    dve.tensor_scalar(above[:, 0:n], s, hi, None, ALU.is_gt, ALU.add, accum_out=need)
                    dve.drain()
                    dve.tensor_scalar(need, need, -1.0, float(TOPK), ALU.mult, ALU.add)
                elif part == 1:
                    dve.scalar_tensor_tensor(band[:, 0:n], s, lo, above[:, 0:n], ALU.is_ge, ALU.subtract)
                elif part == 2:
                    dve.tensor_tensor_scan(rank[:, 0:n], band[:, 0:n], band[:, 0:n], 0.0, ALU.add, ALU.max)
                elif part == 3:
                    dve.scalar_tensor_tensor(band[:, 0:n], rank[:, 0:n], need, band[:, 0:n], ALU.is_le, ALU.mult)
                elif part == 4:
                    dve.tensor_tensor(band[:, 0:n], band[:, 0:n], above[:, 0:n], ALU.add)
                elif part == 5:
                    dve.tensor_scalar(mask[:, T % 2, 0:n], band[:, 0:n], -1.0, BIG, ALU.add, ALU.mult)
                dve.drain()

            def threshold(T, x):
                if x == 0:
                    open_range(T)
                elif x <= NSTEP:
                    halve(T, x - 1)
                elif x <= NSTEP + 6:
                    close_range(T, x - 1 - NSTEP)

            def mask_logits(T, hh, k):
                g = T * AH + hh
                if k == 0 and g >= 2:
                    dve.wait_ge(turned, lcount((g - 2) // AH, (g - 2) % AH, len(chunks((g - 2) // AH)) - 1))
                a, w_ = chunks(T)[k]
                n = lcount(T, hh, k)
                dve.wait_ge(logits, n)
                dve.tensor_tensor_reduce(logit[:, g % 2, a:a + w_], pl[:, n % 3, 0:w_], mask[:, T % 2, a:a + w_],
                                         1.0, -3.0e38, ALU.add, ALU.max, accum_out=mx[:, g % 2, k:k + 1]).then_inc(masked, 1)
                if k + 1 < len(chunks(T)):
                    return
                dve.drain()
                m = mx[:, g % 2, 0:1]
                if len(chunks(T)) > 1:
                    dve.tensor_reduce(m, mx[:, g % 2, 0:len(chunks(T))], AX.X, ALU.max)
                    dve.drain()
                if g >= 4:
                    dve.wait_ge(exp_done, g - 3)
                dve.tensor_scalar(nb[:, g % 4:g % 4 + 1], m, -(HD ** -0.5), None, ALU.mult).then_inc(max_done, 1)

            def normalise(T):
                dve.wait_ge(pv, AH * (T + 1))
                dve.wait_ge(exp_done, AH * (T + 1))
                if T >= 2:
                    dve.wait_ge(att_out[T % 2], 16 * (T // 2))
                dve.reciprocal(rrs[:], rs[:, T % 2, :])
                dve.drain()
                dve.tensor_tensor(att[:, T % 2], po[:].rearrange("p (h d) -> p h d", h=AH), bc(rrs[:], 2, HD), ALU.mult).then_inc(att_done, 1)

            for T in range(FIRST):
                dve.tensor_copy(mask[:, T % 2, width(T) - P:width(T)], c[:, B_CAUSAL:B_CAUSAL + P])
            dve.drain()
            for T, hh in steps:
                ks = len(chunks(T)) if T >= 0 else 1
                for k in range(ks):
                    if T >= 0:
                        mask_logits(T, hh, k)
                    if T >= 1 and hh == 1 and k == 0:
                        normalise(T - 1)
                for x in range(4):
                    if FIRST <= T + 1 < NT:
                        threshold(T + 1, 4 * hh + x)
                if hh == AH - 1:
                    dve.drain().then_inc(ranked, 1)
            normalise(NT - 1)

        @block.gpsimd
        def _(pool):
            pool.wait_ge(loaded, 80)

            def weigh(T, hh):
                hd = head(hh)[2]
                if hh == 0 and T >= FIRST + 3:
                    pool.wait_ge(ranked, T - FIRST - 1)
                for k, (a, w_) in enumerate(chunks(T)):
                    n = icount(T, hh, k)
                    pool.wait_ge(relued, n)
                    out, r, w1 = score[:, T % 3, a:a + w_], relu[:, n % 4, 0:w_], wi[:, TILES[T], hd:hd + 1]
                    if hh == 0:
                        pool.tensor_scalar(out, r, w1, None, ALU.mult).then_inc(weighed, 1)
                    else:
                        pool.tensor_scalar(r, r, w1, None, ALU.mult)
                        pool.drain()
                        pool.tensor_tensor(out, out, r, ALU.add).then_inc(weighed, 1)

            for T in range(FIRST, NT):
                for hh in range(IH):
                    weigh(T, hh)


S_ID, S_PAIR, S_SAME, S_LOWER, S_NEW, S_SLOT, S_ROWBASE, S_IOTA = 0, 128, 144, 272, 400, 404, 406, 470
S_HALF = S_IOTA + TOPK
S_SAMEH = S_HALF + NSTEP
S_W = S_SAMEH + P
CH = 4
CKEYS = PAST // CH
CPAGES = NPAGES // CH


def sample_table():
    c = np.zeros((P, S_W), np.float32)
    p = np.arange(P)
    c[:, S_ID:S_ID + P] = np.eye(P)
    b2, par, tok = p // 64, p // 32 % 2, p % TS
    c[p, S_PAIR + b2 * 8 + par * 4 + tok] = 1
    part, row = p // NS, p % NS
    c[:, S_SAME:S_SAME + P] = row[:, None] == row[None, :]
    c[:, S_LOWER:S_LOWER + P] = (row[:, None] == row[None, :]) & (part[:, None] < part[None, :])
    new = np.arange(TS)
    c[:, S_NEW:S_NEW + TS] = np.where((part[:, None] == CH - 1) & (new[None, :] <= row[:, None] % TS), 0, -BIG)
    for half in range(2):
        c[:, S_SLOT + half] = p + 1 + P * half
        c[:, S_ROWBASE + half:S_ROWBASE + 2 * NS:2] = np.arange(NS) * NPAGES
    c[:, S_IOTA:S_IOTA + TOPK] = np.arange(TOPK) + 1
    c[:, S_SAMEH:S_W] = -0.5 * c[:, S_SAME:S_SAME + P]
    c[:, S_HALF:S_HALF + NSTEP] = 2.0 ** -(np.arange(NSTEP) + 1.0)
    return c


def sample_index_phase(nc, t):
    with ExitStack() as ctx:
        sb = lambda name, shape, dt=F32: ctx.enter_context(nc.sbuf_tensor("s_" + name, shape, dt))
        sem = lambda name: ctx.enter_context(nc.semaphore("s_" + name))
        Q = 4
        GROUPS_Q = 4
        G = Q * GROUPS_Q
        signal = lambda name, per: Signal(sem(name), per, tiles=1)
        PAIRS = NB // 2
        QW = PAGE // Q * HD

        c = sb("consts", [P, S_W])
        ident = c[:, S_ID:S_ID + P]
        pti = sb("pti", [P, NB], I32)
        ptf = sb("ptf", [P, NB])
        rowf = sb("rowf", [P, NB, Q])
        row = sb("row", [P, PAIRS, 2 * Q], U32)
        rown = sb("rown", [P, 2 * Q], U32)
        keys = sb("keys", [P, 2, 2, QW])
        kT = sb("kT", [P, 2, 2, 512])
        qd = sb("qd", [P, IH, NS])
        qb = sb("qb", [P, PAIRS, 2 * 64])
        qn = sb("qn", [P, 2 * 64])
        wv = sb("wv", [P, PAIRS])
        wb = sb("wb", [P, PAIRS, 16])
        wn = sb("wn", [P, 16])
        kin = sb("kin", [P, NS])
        relu = sb("relu", [P, 2, 512])
        out = sb("out", [16, NPAGES, PAGE // 2])
        rnew = sb("rnew", [P, PAIRS * TS])
        onew = sb("onew", [16, PAIRS * TS])
        pk = ctx.enter_context(nc.psum_tensor("s_pk", [P, 2, 2, 512], F32))
        p1 = ctx.enter_context(nc.psum_tensor("s_p1", [P, 2, 512], F32))
        p2 = ctx.enter_context(nc.psum_tensor("s_p2", [P, 2, 512], F32))

        loaded = sem("loaded")
        weights = sem("weights")
        pages = sem("pages")
        ready = sem("ready")
        rows_done = sem("rows_done")
        rown_done = signal("rown_done", 1)
        may_gather = sem("may_gather")
        landed = [sem(f"landed{s}") for s in range(2)]
        new1, new2, new3, new4 = sem("new1"), sem("new2"), sem("new3"), sem("new4")
        pair_ready = signal("pair_ready", 1)
        turned = signal("turned", G)
        kT0 = signal("kT0", G)
        kT1 = signal("kT1", G)
        prod = signal("prod", G)
        relued = signal("relued", G)
        summed = signal("summed", G)
        kept = signal("kept", G)
        stored = sem("stored")
        new_stored = sem("new_stored")

        block = ctx.enter_context(nc.Block())

        @block.sync
        def _(sp):
            sp.sem_inc(stored, 64)
            sp.dma_start(pti[:], t.page_table.rearrange("b p -> p b"), allow_slow_non_contiguous=True).then_inc(pages, 16)
            sp.dma_start(c[:], t.s_c).then_inc(loaded, 16)
            tr = t.tr[SEQ:SEQ + P, :]
            for par in range(2):
                for half in range(2):
                    sp.dma_start(qd[par * HD:(par + 1) * HD, half * 4:half * 4 + 4, :],
                                 tr[half * HD:(half + 1) * HD, 4 * P:8 * P].rearrange("p (j c) -> p j c", j=4)[:, :, 0:NS]).then_inc(loaded, 16)
            sp.dma_start(kin[:], tr[:, 9 * P:9 * P + NS]).then_inc(loaded, 16)
            w = t.kiv[SEQ:SEQ + NS, 320:328].rearrange("(a b t) h -> b h t a", b=2, t=TS)
            for b2 in range(2):
                for par in range(2):
                    for h in range(IH):
                        at = b2 * 64 + par * 32 + h * TS
                        sp.dma_start(wv[at:at + TS, :], w[b2, h], allow_slow_non_contiguous=True).then_inc(weights, 16)
            sp.wait_ge(new4, 1)
            sp.dma_start(t.snew.rearrange("(a r) k -> r a k", a=PAIRS),
                         onew[:].rearrange("r (a k) -> r a k", a=PAIRS)).then_inc(new_stored, 16)
            sp.wait_ge(new_stored, 16)
            sp.nop()
            with sp.Fori(0, PAIRS) as i:
                base = sp.snap(i * 2 * TS)
                dst = t.sscore[bass.ds(base, 2 * TS)].rearrange("(b t) g x k -> b x t g k", b=2)
                sp.wait_ge(kept.sem, kept.at((i, 0)))
                for b2 in range(2):
                    for par in range(2):
                        at = b2 * 8 + par * 4
                        sp.dma_start(dst[b2, par], out[at:at + TS]).then_inc(stored, 16)
            sp.wait_ge(stored, 64 * (PAIRS + 1))

        @block.gpsimd
        def _(pool):
            rown_done.seed(pool)
            src = t.cache_idx.rearrange("n (q w) -> (n q) w", q=Q)
            pool.wait_ge(rows_done, 1)
            with pool.Fori(0, PAIRS) as i:
                pool.tensor_copy(rown[:], row[:, bass.ds(i, 1), :].rearrange("p a n -> p (a n)")).then_inc(rown_done.sem, 1)
                pool.wait_ge(rown_done.sem, rown_done.at((i, 0)))
                for q in range(Q):
                    if q >= 2:
                        pool.wait_ge(turned.sem, turned.at((i, 0), GROUPS_Q * (q - 1)))
                    else:
                        pool.wait_ge(turned.sem, turned.at((i, -1), GROUPS_Q * (q + 3)))
                    pool.sem_inc(may_gather, 1)
                    for b2 in range(2):
                        pool.indirect_dma_start(out=keys[:, q % 2, b2, :], out_offset=None, in_=src,
                                                in_offset=bass.IndirectOffsetOnAxis(ap=rown[:, b2 * Q + q:b2 * Q + q + 1], axis=0)
                                                ).then_inc(landed[q % 2], 16)
                for s in range(2):
                    pool.wait_ge(landed[s], i * 64 + 64)

        @block.tensor
        def _(pe):
            for s in (turned, prod, summed):
                s.seed(pe)
            pe.wait_ge(loaded, 16 * 6)
            pe.wait_ge(ready, 1)
            for a in range(PAIRS):
                for b2 in range(2):
                    m = pe.matmul(p1[b2 * 64:b2 * 64 + 64, 0, a * TS:(a + 1) * TS], qb[:, a, b2 * 64:b2 * 64 + 64],
                                  kin[:, (2 * a + b2) * TS:(2 * a + b2 + 1) * TS], start=True, stop=True)
            m.then_inc(new1, 1)
            pe.wait_ge(new2, 1)
            for a in range(PAIRS):
                m = pe.matmul(p2[0:16, 0, a * TS:(a + 1) * TS], wb[:, a, :], rnew[:, a * TS:(a + 1) * TS], start=True, stop=True)
            m.then_inc(new3, 1)

            def turn(i, g):
                q, gq = divmod(g, GROUPS_Q)
                if gq == 0:
                    pe.wait_ge(landed[q % 2], i * 64 + 32 * (q // 2 + 1))
                for k in (kT0, kT1):
                    pe.wait_ge(k.sem, k.at((i, 0), g - 1))
                for b2 in range(2):
                    for j in range(4):
                        at = (gq * 4 + j) * 2 * HD
                        m = pe.transpose(pk[:, g % 2, b2, j * P:(j + 1) * P], keys[:, q % 2, b2, at:at + 2 * HD], ident)
                m.then_inc(turned.sem, 1)

            def products(i, g):
                pe.wait_ge(relued.sem, relued.at((i, 0), g - 1))
                for b2, k in enumerate((kT0, kT1)):
                    pe.wait_ge(k.sem, k.at((i, 0), g + 1))
                    m = pe.matmul(p1[b2 * 64:b2 * 64 + 64, g % 2, :], qn[:, b2 * 64:b2 * 64 + 64], kT[:, g % 2, b2, :],
                                  start=True, stop=True)
                m.then_inc(prod.sem, 1)

            def sums(i, g):
                pe.wait_ge(kept.sem, kept.at((i, 0), g - 1))
                pe.wait_ge(relued.sem, relued.at((i, 0), g + 1))
                pe.matmul(p2[0:16, g % 2, :], wn[:], relu[:, g % 2, :], start=True, stop=True).then_inc(summed.sem, 1)

            pe.wait_ge(new4, 1)
            with pe.Fori(0, PAIRS) as i:
                for g in range(G + 2):
                    if g < G:
                        turn(i, g)
                    if g == 1:
                        pe.wait_ge(pair_ready.sem, pair_ready.at((i, 0)))
                    if 1 <= g <= G:
                        products(i, g - 1)
                    if g >= 2:
                        sums(i, g - 2)

        @block.scalar
        def _(act):
            for s in (kT0, relued):
                s.seed(act)
            act.wait_ge(new1, 1)
            act.activation(rnew[:], p1[:, 0, 0:PAIRS * TS], ACT.Relu).then_inc(new2, 1)

            with act.Fori(0, PAIRS) as i:
                for g in range(G + 1):
                    if g < G:
                        act.wait_ge(turned.sem, turned.at((i, 0), g + 1))
                        act.wait_ge(prod.sem, prod.at((i, 0), g - 1))
                        act.activation(kT[:, g % 2, 0, :], pk[:, g % 2, 0, :], ACT.Copy).then_inc(kT0.sem, 1)
                    if g >= 1:
                        h = g - 1
                        act.wait_ge(prod.sem, prod.at((i, 0), h + 1))
                        act.wait_ge(summed.sem, summed.at((i, 0), h - 1))
                        act.activation(relu[:, h % 2, :], p1[:, h % 2, :], ACT.Relu).then_inc(relued.sem, 1)

        @block.vector
        def _(dve):
            for s in (pair_ready, kT1, kept):
                s.seed(dve)
            dve.memset(qb[:].rearrange("p a n -> p (a n)"), 0.0)
            dve.wait_ge(pages, 16)
            dve.tensor_copy(ptf[:], pti[:])
            dve.drain()
            for q in range(Q):
                dve.tensor_scalar(rowf[:, :, q], ptf[:], float(Q), float(q), ALU.mult, ALU.add)
            dve.drain()
            dve.tensor_copy(row[:].rearrange("p a n -> p (a n)"), rowf[:].rearrange("p b q -> p (b q)")).then_inc(rows_done, 1)
            dve.wait_ge(loaded, 16 * 6)
            dve.wait_ge(weights, 16 * 4 * IH)
            for par in range(2):
                rows = slice(par * HD, (par + 1) * HD)
                dst = qb[rows].rearrange("p a (b x h t) -> p (a b) x h t", b=2, x=2, h=IH)[:, :, par]
                dve.tensor_copy(dst, qd[rows].rearrange("p h (b t) -> p b h t", b=NB))
            for a in range(PAIRS):
                m = dve.tensor_scalar(wb[:, a, :], c[:, S_PAIR:S_PAIR + 16], wv[:, a:a + 1], None, ALU.mult)
            dve.drain().then_inc(ready, 1)
            dve.wait_ge(new3, 1)
            dve.tensor_copy(onew[:], p2[0:16, 0, 0:PAIRS * TS]).then_inc(new4, 1)

            with dve.Fori(0, PAIRS) as i:
                dve.wait_ge(summed.sem, summed.at((i, -1)))
                dve.tensor_copy(qn[:], qb[:, bass.ds(i, 1), :].rearrange("p a n -> p (a n)"))
                dve.tensor_copy(wn[:], wb[:, bass.ds(i, 1), :].rearrange("p a n -> p (a n)"))
                dve.drain().then_inc(pair_ready.sem, 1)
                for g in range(G + 2):
                    if g < G:
                        dve.wait_ge(turned.sem, turned.at((i, 0), g + 1))
                        dve.wait_ge(prod.sem, prod.at((i, 0), g - 1))
                        dve.tensor_copy(kT[:, g % 2, 1, :], pk[:, g % 2, 1, :]).then_inc(kT1.sem, 1)
                    if g >= 2:
                        h = g - 2
                        dve.wait_ge(summed.sem, summed.at((i, 0), h + 1))
                        if h == 0:
                            dve.wait_ge(stored, i * 64 + 64)
                        dve.tensor_copy(out[:, :, h * 4:h * 4 + 4].rearrange("r g k -> r k g"),
                                        p2[0:16, h % 2, :].rearrange("r (k g) -> r k g", k=4)).then_inc(kept.sem, 1)


TABW = PAGE + 1


def sample_select_phase(nc, t):
    with ExitStack() as ctx:
        sb = lambda name, shape, dt=F32: ctx.enter_context(nc.sbuf_tensor("k_" + name, shape, dt))
        sem = lambda name: ctx.enter_context(nc.semaphore("k_" + name))
        N = CKEYS + TS
        SHARE = CKEYS * 9 // 16
        FULL = TOPK - 0.5 - CH * SHARE / 2
        c = sb("consts", [P, S_W])
        ident = c[:, S_ID:S_ID + P]
        raw = sb("raw", [P, CKEYS])
        score = sb("score", [P, N])
        new = sb("new", [P, TS])
        above = sb("above", [P, N])
        band = sb("band", [P, N])
        rank = sb("rank", [P, N])
        table = sb("table", [P, CPAGES, TABW])
        phi = sb("phi", [P, CPAGES], I32)
        ends = sb("ends", [P, CPAGES])
        newmask = sb("newmask", [P, TS])
        ext = sb("ext", [P, 2])
        extr = sb("extr", [2, CH, NS])
        lim = sb("lim", [P, 8])
        pair = sb("pair", [P, 2])
        step = sb("step", [P, NSTEP])
        mid = sb("mid", [P, NSTEP])
        cnt = sb("cnt", [P, NSTEP])
        signs = sb("signs", [P, NSTEP])
        tot = sb("tot", [P, NSTEP])
        ps = ctx.enter_context(nc.psum_tensor("k_ps", [P, 2, 512], F32))
        lo, hi, took, need = (lim[:, j:j + 1] for j in range(4))

        loaded, new_in, pages_in = sem("loaded"), sem("new_in"), sem("pages_in")
        new_clear = sem("new_clear")
        asked = sem("asked")
        middle = sem("middle")
        counted = sem("counted")
        told = sem("told")
        done, stored = sem("done"), sem("stored")
        block = ctx.enter_context(nc.Block())

        @block.sync
        def _(sp):
            for a in range(CH):
                sp.dma_start(raw[a * NS:(a + 1) * NS, :],
                             t.sscore.rearrange("r (c g) x k -> c r (g x k)", c=CH)[a]).then_inc(loaded, 16)
            sp.dma_start(c[:], t.s_c).then_inc(loaded, 16)
            for a in range(CH):
                for b in range(NB):
                    at = a * NS + b * TS
                    sp.dma_start(phi[at:at + TS, :], t.page_table[b, a * CPAGES:(a + 1) * CPAGES].partition_broadcast(TS)
                                 ).then_inc(pages_in, 16)
            sp.wait_ge(new_clear, 1)
            sp.dma_start(new[(CH - 1) * NS:P, :], t.snew.rearrange("(b x t) k -> x b t k", x=2, t=TS)[0]).then_inc(new_in, 16)
            sp.wait_ge(done, 1)
            for a in range(CH):
                rows = slice(a * NS, (a + 1) * NS)
                sp.dma_start(t.table.rearrange("(r c g) n -> c r (g n)", r=NS, c=CH)[a],
                             table[rows].rearrange("p g n -> p (g n)")).then_inc(stored, 16)
                sp.dma_start(t.pagecum.rearrange("r (c g) -> c r g", c=CH)[a], ends[rows, :]).then_inc(stored, 16)
            sp.dma_start(t.newmask, newmask[(CH - 1) * NS:P, :]).then_inc(stored, 16)
            sp.wait_ge(stored, 16 * (2 * CH + 1))

        asks = ["turn", "back"] + ["count"] * NSTEP + ["same", "lower", "lower"]

        @block.tensor
        def _(pe):
            pe.wait_ge(loaded, 16 * (CH + 1))
            for n, kind in enumerate(asks):
                pe.wait_ge(asked, n + 1)
                out = ps[:, n % 2, :]
                if kind == "turn":
                    m = pe.transpose(out[0:2, 0:P], ext[:], ident)
                elif kind == "back":
                    m = pe.transpose(out[:, 0:2], extr[:].rearrange("x c r -> x (c r)"), ident[0:2, 0:2])
                elif kind == "count":
                    k = n - 2
                    pe.matmul(out[:, 0:1], c[:, S_SAME:S_SAME + P], cnt[:, k:k + 1], start=True, stop=False)
                    pe.wait_ge(counted, k + 1)
                    m = pe.matmul(out[:, 0:1], c[:, S_SAMEH:S_SAMEH + P], signs[:, k:k + 1], start=False, stop=True)
                elif kind == "same":
                    m = pe.matmul(out[:, 0:1], c[:, S_SAME:S_SAME + P], pair[:, 0:1], start=True, stop=True)
                else:
                    m = pe.matmul(out[:, 0:1], c[:, S_LOWER:S_LOWER + P], pair[:, 1:2], start=True, stop=True)
                m.then_inc(told, 1)

        @block.scalar
        def _(act):
            for k in range(NSTEP):
                act.wait_ge(middle, k + 1)
                act.activation(rank[:, 0:SHARE], score[:, 0:SHARE], ACT.Sign, bias=mid[:, k:k + 1], scale=-1.0,
                               accum_out=signs[:, k:k + 1]).then_inc(counted, 1)

        @block.vector
        def _(dve):
            asked_n = [0]

            def ask(ins):
                ins.then_inc(asked, 1)
                asked_n[0] += 1
                dve.wait_ge(told, asked_n[0])
                return ps[:, (asked_n[0] - 1) % 2, :]

            dve.memset(new[:], 0.0).then_inc(new_clear, 1)
            dve.wait_ge(loaded, 16 * (CH + 1))
            dve.tensor_copy(score[:, 0:CKEYS].rearrange("p (g k x) -> p g x k", g=CPAGES, x=2),
                            raw[:].rearrange("p (g x k) -> p g x k", g=CPAGES, x=2))
            dve.wait_ge(new_in, 16)
            dve.tensor_tensor(score[:, CKEYS:N], new[:], c[:, S_NEW:S_NEW + TS], ALU.add)
            dve.drain()
            dve.tensor_reduce(ext[:, 0:1], score[:], AX.X, ALU.max)
            dve.tensor_reduce(ext[:, 1:2], score[:, 0:CKEYS], AX.X, ALU.min)
            dve.drain()
            out = ask(dve.tensor_scalar(ext[:, 1:2], ext[:, 1:2], -1.0, None, ALU.mult))
            dve.tensor_reduce(extr[:, 0, :], out[0:2, 0:P].rearrange("x (c r) -> x r c", c=CH), AX.X, ALU.max)
            dve.drain()
            out = ask(dve.tensor_copy(extr[:, 1:CH, :], bc(extr[:, 0, :], 1, CH - 1)))
            dve.tensor_copy(hi, out[:, 0:1])
            dve.tensor_scalar(lo, out[:, 1:2], -1.0, None, ALU.mult)
            dve.drain()
            dve.tensor_tensor(took, hi, lo, ALU.subtract)
            dve.drain()
            dve.tensor_scalar(step[:], c[:, S_HALF:S_HALF + NSTEP], took, None, ALU.mult)
            dve.drain()
            dve.tensor_tensor(mid[:, 0:1], lo, step[:, 0:1], ALU.add).then_inc(middle, 1)
            dve.drain()
            for k in range(NSTEP):
                out = ask(dve.tensor_scalar(above[:, SHARE:N], score[:, SHARE:N], mid[:, k:k + 1], None, ALU.is_ge, ALU.add,
                                            accum_out=cnt[:, k:k + 1]))
                if k + 1 < NSTEP:
                    dve.tensor_scalar(took, out[:, 0:1], FULL, step[:, k:k + 1], ALU.is_ge, ALU.mult)
                    dve.drain()
                    dve.scalar_tensor_tensor(mid[:, k + 1:k + 2], mid[:, k:k + 1], step[:, k + 1:k + 2], took, ALU.subtract, ALU.add
                                             ).then_inc(middle, 1)
                dve.tensor_copy(tot[:, k:k + 1], out[:, 0:1])
                dve.drain()
            dve.tensor_scalar(tot[:], tot[:], FULL, BIG, ALU.is_ge, ALU.mult)
            dve.drain()
            dve.tensor_tensor(step[:], mid[:], tot[:], ALU.add)
            dve.scalar_tensor_tensor(mid[:], tot[:], -BIG, mid[:], ALU.add, ALU.add)
            dve.drain()
            dve.tensor_reduce(took, step[:], AX.X, ALU.min)
            dve.tensor_reduce(need, mid[:], AX.X, ALU.max)
            dve.drain()
            dve.tensor_tensor(hi, hi, took, ALU.min)
            dve.tensor_tensor(lo, lo, need, ALU.max)
            dve.drain()
            out = ask(dve.tensor_scalar(above[:], score[:], hi, None, ALU.is_gt, ALU.add, accum_out=pair[:, 0:1]))
            dve.tensor_scalar(need, out[:, 0:1], -1.0, float(TOPK), ALU.mult, ALU.add)
            dve.scalar_tensor_tensor(band[:], score[:], lo, above[:], ALU.is_ge, ALU.subtract)
            dve.drain()
            dve.tensor_tensor_scan(rank[:], band[:], band[:], 0.0, ALU.add, ALU.max)
            dve.drain()
            out = ask(dve.tensor_copy(pair[:, 1:2], rank[:, N - 1:N]))
            dve.tensor_tensor(need, need, out[:, 0:1], ALU.subtract)
            dve.drain()
            dve.scalar_tensor_tensor(band[:], rank[:], need, band[:], ALU.is_le, ALU.mult)
            dve.drain()
            dve.tensor_tensor(band[:], band[:], above[:], ALU.add)
            dve.drain()
            dve.tensor_scalar(newmask[:], band[:, CKEYS:N], -1.0, BIG, ALU.add, ALU.mult)
            dve.tensor_tensor_scan(rank[:, 0:CKEYS], band[:, 0:CKEYS], band[:, 0:CKEYS], 0.0, ALU.add, ALU.max)
            dve.drain()
            out = ask(dve.tensor_copy(pair[:, 1:2], rank[:, CKEYS - 1:CKEYS]))
            dve.tensor_copy(lo, out[:, 0:1])
            dve.drain()
            dve.tensor_scalar(table[:, :, 0:PAGE], rank[:, 0:CKEYS].rearrange("p (g n) -> p g n", g=CPAGES), lo, None, ALU.add)
            dve.wait_ge(pages_in, 16 * CH * NB)
            dve.tensor_copy(table[:, :, PAGE], phi[:])
            dve.drain()
            dve.tensor_copy(ends[:], table[:, :, PAGE - 1])
            dve.drain().then_inc(done, 1)


def sample_attend_phase(nc, t):
    with ExitStack() as ctx:
        sb = lambda name, shape, dt=F32: ctx.enter_context(nc.sbuf_tensor("g_" + name, shape, dt))
        sem = lambda name: ctx.enter_context(nc.semaphore("g_" + name))
        S2 = 2 * NS
        W = TOPK + TS
        HALFR = NS // 2

        c = sb("consts", [P, S_W])
        ident = c[:, S_ID:S_ID + P]
        table = sb("table", [P, NS, TABW])
        after = sb("after", [P, NS, TABW])
        beyond = sb("beyond", [P, NS, TOPK])
        less = sb("less", [P, PAGE])
        phys = sb("phys", [P, S2])
        off = sb("off", [P, S2])
        rowk = sb("rowk", [P, S2], U32)
        kvg = sb("kvg", [P, S2, 2 * P])
        kT = sb("kT", [P, NS, W])
        kn = sb("kn", [P, NS])
        vn = sb("vn", [TS, NB, P])
        qT = sb("qT", [P, 4, NS])
        qz = sb("qz", [P, NS * P + 256])
        have = sb("have", [P, 2])
        mask = sb("mask", [P, 2, W])
        logit = sb("logit", [P, 2, W])
        mx = sb("mx", [P, 4])
        rs = sb("rs", [P, 2])
        pT = sb("pT", [P, 2, 2, P])
        pTn = sb("pTn", [TS, 2, P])
        at_ = sb("at", [P, 4, NS])
        att = sb("att", [NS, KVH, 4, HD])
        pk = ctx.enter_context(nc.psum_tensor("g_pk", [P, 4, 512], F32))
        pl = ctx.enter_context(nc.psum_tensor("g_pl", [P, 2, 512], F32))
        po = ctx.enter_context(nc.psum_tensor("g_po", [P, 512], F32))
        pf = ctx.enter_context(nc.psum_tensor("g_pf", [P, 512], F32))

        IB = 3
        BANKS = -(-S2 // IB)
        SPLIT = BANKS // 2
        loaded, table_in, q_in, cleared = sem("loaded"), sem("table_in"), sem("q_in"), sem("cleared")
        beyond_done = sem("beyond_done")
        row_out = sem("row_out")
        row_taken = sem("row_taken")
        rowk_done = sem("rowk_done")
        GROUPS_G = 4
        GS = S2 // GROUPS_G
        kv_in = [sem(f"kv_in{g}") for g in range(GROUPS_G)]
        q_ready = sem("q_ready")
        turned, kT_done = sem("turned"), sem("kT_done")
        logits, max_done, exp_done, normed = sem("logits"), sem("max_done"), sem("exp_done"), sem("normed")
        pturned, pT_done = sem("pturned"), sem("pT_done")
        pv, att_done, fturned, out_done, stored = sem("pv"), sem("att_done"), sem("fturned"), sem("out_done"), sem("stored")
        block = ctx.enter_context(nc.Block())

        @block.sync
        def _(sp):
            src = t.table.rearrange("(r g) n -> g r n", g=NPAGES)
            sp.dma_start(table[:], src).then_inc(table_in, 16)
            sp.wait_ge(cleared, 1)
            sp.dma_start(after[0:P - 1], src[1:NPAGES]).then_inc(table_in, 16)
            sp.dma_start(c[:], t.s_c).then_inc(loaded, 16)
            tr = t.tr[SEQ:SEQ + P, :]
            sp.dma_start(qT[:], tr[:, 0:4 * P].rearrange("p (j c) -> p j c", j=4)[:, :, 0:NS]).then_inc(q_in, 16)
            sp.dma_start(kn[:], tr[:, 8 * P:8 * P + NS]).then_inc(q_in, 16)
            sp.dma_start(vn[:], t.kiv[SEQ:SEQ + NS, 192:320].rearrange("(b t) d -> t b d", b=NB)).then_inc(q_in, 16)
            for g in range(2):
                for r in range(HALFR):
                    row = g * HALFR + r
                    sp.dma_start(have[r * AH:(r + 1) * AH, g:g + 1],
                                 t.pagecum[row, NPAGES - 1:NPAGES].partition_broadcast(AH)).then_inc(q_in, 16)
                    sp.dma_start(mask[r * AH:(r + 1) * AH, g, TOPK:W],
                                 t.newmask[row, :].partition_broadcast(AH)).then_inc(q_in, 16)
            sp.wait_ge(out_done, 1)
            sp.dma_start(t.cat[SEQ:SEQ + NS, 0:512], att[:].rearrange("p v j d -> p (v j d)")).then_inc(stored, 16)
            sp.wait_ge(stored, 16)

        @block.gpsimd
        def _(pool):
            for s in range(S2):
                if s in (0, SPLIT * IB):
                    pool.wait_ge(rowk_done, 1 if s == 0 else 2)
                pool.indirect_dma_start(out=kvg[:, s, :], out_offset=None, in_=t.cache_kv,
                                        in_offset=bass.IndirectOffsetOnAxis(ap=rowk[:, s:s + 1], axis=0)).then_inc(kv_in[s // GS], 16)
            for g in range(GROUPS_G):
                pool.wait_ge(kv_in[g], 16 * GS)

        KG = S2 // 4

        @block.tensor
        def _(pe):
            pe.wait_ge(loaded, 16)
            pe.wait_ge(beyond_done, 1)
            for b in range(BANKS):
                if b >= 4:
                    pe.wait_ge(row_taken, b - 3)
                for x in range(min(IB, S2 - b * IB)):
                    row, half = divmod(b * IB + x, 2)
                    m = pe.matmul(pk[:, b % 4, x * TABW:(x + 1) * TABW], beyond[:, row, half * P:(half + 1) * P], table[:, row, :],
                                  start=True, stop=True)
                m.then_inc(row_out, 1)
            pe.wait_ge(row_taken, BANKS)
            for g in range(2):
                for n in range(g * KG // 2, (g + 1) * KG // 2):
                    if 4 * n % GS == 0:
                        pe.wait_ge(kv_in[4 * n // GS], 16 * GS)
                    if n >= 2:
                        pe.wait_ge(kT_done, n - 1)
                    for j in range(4):
                        m = pe.transpose(pk[:, n % 2, j * P:(j + 1) * P], kvg[:, 4 * n + j, 0:P], ident)
                    m.then_inc(turned, 1)
                pe.wait_ge(q_ready, 1)
                pe.wait_ge(kT_done, (g + 1) * KG // 2)
                for r in range(HALFR):
                    row = g * HALFR + r
                    m = pe.matmul(pl[:, g, 0:W], qz[:, row * P:(row + 1) * P], kT[:, row, :], start=(r == 0), stop=(r == HALFR - 1))
                m.then_inc(logits, 1)
                pe.wait_ge(normed, g + 1)
                for half in range(2):
                    pe.transpose(pk[:, 2 + g, half * P:(half + 1) * P], logit[:, g, half * P:(half + 1) * P], ident)
                pe.transpose(pk[0:TS, 2 + g, 2 * P:3 * P], logit[:, g, TOPK:W], ident).then_inc(pturned, 1)
                pe.wait_ge(pT_done, g + 1)
                for r in range(HALFR):
                    row = g * HALFR + r
                    cols = slice(r * AH, (r + 1) * AH)
                    out = po[:, row * AH:(row + 1) * AH]
                    for half in range(2):
                        pe.matmul(out, kvg[:, 2 * row + half, P:2 * P], pT[:, g, half, cols], start=(half == 0), stop=False)
                    m = pe.matmul(out, vn[:, row // TS, :], pTn[:, g, cols], start=False, stop=True)
            m.then_inc(pv, 1)
            pe.wait_ge(att_done, 1)
            for j in range(4):
                m = pe.transpose(pf[0:NS, j * P:(j + 1) * P], at_[:, j, :], ident)
            m.then_inc(fturned, 1)

        @block.scalar
        def _(act):
            for g in range(2):
                for n in range(g * KG // 2, (g + 1) * KG // 2):
                    act.wait_ge(turned, n + 1)
                    act.activation(kT[:, 2 * n:2 * n + 2, 0:TOPK], pk[:, n % 2, :].rearrange("p (r c) -> p r c", r=2), ACT.Copy).then_inc(kT_done, 1)
                act.wait_ge(max_done, g + 1)
                act.activation(logit[:, g, :], logit[:, g, :], ACT.Exp, bias=mx[:, 2 + g:3 + g], scale=HD ** -0.5,
                               accum_out=rs[:, g:g + 1]).then_inc(exp_done, 1)

        @block.vector
        def _(dve):
            dve.memset(after[:], 0.0).then_inc(cleared, 1)
            dve.wait_ge(loaded, 16)
            dve.wait_ge(table_in, 32)
            dve.tensor_tensor(beyond[:], bc(c[:, S_IOTA:S_IOTA + TOPK], 1, NS), bc(table[:, :, PAGE - 1], 2, TOPK), ALU.is_le)
            dve.drain()
            dve.tensor_tensor(table[:], table[:], after[:], ALU.subtract).then_inc(beyond_done, 1)
            for b in range(BANKS):
                dve.wait_ge(row_out, b + 1)
                items = range(b * IB, min(b * IB + IB, S2))
                got = pk[:, b % 4, 0:len(items) * TABW].rearrange("p (x n) -> p x n", n=TABW)
                dve.tensor_copy(phys[:, items[0]:items[-1] + 1], got[:, :, PAGE])
                for s in items:
                    m = dve.tensor_scalar(less[:], got[:, s - items[0], 0:PAGE], c[:, S_SLOT + s % 2:S_SLOT + s % 2 + 1], None,
                                          ALU.is_lt, ALU.add, accum_out=off[:, s:s + 1])
                    dve.drain()
                m.then_inc(row_taken, 1)
                if b in (SPLIT - 1, BANKS - 1):
                    ss = slice(0, SPLIT * IB) if b < BANKS - 1 else slice(SPLIT * IB, S2)
                    dve.tensor_scalar(off[:, ss], off[:, ss], PAGE - 1.0, None, ALU.min)
                    dve.drain()
                    dve.scalar_tensor_tensor(off[:, ss], phys[:, ss], float(PAGE), off[:, ss], ALU.mult, ALU.add)
                    dve.drain()
                    dve.tensor_copy(rowk[:, ss], off[:, ss]).then_inc(rowk_done, 1)
            dve.memset(qz[:], 0.0)
            dve.drain()
            dve.wait_ge(q_in, 16 * (3 + 2 * NS))
            for kv in range(KVH):
                rows = slice(kv * HD, (kv + 1) * HD)
                for g in range(2):
                    at = g * HALFR * P + kv * 4
                    dst = qz[rows, at:at + HALFR * (P + AH)].rearrange("p (r x) -> p r x", x=P + AH)[:, :, 0:4]
                    m = dve.tensor_copy(dst, qT[rows, :, g * HALFR:(g + 1) * HALFR].rearrange("p j r -> p r j"))
            for g in range(2):
                dve.tensor_scalar(mask[:, g, 0:TOPK], c[:, S_IOTA:S_IOTA + TOPK], have[:, g:g + 1], -BIG, ALU.is_gt, ALU.mult)
            dve.tensor_copy(kT[:, :, TOPK:W].rearrange("p (b t) k -> p b t k", b=NB),
                            kn[:].rearrange("p (b k) -> p b k", b=NB).unsqueeze(2).broadcast_to([P, NB, TS, TS]))
            dve.drain().then_inc(q_ready, 1)
            for g in range(2):
                dve.wait_ge(logits, g + 1)
                dve.tensor_tensor_reduce(logit[:, g, :], pl[:, g, 0:W], mask[:, g, :], 1.0, -3.0e38, ALU.add, ALU.max,
                                         accum_out=mx[:, g:g + 1])
                dve.drain()
                dve.tensor_scalar(mx[:, 2 + g:3 + g], mx[:, g:g + 1], -(HD ** -0.5), None, ALU.mult).then_inc(max_done, 1)
                dve.wait_ge(exp_done, g + 1)
                dve.reciprocal(rs[:, g:g + 1], rs[:, g:g + 1])
                dve.drain()
                dve.tensor_scalar(logit[:, g, :], logit[:, g, :], rs[:, g:g + 1], None, ALU.mult).then_inc(normed, 1)
                dve.wait_ge(pturned, g + 1)
                dve.tensor_copy(pT[:, g].rearrange("p h c -> p (h c)"), pk[:, 2 + g, 0:2 * P])
                dve.tensor_copy(pTn[:, g, :], pk[0:TS, 2 + g, 2 * P:3 * P])
                dve.drain().then_inc(pT_done, 1)
            dve.wait_ge(pv, 1)
            for kv in range(KVH):
                rows = slice(kv * HD, (kv + 1) * HD)
                dve.tensor_copy(at_[rows], po[rows, 0:NS * AH].rearrange("p (r v j) -> p v j r", v=KVH, j=4)[:, kv])
            dve.drain().then_inc(att_done, 1)
            dve.wait_ge(fturned, 1)
            dve.tensor_copy(att[:], pf[0:NS, :].rearrange("p (j v d) -> p v j d", j=4, v=KVH)).then_inc(out_done, 1)


CK = 416
TT = 104
NCHUNK = (SEQ + NS) // CK
FB = DFF // P
KPL = PLE // P
F32R = mybir.dt.float32r

FFN0, DOWN0, PLE0 = KD, KD + 2 * FB, 2 * KD + 2 * FB
MM = PLE0 + 2 * KD
PARTS = [range(0, 8), range(8, 15), range(15, FB)]
NP = len(PARTS)
ITEMS = MM + (NP - 1) * KD


def item_blocks(m):
    m %= ITEMS
    if m < FFN0:
        return 0, m, range(KD)
    if m < DOWN0:
        return 1, (m - FFN0) % 2 * FB + (m - FFN0) // 2, range(KD)
    if m < DOWN0 + NP * KD:
        return 2, (m - DOWN0) // NP, PARTS[(m - DOWN0) % NP]
    col, gate = divmod(m - DOWN0 - NP * KD, 2)
    return (4, col, range(KD)) if gate else (3, col, range(KPL))


def weight_items(w_out, w_ffn_in, w_ffn_out, w_ple_proj, w_ple_gate):
    out = np.zeros((ITEMS, P, KD, P), np.float32)
    for m in range(ITEMS):
        stage, col, blocks = item_blocks(m)
        w_ = (w_out, w_ffn_in, w_ffn_out, w_ple_proj, w_ple_gate)[stage]
        part = w_[blocks[0] * P:(blocks[-1] + 1) * P, col * P:(col + 1) * P]
        out[m, :, :len(blocks)] = part.reshape(len(blocks), P, P).transpose(1, 0, 2)
    return out.reshape(ITEMS, P, KD * P)


def dense_phase(nc, t):
    with ExitStack() as ctx:
        sb = lambda name, shape, dt=F32: ctx.enter_context(nc.sbuf_tensor("d_" + name, shape, dt))
        sem = lambda name: ctx.enter_context(nc.semaphore("d_" + name))
        signal = lambda name, per: Signal(sem(name), per, tiles=1)
        RING = 4
        TB = 3
        ident = sb("ident", [P, P])[:]
        ones = sb("ones", [P, 1])
        gains = sb("gains", [P, 3, KD])
        raw = sb("raw", [P, RING, KD * P])
        wh = sb("wh", [P, RING, KD * P], F32R)
        wl = sb("wl", [P, RING, KD * P], F32R)
        cat = sb("cat", [TT, 2, D])
        x = sb("x", [TT, 2, D])
        ple = sb("ple", [TT, 2, PLE])
        hT = sb("hT", [P, KD, CK])
        nh = sb("nh", [P, KD, CK], F32R)
        nl = sb("nl", [P, KD, CK], F32R)
        pTh = sb("pTh", [P, KPL, CK], F32R)
        pTl = sb("pTl", [P, KPL, CK], F32R)
        ah = sb("ah", [P, FB, CK], F32R)
        al = sb("al", [P, FB, CK], F32R)
        sq = sb("sq", [P, 2, CK])
        acc = sb("acc", [P, CK])
        ms = sb("ms", [TT, 4])
        rstd = sb("rstd", [TT, 4])
        mhalf = sb("mhalf", [TT, 4])
        factor = sb("factor", [P, CK])
        work = sb("work", [P, 4 * CK])
        gate = work[:, 0:2 * CK].rearrange("p (s c) -> p s c", s=2)
        sig = work[:, 2 * CK:4 * CK].rearrange("p (s c) -> p s c", s=2)
        YS = 4
        y = [work[0:TT, a:a + 512] for a in range(0, 4 * CK - 511, 512)] + [sb("y", [TT, 512])[:]]
        pm = ctx.enter_context(nc.psum_tensor("d_pm", [P, 4, 512], F32))
        pt = ctx.enter_context(nc.psum_tensor("d_pt", [P, TB, 512], F32))
        pb = ctx.enter_context(nc.psum_tensor("d_pb", [P, 512], F32))
        pn = pb[0:TT, CK:CK + 4]

        LEAD = RING - 1

        EARLY = 3

        def first_item(p):
            if p >= MM:
                return ITEMS + first_item(p - MM)
            return p if p < DOWN0 else DOWN0 + NP * (p - DOWN0) if p < PLE0 else DOWN0 + NP * KD + p - PLE0

        def blocks_of(m):
            return len(item_blocks(m)[2])

        BEFORE = range(LEAD, LEAD + EARLY + 1)

        def items_at(p, last):
            if p <= EARLY:
                return range(0)
            end = first_item(p + 1) + LEAD
            return range(first_item(p) + LEAD, min(end, ITEMS) if last else end)

        loaded = sem("loaded")
        cat_landed = [sem(f"cat_landed{s}") for s in range(2)]
        x_landed = [sem(f"x_landed{s}") for s in range(2)]
        w_landed = [sem(f"w_landed{s}") for s in range(RING)]
        y_stored = [sem(f"y_stored{s}") for s in range(YS)]
        ones_done = sem("ones_done")
        w_high = signal("w_high", ITEMS)
        w_split = signal("w_split", ITEMS)
        part_used = signal("part_used", (NP - 1) * KD)
        cat_turned = signal("cat_turned", 8)
        x_turned = signal("x_turned", 12)
        y_turned = signal("y_turned", 8)
        cat_high = signal("cat_high", 8)
        p_high = signal("p_high", 4)
        cat_moved = signal("cat_moved", 8)
        x_moved = signal("x_moved", 12)
        y_moved = signal("y_moved", 8)
        prod = signal("prod", MM)
        used = signal("used", MM)
        summed = signal("summed", 3 * KD)
        squared = signal("squared", 3 * KD)
        sq_added = signal("sq_added", 3 * KD)
        n_high = signal("n_high", 2 * KD)
        n_split = signal("n_split", 2 * KD)
        ms_psum = signal("ms_psum", 3)
        ms_done = signal("ms_done", 3)
        rstd_done = signal("rstd_done", 3)
        spread = signal("spread", 3)
        factor_done = signal("factor_done", 3)
        normed = signal("normed", KD)
        gated = signal("gated", KD)
        sig_done = signal("sig_done", FB + KD)
        a_ready = signal("a_ready", FB)
        a_high = signal("a_high", FB)
        a_split = signal("a_split", FB)
        block = ctx.enter_context(nc.Block())

        @block.sync
        def _(sp):
            sp.dma_start(ident, t.c[:, C_ID:C_ID + P]).then_inc(loaded, 16)
            for j, g in enumerate((t.g_ffn, t.g_ple, t.g_final)):
                sp.dma_start(gains[:, j, :], g.rearrange("(k p) -> p k", p=P), allow_slow_non_contiguous=True).then_inc(loaded, 16)

            def load(m):
                cols = slice(0, blocks_of(m) * P)
                sp.dma_start(raw[:, m % RING, cols], t.w_items[m % ITEMS, :, cols]).then_inc(w_landed[m % RING], 16)

            def load_after(n, m):
                sp.wait_ge(w_split.sem, w_split.at(n, m - RING + 1))
                load(m)

            def load_cat(i, j, row):
                if j >= 2:
                    sp.wait_ge(cat_turned.sem, cat_turned.at((i, 0), 2 * (j - 1)))
                else:
                    sp.wait_ge(cat_turned.sem, cat_turned.at((i, -1), 2 * (j + 3)))
                sp.dma_start(cat[:, j % 2, :], t.cat[bass.ds(row, TT), :]).then_inc(cat_landed[j % 2], 16)

            def load_x(i, j, row):
                if j >= 2:
                    sp.wait_ge(x_turned.sem, x_turned.at((i, 0), 3 * (j - 1)))
                else:
                    sp.wait_ge(x_turned.sem, x_turned.at((i, -1), 3 * (j + 3)))
                sp.dma_start(x[:, j % 2, :], t.x[bass.ds(row, TT), :]).then_inc(x_landed[j % 2], 16)
                sp.dma_start(ple[:, j % 2, :], t.p[bass.ds(row, TT), :]).then_inc(x_landed[j % 2], 16)

            def body(i, rows, last):
                n = (i, 0)
                load_x(i, 2, rows[2])
                load_x(i, 3, rows[3])
                for m in range(BEFORE.stop, ITEMS if last else BEFORE.stop + ITEMS):
                    if not last and m == ITEMS // 2:
                        for j in range(2):
                            load_cat((i + 1), j, rows[4 + j])
                            load_x((i + 1), j, rows[4 + j])
                    if not last and m in (ITEMS - 4, ITEMS - 1):
                        j = 2 if m == ITEMS - 4 else 3
                        load_cat((i + 1), j, rows[4 + j])
                    load_after(n, m)

            for j in range(2):
                load_cat(0, j, j * TT)
            for m in range(LEAD):
                load(m)
            for j in range(2):
                load_x(0, j, j * TT)
            for j in range(2, 4):
                load_cat(0, j, j * TT)
            for m in BEFORE:
                load_after((0, 0), m)
            with sp.Fori(0, NCHUNK - 1) as i:
                body(i, [sp.snap(i * CK + j * TT) for j in range(8)], False)
            body(NCHUNK - 1, [(NCHUNK - 1) * CK + j * TT for j in range(4)], True)

        @block.tensor
        def _(pe):
            for s in (cat_turned, x_turned, y_turned, prod, part_used, ms_psum, spread):
                s.seed(pe)
            pe.wait_ge(loaded, 16 * 4)
            pe.wait_ge(ones_done, 1)

            def turn_cat(i, b):
                n = (i, 0)
                j, half = divmod(b, 2)
                if half == 0:
                    pe.wait_ge(cat_landed[j % 2], i * 32 + 16 * (j // 2 + 1))
                if b < TB:
                    pe.wait_ge(x_moved.sem, x_moved.at(n, 0))
                else:
                    pe.wait_ge(cat_moved.sem, cat_moved.at(n, b - TB + 1))
                for k in range(4):
                    col = (half * 4 + k) * P
                    m = pe.transpose(pt[:, b % TB, k * TT:(k + 1) * TT], cat[:, j % 2, col:col + P], ident[0:TT, 0:TT])
                m.then_inc(cat_turned.sem, 1)

            def turn_x(i, j):
                n = (i, 0)
                pe.wait_ge(x_landed[j % 2], i * 64 + 32 * (j // 2 + 1))
                for b in range(3):
                    at = 3 * j + b
                    if at < TB:
                        pe.wait_ge(y_moved.sem, y_moved.at(n, 0))
                    else:
                        pe.wait_ge(x_moved.sem, x_moved.at(n, at - TB + 1))
                    for k in range(4 if b < 2 else KPL):
                        col = (b * 4 + k) * P
                        src = x[:, j % 2, col:col + P] if b < 2 else ple[:, j % 2, k * P:(k + 1) * P]
                        m = pe.transpose(pt[:, at % TB, k * TT:(k + 1) * TT], src, ident[0:TT, 0:TT])
                    m.then_inc(x_turned.sem, 1)

            def turn_y(i, b, last):
                n = (i, 0)
                if b >= TB:
                    pe.wait_ge(y_moved.sem, y_moved.at(n, b - TB + 1))
                elif not last:
                    pe.wait_ge(cat_moved.sem, cat_moved.at(n, 16))
                j, half = divmod(b, 2)
                for k in range(4):
                    pe.wait_ge(normed.sem, normed.at(n, half * 4 + k + 1))
                    m = pe.transpose(pt[0:TT, b % TB, k * P:(k + 1) * P], hT[:, half * 4 + k, j * TT:(j + 1) * TT], ident)
                m.then_inc(y_turned.sem, 1)

            def product(i, p, operand, ready=None):
                n = (i, 0)
                pe.wait_ge(used.sem, used.at(n, p - 3))
                items = range(first_item(p), first_item(p + 1))
                k = 0
                for m in items:
                    pe.wait_ge(w_split.sem, w_split.at(n, m + 1))
                    blocks = blocks_of(m)
                    for b in range(blocks):
                        if ready:
                            ready(k)
                        high, low = operand(k)
                        cols = slice(b * P, (b + 1) * P)
                        out = pm[:, p % 4, 0:CK]
                        last = m == items[-1] and b == blocks - 1
                        pe.matmul(out, wl[:, m % RING, cols], high, start=(k == 0), stop=False)
                        pe.matmul(out, wh[:, m % RING, cols], low, start=False, stop=False)
                        ins = pe.matmul(out, wh[:, m % RING, cols], high, start=False, stop=last)
                        k += 1
                    if not last:
                        ins.then_inc(part_used.sem, 1)
                ins.then_inc(prod.sem, 1)

            def square_sums(i, j):
                pe.wait_ge(sq_added.sem, sq_added.at((i, 0), (j + 1) * KD))
                pe.wait_ge(ms_done.sem, ms_done.at((i, 0), j))
                for b in range(4):
                    m = pe.matmul(pn[:, b:b + 1], acc[:, b * TT:(b + 1) * TT], ones[:], start=True, stop=True)
                m.then_inc(ms_psum.sem, 1)

            def spread_factor(i, j):
                pe.wait_ge(rstd_done.sem, rstd_done.at((i, 0), j + 1))
                pe.wait_ge(factor_done.sem, factor_done.at((i, 0), j))
                for b in range(4):
                    m = pe.matmul(pb[:, b * TT:(b + 1) * TT], rstd[:, b:b + 1].broadcast_to([TT, P]), ident[0:TT, 0:TT],
                                  start=True, stop=True)
                m.then_inc(spread.sem, 1)

            a_part = lambda k: (ah[:, k, :], al[:, k, :])
            n_part = lambda k: (nh[:, k, :], nl[:, k, :])
            p_part = lambda k: (pTh[:, k, :], pTl[:, k, :])
            def body(i, last):
                n = (i, 0)
                turn_x(i, 0)
                turn_x(i, 1)
                product(i, EARLY, a_part)
                turn_x(i, 2)
                turn_x(i, 3)
                for d in range(EARLY + 1, KD):
                    product(i, d, a_part)
                for q in range(2 * FB):
                    product(i, FFN0 + q, n_part, (lambda k: pe.wait_ge(n_split.sem, n_split.at(n, k + 1))) if q == 0 else None)
                    if q == 0:
                        square_sums(i, 0)
                    if q == 1:
                        spread_factor(i, 0)
                for d in range(KD):
                    product(i, DOWN0 + d, a_part, (lambda k: pe.wait_ge(a_split.sem, a_split.at(n, k + 1))) if d == 0 else None)
                pe.wait_ge(x_moved.sem, x_moved.at(n))
                for d in range(KD):
                    if not last:
                        turn_cat(i + 1, d)
                    product(i, PLE0 + 2 * d, p_part)
                    product(i, PLE0 + 2 * d + 1, n_part, (lambda k: pe.wait_ge(n_split.sem, n_split.at(n, KD + k + 1))) if d == 0 else None)
                    if d == 0:
                        square_sums(i, 1)
                    if d == 1:
                        spread_factor(i, 1)
                if not last:
                    pe.wait_ge(cat_moved.sem, cat_moved.at(n, 16))
                    product(i, MM, a_part)
                square_sums(i, 2)
                if not last:
                    product(i, MM + 1, a_part)
                spread_factor(i, 2)
                if not last:
                    product(i, MM + 2, a_part)
                for b in range(8):
                    turn_y(i, b, last)

            for b in range(8):
                turn_cat(0, b)
            pe.wait_ge(cat_moved.sem, cat_moved.at((0, 0)))
            for d in range(EARLY):
                product(0, d, a_part)
            with pe.Fori(0, NCHUNK - 1) as i:
                body(i, False)
            body(NCHUNK - 1, True)

        @block.scalar
        def _(act):
            for s in (cat_high, p_high, squared, n_high, ms_done, sig_done, a_high, w_high):
                s.seed(act)
            for s in range(YS):
                act.sem_inc(y_stored[s], 16)
            act.wait_ge(loaded, 16 * 4)

            def high_part(i, m):
                n = (i, 0)
                cols = slice(0, blocks_of(m) * P)
                act.wait_ge(w_landed[m % RING], i * (16 * ITEMS // RING) + 16 * (m // RING + 1))
                back, before = divmod(m - RING, ITEMS)
                d, part = divmod(before - DOWN0, NP)
                if 0 <= d < KD and part < NP - 1:
                    act.wait_ge(part_used.sem, part_used.at((i, back), d * (NP - 1) + part + 1))
                else:
                    p = before if d < 0 else DOWN0 + d if d < KD else before - (NP - 1) * KD
                    act.wait_ge(prod.sem, prod.at((i, back), p + 1))
                act.activation(wh[:, m % RING, cols], raw[:, m % RING, cols], ACT.Copy).then_inc(w_high.sem, 1)

            def high_parts(i, p, last):
                for m in items_at(p, last):
                    high_part(i, m)

            def squares(i, j, d):
                n = (i, 0)
                act.wait_ge(summed.sem, summed.at(n, j * KD + d + 1))
                if d == 0:
                    act.wait_ge(ms_psum.sem, ms_psum.at(n, j))
                    act.activation(acc[:], hT[:, 0, :], ACT.Square).then_inc(squared.sem, 1)
                else:
                    act.wait_ge(sq_added.sem, sq_added.at(n, j * KD + d - 1))
                    act.activation(sq[:, d % 2, :], hT[:, d, :], ACT.Square).then_inc(squared.sem, 1)

            def scaled(i, j, d):
                act.activation(nh[:, d, :], hT[:, d, :], ACT.Copy, scale=gains[:, j, d:d + 1]).then_inc(n_high.sem, 1)

            def mean(i, j):
                n = (i, 0)
                act.wait_ge(ms_psum.sem, ms_psum.at(n, j + 1))
                act.wait_ge(rstd_done.sem, rstd_done.at(n, j))
                act.activation(ms[:], pn, ACT.Copy, scale=1.0 / D, bias=EPS).then_inc(ms_done.sem, 1)

            def cat_high_part(i, b):
                j, half = divmod(b, 2)
                act.wait_ge(cat_turned.sem, cat_turned.at((i, 0), b + 1))
                act.activation(ah[:, half * 4:half * 4 + 4, j * TT:(j + 1) * TT],
                               pt[:, b % TB, 0:4 * TT].rearrange("p (k c) -> p k c", k=4), ACT.Copy).then_inc(cat_high.sem, 1)

            def body(i, rows, last):
                n = (i, 0)
                for j in range(4):
                    at = 3 * j + 2
                    act.wait_ge(x_turned.sem, x_turned.at(n, at + 1))
                    act.activation(pTh[:, :, j * TT:(j + 1) * TT],
                                   pt[:, at % TB, 0:KPL * TT].rearrange("p (k c) -> p k c", k=KPL), ACT.Copy).then_inc(p_high.sem, 1)
                for d in range(KD):
                    high_parts(i, d, last)
                    squares(i, 0, d)
                    scaled(i, 0, d)
                for f in range(FB):
                    p = FFN0 + 2 * f
                    high_parts(i, p, last)
                    if f == 0:
                        mean(i, 0)
                    act.wait_ge(used.sem, used.at(n, p + 1))
                    act.activation(sig[:, f % 2, :], gate[:, f % 2, :], ACT.Sigmoid).then_inc(sig_done.sem, 1)
                    high_parts(i, p + 1, last)
                    act.wait_ge(a_ready.sem, a_ready.at(n, f + 1))
                    act.activation(ah[:, f, :], sq[:, f % 2, :], ACT.Copy).then_inc(a_high.sem, 1)
                for d in range(KD):
                    high_parts(i, DOWN0 + d, last)
                    squares(i, 1, d)
                    scaled(i, 1, d)
                for d in range(KD):
                    p = PLE0 + 2 * d
                    high_parts(i, p, last)
                    if not last:
                        cat_high_part(i + 1, d)
                    high_parts(i, p + 1, last)
                    if d == 0:
                        mean(i, 1)
                    act.wait_ge(gated.sem, gated.at(n, d + 1))
                    act.activation(sig[:, d % 2, :], gate[:, d % 2, :], ACT.Sigmoid).then_inc(sig_done.sem, 1)
                    if d:
                        squares(i, 2, d - 1)
                squares(i, 2, KD - 1)
                mean(i, 2)
                if not last:
                    for m in BEFORE:
                        high_part(i, ITEMS + m)
                for b in range(8):
                    j, half = divmod(b, 2)
                    act.wait_ge(y_moved.sem, y_moved.at(n, b + 1))
                    act.dma_start(t.y[bass.ds(rows[j], TT), half * 512:(half + 1) * 512], y[b % YS]).then_inc(y_stored[b % YS], 16)
            for m in range(LEAD):
                high_part(0, m)
            for b in range(8):
                cat_high_part(0, b)
            for m in BEFORE:
                high_part(0, m)
            with act.Fori(0, NCHUNK - 1) as i:
                body(i, [act.snap(i * CK + j * TT) for j in range(4)], False)
            body(NCHUNK - 1, [(NCHUNK - 1) * CK + j * TT for j in range(4)], True)
            for s in range(YS):
                act.wait_ge(y_stored[s], 16 + 16 * (8 // YS) * NCHUNK)

        @block.vector
        def _(dve):
            for s in (cat_moved, x_moved, y_moved, used, summed, n_split, factor_done, normed, gated, a_ready, a_split):
                s.seed(dve)
            dve.memset(ones[:], 1.0).then_inc(ones_done, 1)
            dve.wait_ge(loaded, 16 * 4)

            def add_block(i, p, d):
                dve.wait_ge(prod.sem, prod.at((i, 0), p + 1))
                dve.tensor_tensor(hT[:, d, :], pm[:, p % 4, 0:CK], hT[:, d, :], ALU.add).then_inc(used.sem, 1)
                dve.drain().then_inc(summed.sem, 1)

            def low_part(i, j, d):
                dve.wait_ge(n_high.sem, n_high.at((i, 0), j * KD + d + 1))
                dve.scalar_tensor_tensor(nl[:, d, :], hT[:, d, :], gains[:, j, d:d + 1], nh[:, d, :].bitcast(F32), ALU.mult, ALU.subtract
                                         ).then_inc(n_split.sem, 1)

            def take_factor(i, j):
                dve.wait_ge(spread.sem, spread.at((i, 0), j + 1))
                dve.tensor_copy(factor[:], pb[:, 0:CK]).then_inc(factor_done.sem, 1)
                dve.drain()

            def low_activation(i, f):
                dve.wait_ge(a_high.sem, a_high.at((i, 0), f + 1))
                dve.tensor_tensor(al[:, f, :], sq[:, f % 2, :], ah[:, f, :].bitcast(F32), ALU.subtract).then_inc(a_split.sem, 1)

            def cat_low_part(i, b):
                j, half = divmod(b, 2)
                at = (slice(None), slice(half * 4, half * 4 + 4), slice(j * TT, (j + 1) * TT))
                dve.wait_ge(cat_high.sem, cat_high.at((i, 0), b + 1))
                dve.tensor_tensor(al[at], pt[:, b % TB, 0:4 * TT].rearrange("p (k c) -> p k c", k=4), ah[at].bitcast(F32), ALU.subtract
                                  ).then_inc(cat_moved.sem, 1)

            def body(i, last):
                n = (i, 0)
                for j in range(4):
                    cols = slice(j * TT, (j + 1) * TT)
                    for b in range(3):
                        at = 3 * j + b
                        k = 4 if b < 2 else KPL
                        src = pt[:, at % TB, 0:k * TT].rearrange("p (k c) -> p k c", k=k)
                        if b < 2:
                            dve.wait_ge(x_turned.sem, x_turned.at(n, at + 1))
                            dve.tensor_copy(hT[:, b * 4:b * 4 + 4, cols], src).then_inc(x_moved.sem, 1)
                        else:
                            dve.wait_ge(p_high.sem, p_high.at(n, j + 1))
                            dve.tensor_tensor(pTl[:, :, cols], src, pTh[:, :, cols].bitcast(F32), ALU.subtract).then_inc(x_moved.sem, 1)
                dve.drain()
                for d in range(KD):
                    add_block(i, d, d)
                    if d:
                        low_part(i, 0, d - 1)
                low_part(i, 0, KD - 1)
                take_factor(i, 0)
                for slot in y_stored:
                    dve.wait_ge(slot, i * (16 * (8 // YS)) + 16)
                for f in range(FB):
                    p = FFN0 + 2 * f
                    dve.wait_ge(prod.sem, prod.at(n, p + 1))
                    dve.tensor_tensor(gate[:, f % 2, :], pm[:, p % 4, 0:CK], factor[:], ALU.mult).then_inc(used.sem, 1)
                    if f:
                        low_activation(i, f - 1)
                    dve.drain()
                    dve.wait_ge(sig_done.sem, sig_done.at(n, f + 1))
                    dve.tensor_tensor(sig[:, f % 2, :], gate[:, f % 2, :], sig[:, f % 2, :], ALU.mult)
                    dve.drain()
                    dve.tensor_tensor(sig[:, f % 2, :], sig[:, f % 2, :], factor[:], ALU.mult)
                    dve.drain()
                    dve.wait_ge(prod.sem, prod.at(n, p + 2))
                    dve.tensor_tensor(sq[:, f % 2, :], pm[:, (p + 1) % 4, 0:CK], sig[:, f % 2, :], ALU.mult).then_inc(used.sem, 1)
                    dve.drain().then_inc(a_ready.sem, 1)
                low_activation(i, FB - 1)
                for d in range(KD):
                    add_block(i, DOWN0 + d, d)
                    if d:
                        low_part(i, 1, d - 1)
                low_part(i, 1, KD - 1)
                take_factor(i, 1)
                for d in range(KD):
                    p = PLE0 + 2 * d
                    dve.wait_ge(prod.sem, prod.at(n, p + 2))
                    dve.tensor_tensor(gate[:, d % 2, :], pm[:, (p + 1) % 4, 0:CK], factor[:], ALU.mult).then_inc(gated.sem, 1)
                    if not last:
                        cat_low_part(i + 1, d)
                    dve.wait_ge(sig_done.sem, sig_done.at(n, FB + d + 1))
                    dve.tensor_tensor(sig[:, d % 2, :], pm[:, p % 4, 0:CK], sig[:, d % 2, :], ALU.mult).then_inc(used.sem, 1)
                    dve.drain()
                    dve.tensor_tensor(hT[:, d, :], hT[:, d, :], sig[:, d % 2, :], ALU.add).then_inc(used.sem, 1)
                    dve.drain().then_inc(summed.sem, 1)
                take_factor(i, 2)
                for d in range(KD):
                    dve.scalar_tensor_tensor(hT[:, d, :], hT[:, d, :], gains[:, 2, d:d + 1], factor[:], ALU.mult, ALU.mult
                                             ).then_inc(normed.sem, 1)
                for b in range(8):
                    dve.wait_ge(y_turned.sem, y_turned.at(n, b + 1))
                    dve.wait_ge(y_stored[b % YS], i * (16 * (8 // YS)) + 16 * (b // YS + 1))
                    dve.tensor_copy(y[b % YS], pt[0:TT, b % TB, :]).then_inc(y_moved.sem, 1)

            for b in range(8):
                cat_low_part(0, b)
            with dve.Fori(0, NCHUNK - 1) as i:
                body(i, False)
            body(NCHUNK - 1, True)

        @block.gpsimd
        def _(pool):
            for s in (rstd_done, sq_added, w_split):
                s.seed(pool)
            pool.memset(mhalf[:], -0.5)
            pool.drain()

            def low_part(i, m):
                cols = slice(0, blocks_of(m) * P)
                pool.wait_ge(w_high.sem, w_high.at((i, 0), m + 1))
                pool.tensor_tensor(wl[:, m % RING, cols], raw[:, m % RING, cols], wh[:, m % RING, cols].bitcast(F32), ALU.subtract
                                   ).then_inc(w_split.sem, 1)

            def low_parts(i, p, last):
                for m in items_at(p, last):
                    low_part(i, m)

            def add_square(i, j, d):
                pool.wait_ge(squared.sem, squared.at((i, 0), j * KD + d + 1))
                if d == 0:
                    pool.sem_inc(sq_added.sem, 1)
                else:
                    pool.tensor_tensor(acc[:], acc[:], sq[:, d % 2, :], ALU.add).then_inc(sq_added.sem, 1)
                    pool.drain()

            def inverse_root(i, j):
                pool.wait_ge(ms_done.sem, ms_done.at((i, 0), j + 1))
                pool.wait_ge(spread.sem, spread.at((i, 0), j))
                pool.tensor_tensor(rstd[:], ms[:], mhalf[:], ALU.pow).then_inc(rstd_done.sem, 1)

            def body(i, last):
                for p in range(MM):
                    low_parts(i, p, last)
                    if p < FFN0:
                        add_square(i, 0, p)
                    elif p == FFN0:
                        inverse_root(i, 0)
                    elif DOWN0 <= p < PLE0:
                        add_square(i, 1, p - DOWN0)
                    elif p == PLE0 + 1:
                        inverse_root(i, 1)
                    elif p > PLE0 + 1 and (p - PLE0) % 2:
                        add_square(i, 2, (p - PLE0) // 2 - 1)
                add_square(i, 2, KD - 1)
                inverse_root(i, 2)
                if not last:
                    for m in BEFORE:
                        low_part(i, ITEMS + m)

            for m in range(BEFORE.stop):
                low_part(0, m)
            with pool.Fori(0, NCHUNK - 1) as i:
                body(i, False)
            body(NCHUNK - 1, True)


def build(nc, t):
    project_phase(nc, t)
    prompt_phase(nc, t)
    sample_index_phase(nc, t)
    sample_select_phase(nc, t)
    sample_attend_phase(nc, t)
    dense_phase(nc, t)


class Tensors:
    pass


SCRATCH = {
    "tr": (ROWS, TRW), "cat": (ROWS, D), "sscore": (NS, NPAGES, 2, PAGE // 2), "snew": (NB // 2 * 16, TS),
    "table": (NS * NPAGES, TABW), "pagecum": (NS, NPAGES), "newmask": (NS, TS),
}
OUTPUTS = {"y": (ROWS, D), "kiv": (ROWS, KIV), "retn_prompt": (RH, RD, RD), "retn_sample": (NB, RH, RD, RD)}


def kernel(x_prompt, x_sample, cache_k, cache_v, cache_idx_k, state_retn, page_table, p_prompt, p_sample,
           g_mix, w_in, g_retn, w_out, g_ffn, w_ffn_in, w_ffn_out, g_ple, w_ple_gate, w_ple_proj, g_final):
    import concourse.bacc as bacc
    from concourse.bass_utils import run_bass_kernel_spmd

    def rows(prompt, sample, width):
        a = np.asarray(prompt).reshape(SEQ, width)
        b = np.asarray(sample).reshape(NS, width)
        return np.concatenate([a, b, np.zeros((ROWS - SEQ - NS, width), a.dtype)])

    arr = np.asarray
    ins = {
        "x": rows(x_prompt, x_sample, D), "p": rows(p_prompt, p_sample, PLE),
        "cache_kv": np.concatenate([arr(cache_k).reshape(-1, KVH * HD), arr(cache_v).reshape(-1, KVH * HD)], axis=1),
        "cache_idx": arr(cache_idx_k).reshape(-1, PAGE * HD), "state_retn": arr(state_retn).reshape(NB, RH, RD, RD),
        "page_table": arr(page_table), "g_mix": arr(g_mix)[0], "w_in": arr(w_in)[0], "g_retn": arr(g_retn)[0],
        "g_ffn": arr(g_ffn)[0], "g_ple": arr(g_ple)[0],
        "w_items": weight_items(arr(w_out)[0], arr(w_ffn_in)[0], arr(w_ffn_out)[0], arr(w_ple_proj)[0], arr(w_ple_gate)[0]),
        "g_final": arr(g_final), "rope": rope_table(), "c": constant_table(), "b_c": attention_table(), "s_c": sample_table(),
    }
    nc = bacc.Bacc("TRN2", target_bir_lowering=False, num_devices=1)
    t = Tensors()
    for name, a in ins.items():
        t.__dict__[name] = nc.dram_tensor(name, a.shape, mybir.dt.from_np(a.dtype), kind="ExternalInput").ap()
    for name, shape in SCRATCH.items():
        t.__dict__[name] = nc.dram_tensor(name, shape, F32, kind="Internal").ap()
    for name, shape in OUTPUTS.items():
        t.__dict__[name] = nc.dram_tensor(name, shape, F32, kind="ExternalOutput").ap()
    build(nc, t)
    r = run_bass_kernel_spmd(nc, [{n: np.ascontiguousarray(a) for n, a in ins.items()}], core_ids=[0]).results[0]
    y, kiv = r["y"], r["kiv"]
    k, ki, v = kiv[:, 0:128], kiv[:, 128:192], kiv[:, 192:320]
    past, new = slice(0, SEQ), slice(SEQ, SEQ + NS)
    return (y[past].reshape(1, SEQ, D), y[new].reshape(NB, TS, D),
            k[past].reshape(1, 1, SEQ, KVH, HD), v[past].reshape(1, 1, SEQ, KVH, HD), ki[past].reshape(1, 1, SEQ, HD),
            r["retn_prompt"].reshape(1, 1, RH, RD, RD),
            k[new].reshape(1, NB, TS, KVH, HD), v[new].reshape(1, NB, TS, KVH, HD), ki[new].reshape(1, NB, TS, HD),
            r["retn_sample"].reshape(1, NB, RH, RD, RD))
```
